# Optimizing a Trainium2 kernel written in Bass

```python
import jax, jax.numpy as jnp
from jax import lax
import numpy as np
import math

D_MODEL = 1024
BATCH = 1
SEQ = 256
DEPTH = 1

D_MIX = D_MODEL
D_A = D_MIX // 2
D_B = D_MIX - D_A
HEAD_CH = 64
N_HEADS_A = D_A // HEAD_CH
N_HEADS_B = D_B // HEAD_CH
CONV_A_WIDTH = 3
CONV_B_WIDTH = 31
D_IN = 3 * D_A + 2 * D_B
N_GROUPS = 4
EXPERTS_PER_GROUP = 8
N_EXPERTS = N_GROUPS * EXPERTS_PER_GROUP
TOP_K_IN_GROUP = 2
D_EXPERT = D_MODEL // 2
EPS = 1e-6


def rmsnorm(x, g):
    xf = x.astype(jnp.float32)
    r = lax.rsqrt(jnp.mean(xf * xf, axis=-1, keepdims=True) + EPS)
    return (xf * r).astype(x.dtype) * g

def layernorm(x, g, b):
    xf = x.astype(jnp.float32)
    mu = jnp.mean(xf, axis=-1, keepdims=True)
    var = jnp.mean(jnp.square(xf - mu), axis=-1, keepdims=True)
    return ((xf - mu) * lax.rsqrt(var + EPS)).astype(x.dtype) * g + b

def head_rmsnorm(y, n_heads, gain):
    bsz, s, c = y.shape
    yh = y.reshape(bsz, s, n_heads, c // n_heads).astype(jnp.float32)
    yh = yh * lax.rsqrt(jnp.mean(yh * yh, axis=-1, keepdims=True) + EPS)
    return yh.reshape(bsz, s, c).astype(y.dtype) * gain

def depthwise_conv_centred(u, w):
    k = w.shape[0]
    pad = (k - 1) // 2
    return lax.conv_general_dilated(
        u, w[:, None, :].astype(u.dtype), window_strides=(1,), padding=[(pad, pad)],
        dimension_numbers=("NWC", "WIO", "NWC"), feature_group_count=u.shape[-1])

def mixer_block(h, w_in, conv_a_w, conv_b_w, conv_b_bias, ln_b_g, ln_b_b, beta_a, beta_b, w_out):
    proj = jnp.einsum("bsd,dc->bsc", h, w_in)
    a_in, a_b, a_c, b_val, b_gate = jnp.split(
        proj, [D_A, 2 * D_A, 3 * D_A, 3 * D_A + D_B], axis=-1)
    y_a = a_b * depthwise_conv_centred(a_c * a_in, conv_a_w)
    u = b_val * jax.nn.sigmoid(b_gate)
    u = depthwise_conv_centred(u, conv_b_w) + conv_b_bias
    y_b = jax.nn.silu(layernorm(u, ln_b_g, ln_b_b))
    y = jnp.concatenate([head_rmsnorm(y_a, N_HEADS_A, beta_a),
                         head_rmsnorm(y_b, N_HEADS_B, beta_b)], axis=-1)
    return jnp.einsum("bsc,cd->bsd", y, w_out)

def hierarchical_moe(h, w_route_group, b_route_group, w_route_expert, b_route_expert, w1, w3, w2):
    bsz, s, d = h.shape
    t = h.reshape(bsz * s, d)
    p_group = jax.nn.softmax((t @ w_route_group + b_route_group).astype(jnp.float32), axis=-1)
    g_idx = jnp.argmax(p_group, axis=-1)
    p_sel = jnp.take_along_axis(p_group, g_idx[:, None], axis=1)[:, 0]
    le = (t @ w_route_expert + b_route_expert).astype(jnp.float32)
    le = le.reshape(-1, N_GROUPS, EXPERTS_PER_GROUP)
    le_sel = jnp.take_along_axis(le, g_idx[:, None, None], axis=1)[:, 0]
    p_exp = jax.nn.softmax(le_sel, axis=-1)
    top_v, top_i = lax.top_k(p_exp, TOP_K_IN_GROUP)
    top_w = top_v / jnp.sum(top_v, axis=-1, keepdims=True)
    eid = g_idx[:, None] * EXPERTS_PER_GROUP + top_i
    combine = p_sel[:, None] * jnp.einsum(
        "tk,tke->te", top_w, jax.nn.one_hot(eid, N_EXPERTS, dtype=jnp.float32))
    combine = combine.astype(t.dtype)
    out = jnp.zeros_like(t)
    for e in range(N_EXPERTS):
        act = jax.nn.silu(t @ w1[e]) * (t @ w3[e])
        out = out + combine[:, e:e + 1] * (act @ w2[e])
    return out.reshape(bsz, s, d)

def first_inputs(seed: int = 0) -> dict:
    key = jax.random.key(seed)
    ks = jax.random.split(key, 20)
    f32 = jnp.float32
    nrm = lambda k, shape, scale: jax.random.normal(k, shape, f32) * scale
    L = DEPTH
    return {
        "x": jax.random.normal(ks[0], (BATCH, SEQ, D_MODEL), f32),
        "norm_mix_g": 1.0 + nrm(ks[1], (L, D_MODEL), 0.02),
        "w_in": nrm(ks[2], (L, D_MODEL, D_IN), D_MODEL ** -0.5),
        "conv_a_w": nrm(ks[3], (L, CONV_A_WIDTH, D_A), CONV_A_WIDTH ** -0.5),
        "conv_b_w": nrm(ks[4], (L, CONV_B_WIDTH, D_B), CONV_B_WIDTH ** -0.5),
        "conv_b_bias": nrm(ks[5], (L, D_B), 0.02),
        "ln_b_g": 1.0 + nrm(ks[6], (L, D_B), 0.02),
        "ln_b_b": nrm(ks[7], (L, D_B), 0.02),
        "beta_a": 1.0 + nrm(ks[8], (L, D_A), 0.02),
        "beta_b": 1.0 + nrm(ks[9], (L, D_B), 0.02),
        "w_out": nrm(ks[10], (L, D_MIX, D_MODEL), D_MIX ** -0.5),
        "norm_ffn_g": 1.0 + nrm(ks[11], (L, D_MODEL), 0.02),
        "w_route_group": nrm(ks[12], (L, D_MODEL, N_GROUPS), D_MODEL ** -0.5),
        "b_route_group": nrm(ks[13], (L, N_GROUPS), 0.01),
        "w_route_expert": nrm(ks[14], (L, D_MODEL, N_EXPERTS), D_MODEL ** -0.5),
        "b_route_expert": nrm(ks[15], (L, N_EXPERTS), 0.01),
        "w1": nrm(ks[16], (L, N_EXPERTS, D_MODEL, D_EXPERT), D_MODEL ** -0.5),
        "w3": nrm(ks[17], (L, N_EXPERTS, D_MODEL, D_EXPERT), D_MODEL ** -0.5),
        "w2": nrm(ks[18], (L, N_EXPERTS, D_EXPERT, D_MODEL), D_EXPERT ** -0.5),
        "norm_final_g": 1.0 + nrm(ks[19], (D_MODEL,), 0.02),
    }

def first_block(x, norm_mix_g, w_in, conv_a_w, conv_b_w, conv_b_bias, ln_b_g, ln_b_b,
              beta_a, beta_b, w_out, norm_ffn_g, w_route_group, b_route_group,
              w_route_expert, b_route_expert, w1, w3, w2, norm_final_g):
    for l in range(DEPTH):
        h = rmsnorm(x, norm_mix_g[l])
        x = x + mixer_block(h, w_in[l], conv_a_w[l], conv_b_w[l], conv_b_bias[l],
                            ln_b_g[l], ln_b_b[l], beta_a[l], beta_b[l], w_out[l])
        h = rmsnorm(x, norm_ffn_g[l])
        x = x + hierarchical_moe(h, w_route_group[l], b_route_group[l], w_route_expert[l],
                                 b_route_expert[l], w1[l], w3[l], w2[l])
    return rmsnorm(x, norm_final_g)


DEPTH_2 = 2

CHUNK = 64
HEAD_DIM = 64
H_A = 8
LEFT_CHUNKS = 8
REL_MAX = 256
H_B = 4
H_C = 8
H_IDX = 4
D_IDX = 64
TOPK_MAX = 256
H_X = 4
MEM_LEN = 256
D_FF = -(-8 * D_MODEL // (3 * 256)) * 256
QB = 128
ROPE_THETA = 10000.0

W_A = H_A * HEAD_DIM
W_B = H_B * 2 * HEAD_DIM
W_C = H_C * HEAD_DIM
IN_SPLITS = (W_A, W_A, W_A, W_B, W_B, W_B, W_C, W_C, W_C, H_IDX * D_IDX, D_IDX, H_IDX, 3 * D_MODEL)
N_IN = 3 * W_A + 3 * W_B + 3 * W_C + H_IDX * D_IDX + D_IDX + H_IDX + 3 * D_MODEL
REL_TABLE = CHUNK + REL_MAX


def rmsnorm_2(x, g):
    x32 = x.astype(jnp.float32)
    y = x32 * lax.rsqrt(jnp.mean(x32 * x32, axis=-1, keepdims=True) + EPS)
    return y.astype(x.dtype) * g

def rope_tables(seq):
    pos = jnp.arange(seq, dtype=jnp.float32)
    inv = ROPE_THETA ** (-jnp.arange(0, HEAD_DIM, 2, dtype=jnp.float32) / HEAD_DIM)
    ang = pos[:, None] * inv[None, :]
    return jnp.cos(ang), jnp.sin(ang)

def apply_rope(x, cos, sin):
    extra = x.ndim - 3
    shp = (cos.shape[0],) + (1,) * extra + (cos.shape[1],)
    c = cos.reshape(shp).astype(x.dtype)
    s = sin.reshape(shp).astype(x.dtype)
    x1, x2 = jnp.split(x, 2, axis=-1)
    return jnp.concatenate([x1 * c - x2 * s, x2 * c + x1 * s], axis=-1)

def masked_softmax(scores, mask):
    return jax.nn.softmax(jnp.where(mask, scores.astype(jnp.float32), -jnp.inf), axis=-1)

def chunk_band_attention(q, k, v, rel_bias):
    b, s, h, d = q.shape
    nc = s // CHUNK
    band = LEFT_CHUNKS + 1
    pad = ((0, 0), (LEFT_CHUNKS * CHUNK, 0), (0, 0), (0, 0))
    kp = jnp.pad(k, pad)
    vp = jnp.pad(v, pad)
    i = jnp.arange(CHUNK)[:, None]
    j = jnp.arange(band * CHUNK)[None, :]
    rel = jnp.clip(LEFT_CHUNKS * CHUNK + i - j, -(CHUNK - 1), REL_MAX) + (CHUNK - 1)
    bias = rel_bias[:, rel].astype(jnp.float32)
    key_off = jnp.arange(band * CHUNK) // CHUNK - LEFT_CHUNKS
    scale = d ** -0.5

    def one_chunk(n):
        start = n * CHUNK
        qn = lax.dynamic_slice_in_dim(q, start, CHUNK, axis=1)
        kn = lax.dynamic_slice_in_dim(kp, start, band * CHUNK, axis=1)
        vn = lax.dynamic_slice_in_dim(vp, start, band * CHUNK, axis=1)
        sc = jnp.einsum('bqhd,bkhd->bhqk', qn, kn).astype(jnp.float32) * scale + bias[None]
        valid = (n + key_off >= 0)[None, None, None, :]
        p = masked_softmax(sc, valid).astype(v.dtype)
        return jnp.einsum('bhqk,bkhd->bqhd', p, vn)

    o = lax.map(one_chunk, jnp.arange(nc))
    return o.transpose(1, 0, 2, 3, 4).reshape(b, s, h * d)

def diff_attention(q, k, v, lam, lambda_init, subln):
    b, s, h, _, d = q.shape
    key_chunk = jnp.arange(s) // CHUNK
    scale = d ** -0.5

    def one_block(n):
        qn = lax.dynamic_slice_in_dim(q, n * QB, QB, axis=1)
        sc = jnp.einsum('bqhcd,bkhcd->bhcqk', qn, k).astype(jnp.float32) * scale
        q_chunk = (n * QB + jnp.arange(QB)) // CHUNK
        valid = key_chunk[None, :] <= q_chunk[:, None]
        p = masked_softmax(sc, valid)
        a = p[:, :, 0] - lam * p[:, :, 1]
        return jnp.einsum('bhqk,bkhe->bqhe', a.astype(v.dtype), v)

    o = lax.map(one_block, jnp.arange(s // QB))
    o = o.transpose(1, 0, 2, 3, 4).reshape(b, s, h, 2 * d)
    o = rmsnorm_2(o, subln) * (1.0 - lambda_init)
    return o.reshape(b, s, h * 2 * d)

def dsa_attention(q, k, v, q_idx, k_idx, w_idx, topk):
    b, s, h, d = q.shape
    key_pos = jnp.arange(s)
    gather = jax.vmap(lambda t, idx: t[idx])
    scale = d ** -0.5

    def one_chunk(n):
        start = n * CHUNK
        qn = lax.dynamic_slice_in_dim(q, start, CHUNK, axis=1)
        qi = lax.dynamic_slice_in_dim(q_idx, start, CHUNK, axis=1)
        wi = lax.dynamic_slice_in_dim(w_idx, start, CHUNK, axis=1).astype(jnp.float32)
        logits = jnp.einsum('bqhd,bsd->bqhs', qi, k_idx).astype(jnp.float32) * D_IDX ** -0.5
        score = jnp.einsum('bqhs,bqh->bqs', jax.nn.relu(logits), wi)
        admissible = key_pos < start + CHUNK
        score = jnp.where(admissible[None, None, :], score, -jnp.inf)
        vals, idx = lax.top_k(score, topk)
        valid = jnp.isfinite(vals)
        kg = gather(k, idx)
        vg = gather(v, idx)
        sc = jnp.einsum('bqhd,bqkhd->bhqk', qn, kg).astype(jnp.float32) * scale
        p = masked_softmax(sc, valid[:, None]).astype(v.dtype)
        return jnp.einsum('bhqk,bqkhd->bqhd', p, vg)

    o = lax.map(one_chunk, jnp.arange(s // CHUNK))
    return o.transpose(1, 0, 2, 3, 4).reshape(b, s, h * d)

def memory_cross_attention(hn, mem_n, w_q, w_kv, w_o):
    b, s, _ = hn.shape
    m = mem_n.shape[1]
    q = (hn @ w_q).reshape(b, s, H_X, HEAD_DIM)
    kv = (mem_n @ w_kv).reshape(b, m, 2, H_X, HEAD_DIM)
    sc = jnp.einsum('bqhd,bmhd->bhqm', q, kv[:, :, 0]).astype(jnp.float32) * HEAD_DIM ** -0.5
    p = jax.nn.softmax(sc, axis=-1).astype(hn.dtype)
    o = jnp.einsum('bhqm,bmhd->bqhd', p, kv[:, :, 1]).reshape(b, s, H_X * HEAD_DIM)
    return o @ w_o

def swiglu(hn, w_gu, w_down):
    g, u = jnp.split(hn @ w_gu, 2, axis=-1)
    return (jax.nn.silu(g) * u) @ w_down

def second_inputs(seed: int = 0) -> dict:
    key = jax.random.key(seed)
    ks = jax.random.split(key, 20)

    def normal(k, shape, scale):
        return jax.random.normal(k, shape, jnp.float32) * scale

    def gain(k, shape):
        return 1.0 + normal(k, shape, 0.05)

    return {
        'x': normal(ks[0], (BATCH, SEQ, D_MODEL), 1.0),
        'mem': normal(ks[1], (BATCH, MEM_LEN, D_MODEL), 1.0),
        'norm_mix': gain(ks[2], (DEPTH_2, D_MODEL)),
        'w_in': normal(ks[3], (DEPTH_2, D_MODEL, N_IN), D_MODEL ** -0.5),
        'rel_bias_a': normal(ks[4], (DEPTH_2, H_A, REL_TABLE), 0.5),
        'lambda_vecs': normal(ks[5], (DEPTH_2, 4, HEAD_DIM), 0.1),
        'subln_b': gain(ks[6], (DEPTH_2, 2 * HEAD_DIM)),
        'w_up_a': normal(ks[7], (DEPTH_2, W_A, D_MODEL), W_A ** -0.5),
        'w_up_b': normal(ks[8], (DEPTH_2, W_B, D_MODEL), W_B ** -0.5),
        'w_up_c': normal(ks[9], (DEPTH_2, W_C, D_MODEL), W_C ** -0.5),
        'w_out': normal(ks[10], (DEPTH_2, D_MODEL, D_MODEL), D_MODEL ** -0.5),
        'norm_cross': gain(ks[11], (DEPTH_2, D_MODEL)),
        'w_q_x': normal(ks[12], (DEPTH_2, D_MODEL, H_X * HEAD_DIM), D_MODEL ** -0.5),
        'w_kv_x': normal(ks[13], (DEPTH_2, D_MODEL, 2 * H_X * HEAD_DIM), D_MODEL ** -0.5),
        'w_o_x': normal(ks[14], (DEPTH_2, H_X * HEAD_DIM, D_MODEL), (H_X * HEAD_DIM) ** -0.5),
        'norm_ffn': gain(ks[15], (DEPTH_2, D_MODEL)),
        'w_gu': normal(ks[16], (DEPTH_2, D_MODEL, 2 * D_FF), D_MODEL ** -0.5),
        'w_down': normal(ks[17], (DEPTH_2, D_FF, D_MODEL), D_FF ** -0.5),
        'mem_norm': gain(ks[18], (D_MODEL,)),
        'final_norm': gain(ks[19], (D_MODEL,)),
    }

def second_block(x, mem, norm_mix, w_in, rel_bias_a, lambda_vecs, subln_b, w_up_a, w_up_b, w_up_c,
              w_out, norm_cross, w_q_x, w_kv_x, w_o_x, norm_ffn, w_gu, w_down, mem_norm, final_norm):
    b, s, _ = x.shape
    topk = min(TOPK_MAX, s // 4)
    cos, sin = rope_tables(s)
    offsets = [int(o) for o in np.cumsum(IN_SPLITS)[:-1]]
    mem_n = rmsnorm_2(mem, mem_norm)
    shp_a = (b, s, H_A, HEAD_DIM)
    shp_b = (b, s, H_B, 2, HEAD_DIM)
    shp_c = (b, s, H_C, HEAD_DIM)
    for l in range(DEPTH_2):
        xn = rmsnorm_2(x, norm_mix[l])
        (qa, ka, va, qb, kb, vb, qc, kc, vc, qi, ki, wi, gates) = jnp.split(xn @ w_in[l], offsets, axis=-1)
        o_a = chunk_band_attention(qa.reshape(shp_a), ka.reshape(shp_a), va.reshape(shp_a), rel_bias_a[l])
        lam_init = 0.8 - 0.6 * math.exp(-0.3 * l)
        lv = lambda_vecs[l].astype(jnp.float32)
        lam = jnp.exp(jnp.sum(lv[0] * lv[1])) - jnp.exp(jnp.sum(lv[2] * lv[3])) + lam_init
        o_b = diff_attention(apply_rope(qb.reshape(shp_b), cos, sin), apply_rope(kb.reshape(shp_b), cos, sin),
                             vb.reshape(b, s, H_B, 2 * HEAD_DIM), lam, lam_init, subln_b[l])
        o_c = dsa_attention(apply_rope(qc.reshape(shp_c), cos, sin), apply_rope(kc.reshape(shp_c), cos, sin),
                            vc.reshape(shp_c),
                            apply_rope(qi.reshape(b, s, H_IDX, D_IDX), cos, sin),
                            apply_rope(ki[:, :, None, :], cos, sin)[:, :, 0],
                            wi * H_IDX ** -0.5, topk)
        g = jax.nn.sigmoid(gates).reshape(b, s, 3, D_MODEL)
        y = (g[:, :, 0] * (o_a @ w_up_a[l]) + g[:, :, 1] * (o_b @ w_up_b[l])
             + g[:, :, 2] * (o_c @ w_up_c[l]))
        x = x + y @ w_out[l]
        x = x + memory_cross_attention(rmsnorm_2(x, norm_cross[l]), mem_n, w_q_x[l], w_kv_x[l], w_o_x[l])
        x = x + swiglu(rmsnorm_2(x, norm_ffn[l]), w_gu[l], w_down[l])
    return rmsnorm_2(x, final_norm)


def setup_inputs(seed=0):
    out = dict(first_inputs(seed))
    for name, value in second_inputs(seed + 1).items():
        if name != "x":
            out[name + "_2"] = value
    return out


def reference(
    x, norm_mix_g, w_in, conv_a_w, conv_b_w, conv_b_bias, ln_b_g, ln_b_b, beta_a, beta_b, w_out,
    norm_ffn_g, w_route_group, b_route_group, w_route_expert, b_route_expert, w1, w3, w2,
    norm_final_g, mem_2, norm_mix_2, w_in_2, rel_bias_a_2, lambda_vecs_2, subln_b_2, w_up_a_2,
    w_up_b_2, w_up_c_2, w_out_2, norm_cross_2, w_q_x_2, w_kv_x_2, w_o_x_2, norm_ffn_2, w_gu_2,
    w_down_2, mem_norm_2, final_norm_2,
):
    x = first_block(
        x, norm_mix_g, w_in, conv_a_w, conv_b_w, conv_b_bias, ln_b_g, ln_b_b, beta_a, beta_b,
        w_out, norm_ffn_g, w_route_group, b_route_group, w_route_expert, b_route_expert, w1, w3,
        w2, norm_final_g,
    )
    return second_block(
        x, mem_2, norm_mix_2, w_in_2, rel_bias_a_2, lambda_vecs_2, subln_b_2, w_up_a_2,
        w_up_b_2, w_up_c_2, w_out_2, norm_cross_2, w_q_x_2, w_kv_x_2, w_o_x_2, norm_ffn_2,
        w_gu_2, w_down_2, mem_norm_2, final_norm_2,
    )


_drawn_inputs = setup_inputs


def setup_inputs(seed=0):
    import zlib

    import numpy as np

    out = dict(_drawn_inputs(seed))
    spreads = {}
    factors = {'b_route_group': 8.0, 'b_route_expert': 3.048, 'norm_cross_2': 6.014, 'mem_norm_2': 4.153}
    for name, (base, spread) in spreads.items():
        noise = np.random.default_rng([zlib.crc32(name.encode()), seed]).standard_normal(out[name].shape)
        drawn = base * np.exp(spread * noise) if base else spread * noise
        out[name] = __import__('jax').numpy.asarray(drawn.astype(out[name].dtype))
    for name, factor in factors.items():
        out[name] = (out[name] * factor).astype(out[name].dtype)
    return out
```

```python
from contextlib import ExitStack

import numpy as np

import concourse.bass as bass
from concourse import mybir

F32 = mybir.dt.float32
I32 = mybir.dt.int32
ALU = mybir.AluOpType
ACT = mybir.ActivationFunctionType
AX = mybir.AxisListType

P = 128
SEQ = 256
D = 1024
KD = D // P
TT = SEQ // P
HALF = 512
D_A = 512
CH = 64
TAPS_A, TAPS_B = 3, 31
PAD_A, PAD_B = 1, 15
EPS = 1e-6
N_GROUPS, PER_GROUP = 4, 8
N_EXPERTS = N_GROUPS * PER_GROUP
PAIRS = N_EXPERTS // 2
D_EXPERT = 512
SLOTS = 64
MAX_PASSES = SEQ // SLOTS
LAYERS = 2
CHUNK = 64
REL = 320
REL_ROW = CHUNK + REL
TOPK = min(256, SEQ // 4)
D_FF = 2816
KF = D_FF // P
SCALE = float(CH) ** -0.5
NEG = -1.0e30
LAYER_LINKS = 124
TAKEN = -3.0e38

RING = 6
PIECE = 4096
DUOS = 4
DUO = 1024

CONST = {}
_at = 0
for _name, _width in (("ident", P), ("mean_model", P), ("mean_mixb", P), ("mean_head", P), ("mean_sub", P),
                      ("rotate", P), ("before", P), ("ones", P), ("cos", SEQ), ("sin", SEQ), ("mask", SEQ),
                      ("iota", SLOTS), ("first", PER_GROUP)):
    CONST[_name] = (_at, _at + _width)
    _at += _width
N_CONST = _at

VEC1 = {}
_at = 0
for _name, _width in (("norm_mix", KD), ("conv_a", 4 * TAPS_A), ("conv_b", 4 * TAPS_B), ("conv_bias", 4), ("ln_g", 4),
                      ("ln_b", 4), ("beta", 8), ("norm_ffn", KD), ("norm_final", KD), ("mem_norm", KD),
                      ("last_norm", KD), ("route_b", N_GROUPS + N_EXPERTS),
                      ("route_w", KD * (N_GROUPS + N_EXPERTS))):
    VEC1[_name] = (_at, _at + _width)
    _at += _width
N_VEC1 = _at

VEC2 = {}
_at = 0
for _name, _width in (("norm_mix", KD), ("norm_cross", KD), ("norm_ffn", KD), ("subln", 1), ("lam_init", 1),
                      ("one_less", 1), ("lambda", 4 * CH)):
    VEC2[_name] = (_at, _at + _width)
    _at += _width
N_VEC2 = _at

MIX_PIECES = [("w_in", c) for c in (3, 4, 0, 2, 1)] + [("w_out", 0), ("w_out", 1)]
Q_A, K_A, V_A, Q_B, K_B, V_B, Q_C, K_C, V_C = (("in", 512 * i, 512) for i in range(9))
IDX = ("in", 4608, 324)
GATES = [("in", 4932 + 512 * i, 512) for i in range(6)]
DOWN = [(0, 3), (3, 6), (6, 9), (9, 12), (12, 15), (15, 18), (18, 22)]
LAYER_PIECES = ([Q_A, K_A, V_A, Q_B, K_B, V_B, IDX] + GATES[:2] + [Q_C, K_C, V_C] + GATES[2:]
                + [("up", b) for b in range(3)] + [("out", 0), ("out", 1), ("q_x",), ("kv_x",), ("o_x",)]
                + [("gu", i) for i in range(KF // 2)] + [("down", i) for i in range(len(DOWN))])
N_MIX, N_LAYER = len(MIX_PIECES), len(LAYER_PIECES)
assert N_LAYER % RING == 0

EARLY = (["mem0", "mem1", "x0", "x1", "n_mem", "n_mix"] + [f"win{i}" for i in range(5)]
         + ["ln_mean", "ln_var", "heads0", "heads1", "wout0", "wout1", "n_ffn", "tok0", "tok1", "logits", "rank"])
LATE = ["n_final"]
LAST = ["n_last", "out0", "out1"]

UNITS = ([("A", c, t) for c in range(4) for t in range(TT)] + [("B", c, t) for c in range(4) for t in range(TT)]
         + [("C", c, t) for c in range(4) for t in range(TT)] + [("X", c, t) for c in range(2) for t in range(TT)])
N_UNITS = len(UNITS)
ROPES = ["qb", "kb", "idx", "qc", "kc"]

def attention(first, last, extra):
    steps = []
    for s in range(first, last + 2):
        if s < last:
            steps.append(("scores", s))
        steps += extra.get(s, [])
        if first <= s - 1 < last:
            steps.append(("turn", s - 1))
        if first <= s - 2 < last:
            steps.append(("apply", s - 2))
    return steps


def gate_parts(starts, piece, gate):
    return {s + o: [("gates", piece + i, gate + i, o)] for i, s in enumerate(starts) for o in range(4)}


WORK = ([("norm", "mix"), ("lam",), ("proj", 0, "qa"), ("proj", 1, "ka"), ("proj_v", 2, "va"),
         ("proj", 3, "qb"), ("proj", 4, "kb"), ("rope", 0, "qb"), ("proj_v", 5, "vb"), ("rope", 1, "kb"),
         ("index_proj", 6)]
        + [("rope", 2, "idx")]
        + attention(0, 8, gate_parts((1, 5), 7, 0))
        + [("index", 0), ("index", 1), ("proj", 9, "qc"), ("proj", 10, "kc"), ("rope", 3, "qc"),
           ("proj_v", 11, "vc"), ("rope", 4, "kc")]
        + attention(8, 24, gate_parts((9, 13, 17, 21), 12, 2))
        + [("subln",)] + [("up", 16 + b, b) for b in range(3)]
        + [("out", 19, 0), ("out", 20, 1), ("norm", "cross"), ("cross_q", 21), ("cross_kv", 22)]
        + attention(24, 28, {}) + [("cross_o", 23), ("norm", "ffn")]
        + [("gate_up", 24 + i, i) for i in range(KF // 2)] + [("down",)])


def tenants(work):
    names = []
    for w in work:
        kind = w[0]
        if kind == "norm":
            names.append(f"l_{w[1]}")
        elif kind in ("proj", "proj_v"):
            names.append(f"p_{w[2]}")
        elif kind == "rope":
            names.append(f"r_{w[2]}")
        elif kind == "index_proj":
            names.append("p_idx")
        elif kind == "index":
            names.append(f"i_{w[1]}")
        elif kind == "gates":
            names += [f"g_{w[2]}"] if w[3] == 0 else []
        elif kind == "scores":
            names.append(f"u_{w[1]}")
        elif kind == "subln":
            names.append("subln")
        elif kind == "up":
            names += [f"up_{w[2]}_0", f"up_{w[2]}_1"]
        elif kind == "out":
            names.append(f"out_{w[2]}")
        elif kind == "cross_q":
            names.append("xq")
        elif kind == "cross_kv":
            names.append("xkv")
        elif kind == "cross_o":
            names += ["xo_0", "xo_1"]
        elif kind == "gate_up":
            names.append(f"gu_{w[2]}")
        elif kind == "down":
            names += ["dn_0", "dn_1"]
    return names


def seat(names, before, at):
    units = others = 0
    for name in names:
        assert name not in at, name
        if name.startswith("u_"):
            d, units = units % 3, units + 1
        elif name.startswith("g_"):
            d = 3
        else:
            d, others = others % DUOS, others + 1
        at[name] = (d, before[d])
        before[d] += 1


def build(nc, x, mem, cst, vec1, vec2, relpad, w_in, w_out, w1, w3, w2, w_in_2, w_up_a, w_up_b, w_up_c,
          w_out_2, w_q_x, w_kv_x, w_o_x, w_gu, w_down, out):
    seats, tenancies = {}, [0] * DUOS
    seat(EARLY + LATE, tenancies, seats)
    start = list(tenancies)
    seat(tenants(WORK), tenancies, seats)
    layer_tenancies = [b - a for a, b in zip(start, tenancies)]
    for i, name in enumerate(LAST):
        d = i % DUOS
        seats[name] = (d, tenancies[d] + (LAYERS - 1) * layer_tenancies[d])

    with ExitStack() as ctx:
        def sb(name, shape, dt=F32):
            return ctx.enter_context(nc.sbuf_tensor(name, shape, dt))

        def sem(name):
            return ctx.enter_context(nc.semaphore(name))

        psum = ctx.enter_context(nc.psum_tensor("psum", [P, DUOS, DUO], F32))

        ring = sb("ring", [P, RING, PIECE])
        xT = sb("xT", [P, KD, SEQ])
        hT = sb("hT", [P, KD, SEQ])
        sq = sb("sq", [P, KD, SEQ])
        consts = sb("consts", [P, N_CONST])
        memT = sb("memT", [P, KD, SEQ])
        std = sb("std", [P, SEQ])
        rstd = sb("rstd", [P, SEQ])
        eps = sb("eps", [P, 1])
        v1 = sb("v1", [P, N_VEC1])
        v2 = sb("v2", [P, N_VEC2])
        big = sb("big", [P, 24 * SEQ])
        qk = sb("qk", [P, 16 * SEQ])
        vals = sb("vals", [P, 2, TT, HALF])
        outs = sb("outs", [P, 3, 4, SEQ])
        win = sb("win", [P, 8, SEQ])
        probs = sb("probs", [P, 3, 2, SEQ])
        probsT = sb("probsT", [P, 2, 2 * TT * P])
        stat = sb("stat", [P, 3, 6])
        qiT = sb("qiT", [P, 3, SEQ])
        wi = sb("wi", [P, TT, 4])
        score = sb("score", [P, SEQ])
        top8 = sb("top8", [P, 8])
        lam = sb("lam", [P, 8])
        route = vals[:, 0].rearrange("p t n -> p (t n)")
        passes = sb("passes", [P, 2], I32)

        def c(name):
            a, b = CONST[name]
            return consts[:, a:b]

        def g1(name):
            a, b = VEC1[name]
            return v1[:, a:b]

        def g2(name):
            a, b = VEC2[name]
            return v2[:, a:b]

        ident = c("ident")

        def view(t, at, *dims):
            n = int(np.prod(dims))
            ap = t[:, at:at + n]
            if len(dims) == 2:
                return ap.rearrange("p (a b) -> p a b", a=dims[0])
            if len(dims) == 3:
                return ap.rearrange("p (a b c) -> p a b c", a=dims[0], b=dims[1])
            return ap

        mtok = view(big, 0, TT, D)
        xtok = view(big, TT * D, TT, D)
        ua = view(qk, 0, 4, SEQ + 2 * PAD_A)
        ub = view(qk, 4 * (SEQ + 2 * PAD_A), 4, SEQ + 2 * PAD_B)
        ab = view(big, 4096, 4, SEQ)
        sg = view(big, 5120, 4, SEQ)
        cb = outs[:, 0]
        yT = view(big, 0, KD, SEQ)
        root_heads = view(big, 4096, KD, SEQ)
        htok = view(big, 0, TT, D)
        sel = view(big, 2048, TT, 2, SLOTS)
        selw = view(big, 2048 + 256, TT, 2, SLOTS)
        xs = view(big, 2048 + 512, KD, P)
        selwT = view(big, 2048 + 512 + 1024, SEQ)
        silu1 = view(big, 3840 + 256, D_EXPERT)
        hid = view(big, 3840 + 768, D_EXPERT)
        hidT = view(big, 3840 + 1280, 4, P)
        ysb = view(qk, 0, D)
        gates = view(big, 0, 24, SEQ)
        act = view(big, 0, KF, SEQ)
        heads = {n: view(qk, 4 * SEQ * i, 4, SEQ) for i, n in enumerate(("qa", "ka", "qb", "kb"))}
        heads["qc"], heads["kc"] = heads["qa"], heads["ka"]
        heads["idx"] = qiT
        values = {"va": vals[:, 0], "vb": vals[:, 1], "vc": vals[:, 0]}
        relu = win[:, 0:4]
        selneg = win[:, 4:6]
        qx, kx = heads["qb"][:, 0:2], heads["qb"][:, 2:4]
        vx = view(qk, 12 * SEQ, TT, SEQ)
        ox = outs[:, 0, 0:2]
        o_of = {"A": outs[:, 0], "B": outs[:, 1], "C": outs[:, 2], "X": ox}
        otok = view(big, 0, TT, D)

        used = [0]

        def small(*dims):
            n = int(np.prod(dims))
            at = used[0]
            used[0] += n
            assert used[0] <= 1024
            return view(route, at, *dims) if len(dims) > 1 else route[:, at:at + n]

        G, E = N_GROUPS, PER_GROUP
        logit = small(TT, G + N_EXPERTS)
        gmax, gsum, psel = small(TT, 1), small(TT, 1), small(TT, 1)
        gexp = small(TT, G)
        gc, gone = small(TT, G), small(TT, G)
        gcm = small(TT, 1)
        le4 = small(TT * G, E)
        le = small(TT, E)
        m1, m2, d12, e12, wa, wb = (small(TT, 1) for _ in range(6))
        f1, f2, fc, le2 = (small(TT, E) for _ in range(4))
        fm = small(TT, 1)
        wsum, fsum = small(TT, E), small(TT, E)
        member = small(TT * G, E)
        combine = small(TT * G, E)
        rank = small(TT, N_EXPERTS)
        count, most, more = small(1), small(1), small(3)

        ring_full = [sem(f"ring_full{i}") for i in range(RING)]
        moe_full = [sem(f"moe_full{i}") for i in range(RING)]
        duo_free = [sem(f"duo_free{i}") for i in range(DUOS)]
        piece_done = sem("piece_done")
        (consts_in, mem_in, x_in, vec2_in, turned, sq_ready, sums_done, std_ready, h_ready, x_ready,
         dve_chain, act_chain, pad_ready, conv_a_ready, gate_b_ready, ub_ready, yb_raw, centred, silu_b, y_ready,
         logits_done, gexp_ready, gneg_ready, d12_ready, e12_ready, member_ready, ranks_done, passes_ready,
         credit_moe, sel_ready, gathered, xs_ready, w1_done, w3_done, silu1_ready, hid_ready, hidT_done, hidT_ready,
         w2_done, ysb_ready, scat_done, scat_added, moe_chain,
         lam_dot, lam_exp, rot_done, cos_ready, rope_ready, idx_raw, idx_done, relu_ready, selneg_ready,
         scores_done, rowmax_ready, exp_ready, probs_ready, probsT_done, probsT_ready, attn_done, subln_ready,
         gates_ready, held, conv_ready, shifted, kx_ready, mixed_ready, silu_ready, layer_chain, last_chain, otok_ready, out_done) = (sem(n) for n in (
            "consts_in mem_in x_in vec2_in turned sq_ready sums_done std_ready h_ready x_ready "
            "dve_chain act_chain pad_ready conv_a_ready gate_b_ready ub_ready yb_raw centred silu_b y_ready "
            "logits_done gexp_ready gneg_ready d12_ready e12_ready member_ready ranks_done passes_ready "
            "credit_moe sel_ready gathered xs_ready w1_done w3_done silu1_ready hid_ready hidT_done hidT_ready "
            "w2_done ysb_ready scat_done scat_added moe_chain "
            "lam_dot lam_exp rot_done cos_ready rope_ready idx_raw idx_done relu_ready selneg_ready "
            "scores_done rowmax_ready exp_ready probs_ready probsT_done probsT_ready attn_done subln_ready "
            "gates_ready held conv_ready shifted kx_ready mixed_ready silu_ready layer_chain last_chain otok_ready out_done").split())

        def duo(name):
            return psum[:, seats[name][0], :]

        def enter(eng, name, l=0):
            d, n = seats[name]
            eng.wait_ge(duo_free[d], l * layer_tenancies[d] + n + 1)

        def freed(eng, name, l=0):
            d, n = seats[name]
            eng.wait_ge(duo_free[d], l * layer_tenancies[d] + n + 2)

        def free_of(name):
            return duo_free[seats[name][0]]

        def slot_of(i):
            return ring[:, i % RING, :]

        def done_piece(eng, i, l=0):
            eng.wait_ge(piece_done, l * N_LAYER + i + 1)

        def loads_by(i):
            pieces = MIX_PIECES + LAYER_PIECES
            n = [2 if piece[0] == "gu" else 1 for piece in pieces]
            return (sum(n[j] for j in range(i % RING, i + 1, RING)),
                    sum(n[j] for j in range(N_MIX, len(pieces)) if j % RING == i % RING))

        def arrived(eng, i, l=0):
            slot_loads, layer_loads = loads_by(i)
            eng.wait_ge(ring_full[i % RING], (l * layer_loads + slot_loads) * 16)

        def linker(eng, chain, per=0, index=0):
            linked = [0]

            def link(ins):
                linked[0] += 1
                ins.then_inc(chain, 1)
                eng.wait_ge(chain, index * per + linked[0])

            return link, linked

        def moe_ap(w):
            return w.rearrange("l e (k p) n -> (l e) p k n", p=P)

        w1_v, w3_v, w2_v = moe_ap(w1), moe_ap(w3), moe_ap(w2)

        def expert_cols(ap, q):
            return ap[:, :, bass.ds(q * 2, 2)].unsqueeze(3).broadcast_to([P, TT, 2, SLOTS])

        def unit_aps(u):
            kind, cc, qt = UNITS[u]
            nk = SEQ if kind == "X" else P * (qt + 1)
            if kind == "X":
                q, k = qx, kx
            else:
                q, k = {"A": (heads["qa"], heads["ka"]), "B": (heads["qb"], heads["kb"]),
                        "C": (heads["qc"], heads["kc"])}[kind]
            return kind, cc, qt, nk, q, k

        block = ctx.enter_context(nc.Block())

        @block.sync
        def _(sp):
            sp.dma_start(consts[:], cst).then_inc(consts_in, 16)
            sp.dma_start(mtok, mem.rearrange("b (t p) d -> p (b t) d", p=P)).then_inc(mem_in, 16)
            sp.dma_start(xtok, x.rearrange("b (t p) d -> p (b t) d", p=P)).then_inc(x_in, 16)
            sp.dma_start(v1[:], vec1).then_inc(consts_in, 16)
            w_in_v = w_in.rearrange("l (k p) n -> p (l k) n", p=P)
            w_out_v = w_out.rearrange("l (k p) n -> p (l k) n", p=P)
            for i, (name, col) in enumerate(MIX_PIECES):
                if i >= RING:
                    done_piece(sp, i - RING)
                src = w_in_v if name == "w_in" else w_out_v
                sp.dma_start(view(ring[:, i % RING, :], 0, KD, HALF),
                             src[:, :, col * HALF:(col + 1) * HALF]).then_inc(ring_full[i % RING], 16)

            def load_pair(q, n):
                for at, done, src, k in ((0, w1_done, w1_v, KD), (2, w3_done, w3_v, KD), (4, w2_done, w2_v, 4)):
                    sp.wait_ge(done, n + 1)
                    for e in range(2):
                        sp.dma_start(view(ring[:, at + e, :], 0, k, PIECE // k),
                                     src[bass.ds(q * 2 + e, 1)].rearrange("a p k n -> (a p) k n")
                                     ).then_inc(moe_full[at + e], 16)

            done_piece(sp, N_MIX - 1)
            with sp.Fori(0, PAIRS) as q:
                load_pair(q, q)
            sp.wait_ge(passes_ready, 1)
            n_pass = sp.value_load(passes[0:1, 0:1], min_val=1, max_val=MAX_PASSES)
            n_more = sp.value_load(passes[0:1, 1:2], min_val=0, max_val=MAX_PASSES - 1)
            with sp.If(n_more):
                with sp.Fori(1, n_pass) as p:
                    with sp.Fori(0, PAIRS) as q:
                        load_pair(q, p * PAIRS + q)
            sp.wait_ge(w2_done, n_pass * PAIRS + 1)
            sp.sem_inc(held, 1)

            with sp.Fori(0, LAYERS) as l:
                sp.wait_ge(h_ready, l * 3 + 4)
                sp.dma_start(v2[:], vec2[bass.ds(l, 1)].rearrange("a p n -> (a p) n")).then_inc(vec2_in, 16)
                window = bass.AP(relpad.tensor, l * (8 * REL_ROW), [[1, P], [REL_ROW, 8], [1, SEQ]])
                sp.dma_start(win[:], window).then_inc(vec2_in, 16)
                first = N_MIX
                for i, piece in enumerate(LAYER_PIECES):
                    j = first + i
                    sp.wait_ge(piece_done, l * N_LAYER + j - RING + 1)
                    slot = ring[:, j % RING, :]
                    kind = piece[0]

                    def rows(w, k):
                        return w[bass.ds(l, 1)].rearrange("a (k p) n -> (a p) k n", p=P)

                    if kind == "in":
                        _, at, n = piece
                        dst, src = view(slot, 0, KD, n), rows(w_in_2, KD)[:, :, at:at + n]
                    elif kind == "up":
                        w = (w_up_a, w_up_b, w_up_c)[piece[1]]
                        dst, src = view(slot, 0, 4, D), rows(w, 4)
                    elif kind == "out":
                        a = piece[1] * HALF
                        dst, src = view(slot, 0, KD, HALF), rows(w_out_2, KD)[:, :, a:a + HALF]
                    elif kind == "q_x":
                        dst, src = view(slot, 0, KD, SEQ), rows(w_q_x, KD)
                    elif kind == "kv_x":
                        dst, src = view(slot, 0, KD, HALF), rows(w_kv_x, KD)
                    elif kind == "o_x":
                        dst, src = view(slot, 0, 2, D), rows(w_o_x, 2)
                    elif kind == "gu":
                        a = piece[1] * 2 * P
                        dst = view(slot, 0, KD, 2, 2 * P)
                        src = w_gu[bass.ds(l, 1)].rearrange("a (k p) (g n) -> (a p) k g n", p=P, g=2)[:, :, :, a:a + 2 * P]
                        sp.dma_start(dst[:, :, 0, :], src[:, :, 0, :]).then_inc(ring_full[j % RING], 16)
                        dst, src = dst[:, :, 1, :], src[:, :, 1, :]
                    else:
                        a, b = DOWN[piece[1]]
                        dst, src = view(slot, 0, b - a, D), rows(w_down, KF)[:, a:b, :]
                    sp.dma_start(dst, src).then_inc(ring_full[j % RING], 16)

            sp.wait_ge(otok_ready, 2)
            sp.dma_start(out.rearrange("b (t p) d -> p (b t) d", p=P), otok).then_inc(out_done, 16)
            sp.wait_ge(out_done, 16)

        @block.tensor
        def _(pe):
            mm = pe.matmul

            def transpose_tokens(names, src):
                for half, name in enumerate(names):
                    enter(pe, name)
                    to = view(duo(name), 0, 4, SEQ)
                    for k in range(4):
                        for t in range(TT):
                            kk = half * 4 + k
                            last = pe.transpose(to[:, k, t * P:(t + 1) * P], src[:, t, kk * P:(kk + 1) * P], ident)
                    last.then_inc(turned, 1)

            def sums(name, mean, source, chunks, l=0):
                enter(pe, name, l)
                for k in range(chunks):
                    last = mm(duo(name)[:, 0:SEQ], mean, source[:, k, :], start=(k == 0), stop=(k == chunks - 1))
                last.then_inc(sums_done, 1)

            def project(i, name, rhs, l=0, chunks=4, k_chunks=KD, width=HALF, signal=None):
                arrived(pe, i, l)
                enter(pe, name, l)
                w = view(slot_of(i), 0, k_chunks, width)
                to = view(duo(name), 0, 4, SEQ)
                for o in range(chunks):
                    for k in range(k_chunks):
                        last = mm(to[:, o, :], w[:, k, o * P:(o + 1) * P], rhs[:, k, :],
                                  start=(k == 0), stop=(k == k_chunks - 1))
                last.then_inc(piece_done, 1)

            pe.wait_ge(consts_in, 32)
            pe.wait_ge(mem_in, 16)
            transpose_tokens(("mem0", "mem1"), mtok)
            pe.wait_ge(x_in, 16)
            transpose_tokens(("x0", "x1"), xtok)
            pe.wait_ge(sq_ready, 1)
            sums("n_mem", c("mean_model"), sq, KD)
            pe.wait_ge(sq_ready, 2)
            sums("n_mix", c("mean_model"), sq, KD)
            pe.wait_ge(h_ready, 2)
            for i in range(5):
                project(i, f"win{i}", hT)
            pe.wait_ge(conv_ready, 1)
            sums("ln_mean", c("mean_mixb"), cb, 4)
            pe.wait_ge(sq_ready, 3)
            sums("ln_var", c("mean_mixb"), sq, 4)
            pe.wait_ge(sq_ready, 4)
            for half in range(2):
                name = f"heads{half}"
                enter(pe, name)
                for k in range(4):
                    last = mm(view(duo(name), 0, 4, SEQ)[:, k, :], c("mean_head"), sq[:, half * 4 + k, :],
                              start=True, stop=True)
                last.then_inc(sums_done, 1)
            pe.wait_ge(y_ready, 1)
            for i in range(2):
                project(5 + i, f"wout{i}", yT)
            pe.wait_ge(sq_ready, 5)
            sums("n_ffn", c("mean_model"), sq, KD)
            pe.wait_ge(h_ready, 3)
            enter(pe, "tok0")
            enter(pe, "tok1")
            for half in range(2):
                to = duo(f"tok{half}")
                for k in range(KD):
                    last = pe.transpose(to[:, k * P:(k + 1) * P], hT[:, k, half * P:(half + 1) * P], ident)
                last.then_inc(turned, 1)
            enter(pe, "logits")
            wr = view(g1("route_w"), 0, KD, N_GROUPS + N_EXPERTS)
            for t in range(TT):
                for k in range(KD):
                    last = mm(view(duo("logits"), 0, TT, N_GROUPS + N_EXPERTS)[:, t, :], hT[:, k, t * P:(t + 1) * P],
                              wr[:, k, :], start=(k == 0), stop=(k == KD - 1))
            last.then_inc(logits_done, 1)
            pe.wait_ge(member_ready, 1)
            enter(pe, "rank")
            to = view(duo("rank"), 0, 3, N_EXPERTS)
            mem_t = member.rearrange("p (t g) e -> p t (g e)", t=TT)
            mm(to[:, 0, :], c("before"), mem_t[:, 0, :], start=True, stop=True)
            for o, (a, b) in ((1, ("ones", "before")), (2, ("ones", "ones"))):
                mm(to[:, o, :], c(a), mem_t[:, 0, :], start=True, stop=False)
                last = mm(to[:, o, :], c(b), mem_t[:, 1, :], start=False, stop=True)
            last.then_inc(ranks_done, 1)

            pe.wait_ge(passes_ready, 1)
            n_pass = pe.value_load(passes[0:1, 0:1], min_val=1, max_val=MAX_PASSES)
            for credit in (w1_done, w3_done, w2_done):
                pe.sem_inc(credit, 1)
            with pe.Fori(0, n_pass) as p:
                with pe.Fori(0, PAIRS) as q:
                    n = p * PAIRS + q
                    pe.wait_ge(sel_ready, n + 1)
                    pe.wait_ge(scat_added, n * 2 + 2)
                    g = view(psum[:, 0, :], 0, KD, P)
                    for k in range(KD):
                        for t in range(TT):
                            mm(g[:, k, :], htok[:, t, k * P:(k + 1) * P],
                               sel[:, t].rearrange("p e s -> p (e s)"), start=(t == 0), stop=(t == TT - 1))
                    for t in range(TT):
                        last = pe.transpose(psum[:, 3, t * P:(t + 1) * P], selw[:, t].rearrange("p e s -> p (e s)"), ident)
                    last.then_inc(gathered, 1)
                    pe.wait_ge(xs_ready, n * 2 + 2)
                    for at, bank, done in ((0, 0, w1_done), (2, 1, w3_done)):
                        for e in range(2):
                            pe.wait_ge(moe_full[at + e], n * 16 + 16)
                        for k in range(KD):
                            for e in range(2):
                                rows = slice(e * SLOTS, (e + 1) * SLOTS)
                                last = mm(psum[rows, 1, bank * 512:bank * 512 + 512], xs[:, k, rows],
                                          view(ring[:, at + e, :], 0, KD, D_EXPERT)[:, k, :],
                                          start=(k == 0), stop=(k == KD - 1), skip_group_check=True)
                        last.then_inc(done, 1)
                    pe.wait_ge(hid_ready, n + 1)
                    for f in range(4):
                        last = pe.transpose(psum[:, 3, 512 + f * P:512 + (f + 1) * P], hid[:, f * P:(f + 1) * P], ident)
                    last.then_inc(hidT_done, 1)
                    pe.wait_ge(hidT_ready, n + 1)
                    for e in range(2):
                        pe.wait_ge(moe_full[4 + e], n * 16 + 16)
                    for f in range(4):
                        for half in range(2):
                            for e in range(2):
                                rows = slice(e * SLOTS, (e + 1) * SLOTS)
                                last = mm(psum[rows, 2, half * 512:half * 512 + 512], hidT[:, f, rows],
                                          view(ring[:, 4 + e, :], 0, 4, D)[:, f, half * 512:half * 512 + 512],
                                          start=(f == 0), stop=(f == 3), skip_group_check=True)
                    last.then_inc(w2_done, 1)
                    pe.wait_ge(ysb_ready, n + 1)
                    for half, d in enumerate((0, 3)):
                        for k in range(4):
                            kk = half * 4 + k
                            last = mm(view(psum[:, d, :], 0, 4, SEQ)[:, k, :], ysb[:, kk * P:(kk + 1) * P], selwT,
                                      start=True, stop=True)
                        last.then_inc(scat_done, 1)
            pe.wait_ge(scat_added, n_pass * (2 * PAIRS) + 2)
            pe.wait_ge(sq_ready, 6)
            sums("n_final", c("mean_model"), sq, KD)

            with pe.Fori(0, LAYERS) as l:
                norm_no = 0
                for w in WORK:
                    kind = w[0]
                    if kind == "norm":
                        at = {"mix": 0, "cross": 2, "ffn": 3}[w[1]]
                        pe.wait_ge(sq_ready, l * 4 + 6 + at + 1)
                        sums(f"l_{w[1]}", c("mean_model"), sq, KD, l)
                        pe.wait_ge(h_ready, l * 3 + 4 + norm_no + 1)
                        norm_no += 1
                    elif kind == "proj":
                        project(N_MIX + w[1], f"p_{w[2]}", hT, l)
                    elif kind == "proj_v":
                        i, name = N_MIX + w[1], f"p_{w[2]}"
                        arrived(pe, i, l)
                        enter(pe, name, l)
                        wv = view(slot_of(i), 0, KD, HALF)
                        for t in range(TT):
                            for k in range(KD):
                                last = mm(duo(name)[:, t * 512:(t + 1) * 512], hT[:, k, t * P:(t + 1) * P], wv[:, k, :],
                                          start=(k == 0), stop=(k == KD - 1))
                        last.then_inc(piece_done, 1)
                    elif kind == "index_proj":
                        i = N_MIX + w[1]
                        arrived(pe, i, l)
                        enter(pe, "p_idx", l)
                        wx = view(slot_of(i), 0, KD, 324)
                        to = duo("p_idx")
                        for o in range(2):
                            for k in range(KD):
                                mm(to[:, o * SEQ:(o + 1) * SEQ], wx[:, k, o * P:(o + 1) * P], hT[:, k, :],
                                   start=(k == 0), stop=(k == KD - 1))
                        for half in range(2):
                            for k in range(KD):
                                mm(to[half * 64:half * 64 + 64, 512:512 + SEQ], wx[:, k, 256:320], hT[:, k, :],
                                   start=(k == 0), stop=(k == KD - 1))
                        for t in range(TT):
                            for k in range(KD):
                                last = mm(to[:, 768 + 4 * t:772 + 4 * t], hT[:, k, t * P:(t + 1) * P], wx[:, k, 320:324],
                                          start=(k == 0), stop=(k == KD - 1))
                        last.then_inc(piece_done, 1)
                    elif kind == "rope":
                        r, name = w[1], w[2]
                        freed(pe, f"p_{name}", l)
                        enter(pe, f"r_{name}", l)
                        to = view(duo(f"r_{name}"), 0, 4, SEQ)
                        for k in range(3 if name == "idx" else 4):
                            last = mm(to[:, k, :], c("rotate"), heads[name][:, k, :], start=True, stop=True)
                        last.then_inc(rot_done, 1)
                    elif kind == "index":
                        t = w[1]
                        nk = P * (t + 1)
                        name = f"i_{t}"
                        pe.wait_ge(rope_ready, l * 5 + 3)
                        enter(pe, name, l)
                        for h in range(4):
                            cc, r = h // 2, h % 2
                            rows = slice(64 * r, 64 * r + 64)
                            last = mm(duo(name)[:, r * 512 + cc * SEQ:r * 512 + cc * SEQ + nk],
                                      qiT[rows, cc, t * P:(t + 1) * P], qiT[rows, 2, 0:nk], start=True, stop=True)
                        last.then_inc(idx_done, 1)
                    elif kind == "gates":
                        i, name, o = N_MIX + w[1], f"g_{w[2]}", w[3]
                        if o == 0:
                            arrived(pe, i, l)
                            enter(pe, name, l)
                        wg = view(slot_of(i), 0, KD, HALF)
                        for k in range(KD):
                            last = mm(duo(name)[:, o * SEQ:(o + 1) * SEQ], wg[:, k, o * P:(o + 1) * P], hT[:, k, :],
                                      start=(k == 0), stop=(k == KD - 1))
                        if o == 3:
                            last.then_inc(piece_done, 1)
                    elif kind == "scores":
                        u = w[1]
                        ukind, cc, qt, nk, qb, kb = unit_aps(u)
                        if u == 0:
                            freed(pe, "p_ka", l)
                        elif u == 8:
                            pe.wait_ge(rope_ready, l * 5 + 2)
                        elif u == 16:
                            pe.wait_ge(rope_ready, l * 5 + 5)
                        elif u == 24:
                            freed(pe, "xkv", l)
                        enter(pe, f"u_{u}", l)
                        for r in range(2):
                            rows = slice(64 * r, 64 * r + 64)
                            last = mm(duo(f"u_{u}")[:, r * 512:r * 512 + nk], qb[rows, cc, qt * P:(qt + 1) * P],
                                      kb[rows, cc, 0:nk], start=True, stop=True)
                        last.then_inc(scores_done, 1)
                    elif kind == "turn":
                        u = w[1]
                        ukind, cc, qt, nk, _, _ = unit_aps(u)
                        pe.wait_ge(probs_ready, l * N_UNITS + u + 1)
                        at = 0
                        for r in range(1 if ukind == "B" else 2):
                            for kt in range(nk // P):
                                last = pe.transpose(duo(f"u_{u}")[:, at * P:(at + 1) * P],
                                                    probs[:, u % 3, r, kt * P:(kt + 1) * P], ident)
                                at += 1
                        last.then_inc(probsT_done, 1)
                    elif kind == "apply":
                        u = w[1]
                        ukind, cc, qt, nk, _, _ = unit_aps(u)
                        pe.wait_ge(probsT_ready, l * N_UNITS + u + 1)
                        nt = nk // P
                        to = duo(f"u_{u}")
                        if ukind == "B":
                            for kt in range(nt):
                                last = mm(to[:, 512:512 + P], values["vb"][:, kt, cc * P:(cc + 1) * P],
                                          probsT[:, u % 2, kt * P:(kt + 1) * P], start=(kt == 0), stop=(kt == nt - 1))
                        else:
                            v = vx if ukind == "X" else vals[:, 0]
                            for r in range(2):
                                for kt in range(nt):
                                    at = r * nt + kt
                                    last = mm(to[64 * r:64 * r + 64, 512:512 + P],
                                              v[:, kt, (2 * cc + r) * CH:(2 * cc + r + 1) * CH],
                                              probsT[:, u % 2, at * P:(at + 1) * P],
                                              start=(kt == 0), stop=(kt == nt - 1))
                        last.then_inc(attn_done, 1)
                    elif kind == "subln":
                        pe.wait_ge(sq_ready, l * 4 + 6 + 2)
                        enter(pe, "subln", l)
                        for k in range(4):
                            last = mm(view(duo("subln"), 0, 4, SEQ)[:, k, :], c("mean_sub"), sq[:, k, :],
                                      start=True, stop=True)
                        last.then_inc(sums_done, 1)
                    elif kind == "up":
                        i, b = N_MIX + w[1], w[2]
                        if b == 0:
                            freed(pe, "u_7", l)
                        elif b == 1:
                            pe.wait_ge(subln_ready, l + 1)
                        else:
                            freed(pe, "u_23", l)
                        arrived(pe, i, l)
                        wu = view(slot_of(i), 0, 4, D)
                        for half in range(2):
                            enter(pe, f"up_{b}_{half}", l)
                            to = view(duo(f"up_{b}_{half}"), 0, 4, SEQ)
                            for o in range(4):
                                oo = half * 4 + o
                                for k in range(4):
                                    last = mm(to[:, o, :], wu[:, k, oo * P:(oo + 1) * P], outs[:, b, k, :],
                                              start=(k == 0), stop=(k == 3))
                        last.then_inc(piece_done, 1)
                    elif kind == "out":
                        if w[2] == 0:
                            pe.wait_ge(mixed_ready, l + 1)
                        project(N_MIX + w[1], f"out_{w[2]}", hT, l)
                    elif kind == "cross_q":
                        project(N_MIX + w[1], "xq", hT, l, chunks=2, width=SEQ)
                    elif kind == "cross_kv":
                        i = N_MIX + w[1]
                        arrived(pe, i, l)
                        enter(pe, "xkv", l)
                        wk = view(slot_of(i), 0, KD, HALF)
                        to = view(duo("xkv"), 0, 4, SEQ)
                        for o in range(2):
                            for k in range(KD):
                                mm(to[:, o, :], wk[:, k, o * P:(o + 1) * P], memT[:, k, :],
                                   start=(k == 0), stop=(k == KD - 1))
                        for t in range(TT):
                            for k in range(KD):
                                last = mm(to[:, 2 + t, :], memT[:, k, t * P:(t + 1) * P], wk[:, k, SEQ:2 * SEQ],
                                          start=(k == 0), stop=(k == KD - 1))
                        last.then_inc(piece_done, 1)
                    elif kind == "cross_o":
                        i = N_MIX + w[1]
                        arrived(pe, i, l)
                        freed(pe, "u_27", l)
                        wo = view(slot_of(i), 0, 2, D)
                        for half in range(2):
                            enter(pe, f"xo_{half}", l)
                            to = view(duo(f"xo_{half}"), 0, 4, SEQ)
                            for o in range(4):
                                oo = half * 4 + o
                                for k in range(2):
                                    last = mm(to[:, o, :], wo[:, k, oo * P:(oo + 1) * P], ox[:, k, :],
                                              start=(k == 0), stop=(k == 1))
                        last.then_inc(piece_done, 1)
                    elif kind == "gate_up":
                        project(N_MIX + w[1], f"gu_{w[2]}", hT, l)
                    elif kind == "down":
                        for half in range(2):
                            enter(pe, f"dn_{half}", l)
                        for j, (a, b) in enumerate(DOWN):
                            i = N_MIX + 35 + j
                            arrived(pe, i, l)
                            wd = view(slot_of(i), 0, b - a, D)
                            for f in range(a, b):
                                freed(pe, f"gu_{f // 2}", l)
                                for oo in range(8):
                                    last = mm(view(duo(f"dn_{oo // 4}"), 0, 4, SEQ)[:, oo % 4, :],
                                              wd[:, f - a, oo * P:(oo + 1) * P], act[:, f, :],
                                              start=(f == 0 and oo % 2 == 0), stop=(f == KF - 1),
                                              skip_group_check=True)
                            last.then_inc(piece_done, 1)

            pe.wait_ge(sq_ready, 6 + 4 * LAYERS + 1)
            sums("n_last", c("mean_model"), sq, KD)
            pe.wait_ge(h_ready, 4 + 3 * LAYERS + 1)
            for t in range(TT):
                enter(pe, f"out{t}")
                for k in range(KD):
                    last = pe.transpose(duo(f"out{t}")[:, k * P:(k + 1) * P], hT[:, k, t * P:(t + 1) * P], ident)
                last.then_inc(turned, 1)

        @block.scalar
        def _(act_e):
            nca = nc.scalar

            def f(out_ap, in_ap, func, **kw):
                return nca.activation(out_ap, in_ap, func, **kw)

            def copy(out_ap, in_ap):
                return nca.activation(out_ap, in_ap, ACT.Copy)

            def root(name, sums_no, l=0, per=0):
                act_e.wait_ge(sums_done, l * per + sums_no)
                return f(std[:], duo(name)[:, 0:SEQ], ACT.Sqrt, bias=eps[:])

            for d in range(DUOS):
                act_e.sem_inc(duo_free[d], 1)
            for half in range(2):
                act_e.wait_ge(turned, half + 1)
                copy(hT[:, half * 4:half * 4 + 4, :], view(duo(f"mem{half}"), 0, 4, SEQ)).then_inc(free_of(f"mem{half}"), 1)
            freed(act_e, "mem0")
            freed(act_e, "mem1")
            f(sq[:], hT[:], ACT.Square).then_inc(sq_ready, 1)
            for half in range(2):
                act_e.wait_ge(turned, half + 3)
                copy(xT[:, half * 4:half * 4 + 4, :], view(duo(f"x{half}"), 0, 4, SEQ)).then_inc(free_of(f"x{half}"), 1)
            act_e.wait_ge(pad_ready, 3)
            root("n_mem", 1).then_inc(std_ready, 1)
            freed(act_e, "x0")
            freed(act_e, "x1")
            f(sq[:], xT[:], ACT.Square).then_inc(sq_ready, 1)
            act_e.wait_ge(h_ready, 1)
            root("n_mix", 2).then_inc(std_ready, 1)

            done_piece(act_e, 0)
            copy(ub[:, :, PAD_B:PAD_B + SEQ], view(duo("win0"), 0, 4, SEQ)).then_inc(free_of("win0"), 1)
            done_piece(act_e, 1)
            f(sg, view(duo("win1"), 0, 4, SEQ), ACT.Sigmoid).then_inc(free_of("win1"), 1)
            done_piece(act_e, 2)
            copy(ua[:, :, PAD_A:PAD_A + SEQ], view(duo("win2"), 0, 4, SEQ)).then_inc(free_of("win2"), 1)
            done_piece(act_e, 4)
            copy(ab, view(duo("win4"), 0, 4, SEQ)).then_inc(free_of("win4"), 1)
            act_e.wait_ge(centred, 1)
            f(sq[:, 0:4], cb, ACT.Square).then_inc(sq_ready, 1)
            root("ln_var", 4).then_inc(std_ready, 1)
            act_e.wait_ge(yb_raw, 1)
            for k in range(4):
                last = f(yT[:, 4 + k, :], cb[:, k, :], ACT.Silu, bias=g1("ln_b")[:, k:k + 1])
            last.then_inc(silu_b, 1)
            act_e.wait_ge(silu_b, 1)
            act_e.wait_ge(conv_a_ready, 1)
            f(sq[:], yT, ACT.Square).then_inc(sq_ready, 1)
            for half in range(2):
                act_e.wait_ge(sums_done, 5 + half)
                f(root_heads[:, half * 4:half * 4 + 4, :], view(duo(f"heads{half}"), 0, 4, SEQ), ACT.Sqrt,
                  bias=eps[:]).then_inc(std_ready, 1)
            freed(act_e, "wout0")
            freed(act_e, "wout1")
            f(sq[:], xT[:], ACT.Square).then_inc(sq_ready, 1)
            root("n_ffn", 7).then_inc(std_ready, 1)
            for t in range(TT):
                act_e.wait_ge(turned, 5 + t)
                copy(htok[:, t, :], duo(f"tok{t}")).then_inc(free_of(f"tok{t}"), 1)
            act_e.wait_ge(gneg_ready, 1)
            f(gexp, gexp, ACT.Exp).then_inc(gexp_ready, 1)
            act_e.wait_ge(d12_ready, 1)
            f(e12, d12, ACT.Exp).then_inc(e12_ready, 1)

            act_e.wait_ge(passes_ready, 1)
            n_pass = act_e.value_load(passes[0:1, 0:1], min_val=1, max_val=MAX_PASSES)
            with act_e.Fori(0, n_pass) as p:
                with act_e.Fori(0, PAIRS) as q:
                    n = p * PAIRS + q
                    act_e.wait_ge(gathered, n + 1)
                    copy(xs, view(psum[:, 0, :], 0, KD, P)).then_inc(xs_ready, 1)
                    copy(selwT, psum[:, 3, 0:SEQ]).then_inc(xs_ready, 1)
                    act_e.wait_ge(w1_done, n + 2)
                    f(silu1, psum[:, 1, 0:512], ACT.Silu).then_inc(silu1_ready, 1)
                    act_e.wait_ge(hidT_done, n + 1)
                    copy(hidT, view(psum[:, 3, 512:1024], 0, 4, P)).then_inc(hidT_ready, 1)
                    act_e.wait_ge(w2_done, n + 2)
                    copy(ysb, psum[:, 2, :]).then_inc(ysb_ready, 1)
            act_e.wait_ge(scat_added, n_pass * (2 * PAIRS) + 2)
            f(sq[:], xT[:], ACT.Square).then_inc(sq_ready, 1)
            root("n_final", 8).then_inc(std_ready, 1)

            with act_e.Fori(0, LAYERS) as l:
                norm_no = 0
                for w in WORK:
                    kind = w[0]
                    if kind == "norm":
                        name = f"l_{w[1]}"
                        if w[1] == "mix":
                            act_e.wait_ge(x_ready, l + 1)
                        elif w[1] == "cross":
                            freed(act_e, "out_0", l)
                            freed(act_e, "out_1", l)
                        else:
                            freed(act_e, "xo_0", l)
                            freed(act_e, "xo_1", l)
                        f(sq[:], xT[:], ACT.Square).then_inc(sq_ready, 1)
                        act_e.wait_ge(h_ready, l * 3 + 4 + norm_no)
                        norm_no += 1
                        root(name, 8 + {"mix": 0, "cross": 2, "ffn": 3}[w[1]] + 1, l, 4).then_inc(std_ready, 1)
                    elif kind == "lam":
                        act_e.wait_ge(lam_dot, l + 1)
                        f(lam[:, 0:2], lam[:, 0:2], ACT.Exp).then_inc(lam_exp, 1)
                    elif kind == "proj":
                        done_piece(act_e, N_MIX + w[1], l)
                        name = w[2]
                        copy(heads[name], view(duo(f"p_{name}"), 0, 4, SEQ)).then_inc(free_of(f"p_{name}"), 1)
                    elif kind == "proj_v":
                        done_piece(act_e, N_MIX + w[1], l)
                        name = w[2]
                        copy(values[name], view(duo(f"p_{name}"), 0, TT, HALF)).then_inc(free_of(f"p_{name}"), 1)
                    elif kind == "index_proj":
                        done_piece(act_e, N_MIX + w[1], l)
                        copy(qiT[:], view(duo("p_idx"), 0, 3, SEQ)).then_inc(idx_raw, 1)
                    elif kind == "gates":
                        if w[3] == 3:
                            done_piece(act_e, N_MIX + w[1], l)
                            g = w[2]
                            f(gates[:, 4 * g:4 * g + 4, :], view(duo(f"g_{g}"), 0, 4, SEQ), ACT.Tanh, scale=0.5
                              ).then_inc(free_of(f"g_{g}"), 1)
                    elif kind == "scores":
                        u = w[1]
                        _, _, _, nk, _, _ = unit_aps(u)
                        act_e.wait_ge(rowmax_ready, l * N_UNITS + u + 1)
                        for r in range(2):
                            last = f(probs[:, u % 3, r, 0:nk], probs[:, u % 3, r, 0:nk], ACT.Exp,
                                     bias=stat[:, u % 3, r:r + 1], accum_out=stat[:, u % 3, 2 + r:3 + r])
                        last.then_inc(exp_ready, 1)
                    elif kind == "turn":
                        u = w[1]
                        ukind, _, _, nk, _, _ = unit_aps(u)
                        n = nk * (1 if ukind == "B" else 2)
                        act_e.wait_ge(probsT_done, l * N_UNITS + u + 1)
                        copy(probsT[:, u % 2, 0:n], duo(f"u_{u}")[:, 0:n]).then_inc(probsT_ready, 1)
                    elif kind == "apply":
                        u = w[1]
                        ukind, cc, qt, nk, _, _ = unit_aps(u)
                        act_e.wait_ge(attn_done, l * N_UNITS + u + 1)
                        copy(o_of[ukind][:, cc, qt * P:(qt + 1) * P], duo(f"u_{u}")[:, 512:512 + P]
                             ).then_inc(free_of(f"u_{u}"), 1)
                    elif kind == "index":
                        t = w[1]
                        nk = P * (t + 1)
                        act_e.wait_ge(idx_done, l * 2 + t + 1)
                        if t:
                            act_e.wait_ge(selneg_ready, l * 2 + t)
                        f(relu[:, :, 0:nk], view(duo(f"i_{t}"), 0, 4, SEQ)[:, :, 0:nk], ACT.Relu, scale=SCALE
                          ).then_inc(relu_ready, 1)
                    elif kind == "subln":
                        freed(act_e, "u_15", l)
                        act_e.wait_ge(rope_ready, l * 5 + 5)
                        f(sq[:, 0:4], outs[:, 1], ACT.Square).then_inc(sq_ready, 1)
                        act_e.wait_ge(sums_done, l * 4 + 8 + 2)
                        f(sq[:, 4:8], view(duo("subln"), 0, 4, SEQ), ACT.Sqrt, bias=eps[:]).then_inc(std_ready, 1)
                    elif kind == "cross_q":
                        done_piece(act_e, N_MIX + w[1], l)
                        copy(qx, view(duo("xq"), 0, 2, SEQ)).then_inc(free_of("xq"), 1)
                    elif kind == "cross_kv":
                        done_piece(act_e, N_MIX + w[1], l)
                        copy(kx, view(duo("xkv"), 0, 2, SEQ)).then_inc(kx_ready, 1)
                        copy(vx, view(duo("xkv"), 512, TT, SEQ)).then_inc(free_of("xkv"), 1)
                    elif kind == "gate_up":
                        i = w[2]
                        done_piece(act_e, N_MIX + w[1], l)
                        if i >= 2:
                            freed(act_e, f"gu_{i - 2}", l)
                        f(probs[:, i % 2], view(duo(f"gu_{i}"), 0, 2, SEQ), ACT.Silu).then_inc(silu_ready, 1)

            act_e.wait_ge(x_ready, LAYERS + 1)
            f(sq[:], xT[:], ACT.Square).then_inc(sq_ready, 1)
            root("n_last", 8 + 4 * LAYERS + 1).then_inc(std_ready, 1)
            for t in range(TT):
                act_e.wait_ge(turned, 7 + t)
                copy(otok[:, t, :], duo(f"out{t}")).then_inc(otok_ready, 1)

        @block.vector
        def _(v):
            link, linked = linker(v, dve_chain)

            def wide(ap, shape):
                return ap.broadcast_to(shape)

            def norm(name, std_no, src, gain, dst, l=0, per=0):
                v.wait_ge(std_ready, l * per + std_no)
                link(v.reciprocal(rstd[:], std[:]))
                for k in range(KD):
                    last = v.scalar_tensor_tensor(dst[:, k, :], src[:, k, :], gain[:, k:k + 1], rstd[:], ALU.mult, ALU.mult)
                    if k == 0:
                        last.then_inc(free_of(name), 1)
                last.then_inc(h_ready, 1)

            v.memset(eps[:], EPS).then_inc(pad_ready, 1)
            v.memset(ua, 0.0).then_inc(pad_ready, 1)
            v.memset(ub, 0.0).then_inc(pad_ready, 1)
            v.wait_ge(consts_in, 32)
            norm("n_mem", 1, hT, g1("mem_norm"), memT)
            norm("n_mix", 2, xT, g1("norm_mix"), hT)

            freed(v, "win0")
            freed(v, "win1")
            ub_mid = ub[:, :, PAD_B:PAD_B + SEQ]
            link(v.tensor_tensor(ub_mid, ub_mid, sg, ALU.mult))

            def convolve(dst, src, taps, weight, bias, count):
                for j in range(taps):
                    for k in range(4):
                        if j:
                            v.wait_ge(dve_chain, linked[0] - 3)
                        tap = weight[:, j * 4 + k:j * 4 + k + 1]
                        if j == 0:
                            ins = v.tensor_scalar(dst[:, k, :], src[:, k, 0:SEQ], tap, bias[:, k:k + 1] if bias is not None else 0.0,
                                                  ALU.mult, ALU.add)
                        else:
                            ins = v.scalar_tensor_tensor(dst[:, k, :], src[:, k, j:j + SEQ], tap, dst[:, k, :],
                                                         ALU.mult, ALU.add)
                        linked[0] += 1
                        ins.then_inc(dve_chain, 1)
                v.wait_ge(dve_chain, linked[0])

            convolve(cb, ub, TAPS_B, g1("conv_b"), g1("conv_bias"), 4)
            v.sem_inc(conv_ready, 1)
            done_piece(v, 3)
            freed(v, "win2")
            ua_mid = ua[:, :, PAD_A:PAD_A + SEQ]
            v.tensor_tensor(ua_mid, view(duo("win3"), 0, 4, SEQ), ua_mid, ALU.mult).then_inc(free_of("win3"), 1)
            freed(v, "win3")
            convolve(yT[:, 0:4], ua, TAPS_A, g1("conv_a"), None, 4)
            freed(v, "win4")
            v.tensor_tensor(yT[:, 0:4], yT[:, 0:4], ab, ALU.mult).then_inc(conv_a_ready, 1)
            v.wait_ge(sums_done, 3)
            v.tensor_tensor(cb, cb, duo("ln_mean")[:, 0:SEQ].unsqueeze(1).broadcast_to([P, 4, SEQ]),
                            ALU.subtract).then_inc(centred, 1)
            v.wait_ge(centred, 1)
            v.sem_inc(free_of("ln_mean"), 1)
            v.wait_ge(std_ready, 3)
            link(v.reciprocal(rstd[:], std[:]))
            for k in range(4):
                last = v.scalar_tensor_tensor(cb[:, k, :], cb[:, k, :], g1("ln_g")[:, k:k + 1], rstd[:], ALU.mult, ALU.mult)
                if k == 0:
                    last.then_inc(free_of("ln_var"), 1)
            last.then_inc(yb_raw, 1)
            for half in range(2):
                v.wait_ge(std_ready, 4 + half)
                part = root_heads[:, half * 4:half * 4 + 4, :]
                link(v.reciprocal(part, part))
                for k in range(4):
                    kk = half * 4 + k
                    last = v.scalar_tensor_tensor(yT[:, kk, :], yT[:, kk, :], g1("beta")[:, kk:kk + 1],
                                                  root_heads[:, kk, :], ALU.mult, ALU.mult)
                    if k == 0:
                        last.then_inc(free_of(f"heads{half}"), 1)
            last.then_inc(y_ready, 1)
            for half in range(2):
                done_piece(v, 5 + half)
                part = xT[:, half * 4:half * 4 + 4, :]
                v.tensor_tensor(part, part, view(duo(f"wout{half}"), 0, 4, SEQ), ALU.add).then_inc(free_of(f"wout{half}"), 1)
            norm("n_ffn", 6, xT, g1("norm_ffn"), hT)

            v.wait_ge(logits_done, 1)
            nl = G + N_EXPERTS
            v.tensor_tensor(logit, view(duo("logits"), 0, TT, nl),
                            g1("route_b").unsqueeze(1).broadcast_to([P, TT, nl]), ALU.add).then_inc(free_of("logits"), 1)
            freed(v, "logits")
            lg, lex = logit[:, :, 0:G], logit[:, :, G:nl]

            def bc(ap, n):
                return ap.broadcast_to([P, TT, n])

            def first_of(dst, values_ap, peak, tmp, tmp_max, n):
                order = c("first")[:, 0:n].unsqueeze(1).broadcast_to([P, TT, n])
                link(v.tensor_tensor(tmp, values_ap, bc(peak, n), ALU.is_equal))
                link(v.tensor_tensor(tmp, tmp, order, ALU.mult))
                link(v.tensor_reduce(tmp_max, tmp, AX.X, ALU.max))
                link(v.tensor_tensor(dst, tmp, bc(tmp_max, n), ALU.is_equal))

            link(v.tensor_reduce(gmax, lg, AX.X, ALU.max))
            v.tensor_tensor(gexp, lg, bc(gmax, G), ALU.subtract).then_inc(gneg_ready, 1)
            first_of(gone, lg, gmax, gc, gcm, G)
            gone8 = gone.rearrange("p t g -> p (t g)").unsqueeze(2).broadcast_to([P, TT * G, E])
            for t in range(TT):
                link(v.tensor_tensor(le4[:, t * G:(t + 1) * G, :], lex[:, t, :].rearrange("p (g e) -> p g e", g=G),
                                     gone8[:, t * G:(t + 1) * G, :], ALU.mult))
                link(v.tensor_reduce(le[:, t, :], le4[:, t * G:(t + 1) * G, :].rearrange("p g e -> p e g"), AX.X, ALU.add))
            link(v.tensor_reduce(m1, le, AX.X, ALU.max))
            first_of(f1, le, m1, fc, fm, E)
            link(v.scalar_tensor_tensor(le2, f1, NEG, le, ALU.mult, ALU.add))
            link(v.tensor_reduce(m2, le2, AX.X, ALU.max))
            v.tensor_tensor(d12, m2, m1, ALU.subtract).then_inc(d12_ready, 1)
            first_of(f2, le2, m2, fc, fm, E)
            v.wait_ge(gexp_ready, 1)
            link(v.tensor_reduce(gsum, gexp, AX.X, ALU.add))
            link(v.reciprocal(psel, gsum))
            v.wait_ge(e12_ready, 1)
            link(v.tensor_scalar(wa, e12, 1.0, None, ALU.add))
            link(v.reciprocal(wa, wa))
            link(v.tensor_tensor(wa, wa, psel, ALU.mult))
            link(v.tensor_tensor(wb, e12, wa, ALU.mult))
            link(v.tensor_tensor(wsum, f1, bc(wa, E), ALU.mult))
            link(v.tensor_tensor(fc, f2, bc(wb, E), ALU.mult))
            link(v.tensor_tensor(wsum, wsum, fc, ALU.add))
            link(v.tensor_tensor(fsum, f1, f2, ALU.add))
            for t in range(TT):
                g8 = gone8[:, t * G:(t + 1) * G, :]
                link(v.tensor_tensor(combine[:, t * G:(t + 1) * G, :], g8,
                                     wsum[:, t, :].unsqueeze(1).broadcast_to([P, G, E]), ALU.mult))
                link(v.tensor_tensor(member[:, t * G:(t + 1) * G, :], g8,
                                     fsum[:, t, :].unsqueeze(1).broadcast_to([P, G, E]), ALU.mult))
            v.sem_inc(member_ready, 1)
            member2 = member.rearrange("p (t g) e -> p t (g e)", t=TT)
            combine2 = combine.rearrange("p (t g) e -> p t (g e)", t=TT)
            link(v.tensor_scalar(rank, member2, -4096.0, 4096.0, ALU.mult, ALU.add))
            v.wait_ge(ranks_done, 1)
            placed = view(duo("rank"), 0, 3, N_EXPERTS)
            link(v.tensor_tensor(rank, rank, placed[:, 0:2, :], ALU.add))
            link(v.tensor_reduce(most, placed[:, 2, :], AX.X, ALU.max))
            v.sem_inc(free_of("rank"), 1)
            for i in range(3):
                link(v.tensor_scalar(more[:, i:i + 1], most, float((i + 1) * SLOTS), None, ALU.is_gt))
            link(v.tensor_reduce(count, more, AX.X, ALU.add))
            link(v.tensor_scalar(passes[:, 0:1], count, 1.0, None, ALU.add))
            v.tensor_copy(passes[:, 1:2], count).then_inc(passes_ready, 1)
            v.wait_ge(passes_ready, 1)

            n_pass = v.value_load(passes[0:1, 0:1], min_val=1, max_val=MAX_PASSES)
            v.sem_inc(scat_added, 2)
            slots = c("iota").unsqueeze(1).unsqueeze(1).broadcast_to([P, TT, 2, SLOTS])
            with v.Fori(0, n_pass) as p:
                with v.Fori(0, PAIRS) as q:
                    n = p * PAIRS + q
                    v.tensor_tensor(sel, slots, expert_cols(rank, q), ALU.is_equal).then_inc(moe_chain, 1)
                    v.wait_ge(moe_chain, n + 1)
                    v.tensor_tensor(selw, sel, expert_cols(combine2, q), ALU.mult).then_inc(sel_ready, 1)
                    v.wait_ge(silu1_ready, n + 1)
                    v.wait_ge(w3_done, n + 2)
                    v.tensor_tensor(hid, silu1, psum[:, 1, 512:1024], ALU.mult).then_inc(hid_ready, 1)
                    for half, d in enumerate((0, 3)):
                        v.wait_ge(scat_done, n * 2 + half + 1)
                        part = xT[:, half * 4:half * 4 + 4, :]
                        v.tensor_tensor(part, part, view(psum[:, d, :], 0, 4, SEQ), ALU.add).then_inc(scat_added, 1)
                v.tensor_scalar(rank, rank, -float(SLOTS), None, ALU.add).then_inc(shifted, 1)
                v.wait_ge(shifted, p + 1)
            v.wait_ge(scat_added, n_pass * (2 * PAIRS) + 2)
            norm("n_final", 7, xT, g1("norm_final"), xT)
            v.wait_ge(h_ready, 4)
            v.sem_inc(x_ready, 1)

            with v.Fori(0, LAYERS) as l:
                link, linked = linker(v, layer_chain, LAYER_LINKS, l)
                for w in WORK:
                    kind = w[0]
                    if kind == "norm":
                        if w[1] == "mix":
                            v.wait_ge(vec2_in, l * 32 + 32)
                        norm(f"l_{w[1]}", 7 + {"mix": 0, "cross": 2, "ffn": 3}[w[1]] + 1, xT, g2(f"norm_{w[1]}"), hT, l, 4)
                    elif kind == "lam":
                        lv = view(g2("lambda"), 0, 2, 2, CH)
                        dots = view(score, 0, 2, CH)
                        link(v.tensor_tensor(dots, lv[:, :, 0, :], lv[:, :, 1, :], ALU.mult))
                        v.tensor_reduce(lam[:, 0:2], dots, AX.X, ALU.add).then_inc(lam_dot, 1)
                        link(v.memset(win[0:CHUNK, :, 0:CHUNK], NEG))
                        link(v.tensor_tensor(lam[:, 3:4], g2("subln"), g2("one_less"), ALU.mult))
                        v.wait_ge(lam_exp, l + 1)
                        link(v.tensor_tensor(lam[:, 2:3], lam[:, 1:2], lam[:, 0:1], ALU.subtract))
                        link(v.tensor_tensor(lam[:, 2:3], lam[:, 2:3], g2("lam_init"), ALU.subtract))
                    elif kind == "rope":
                        r, name = w[1], w[2]
                        k = 3 if name == "idx" else 4
                        v.wait_ge(rot_done, l * 5 + r + 1)
                        v.tensor_tensor(sq[:, 0:k], view(duo(f"r_{name}"), 0, 4, SEQ)[:, 0:k],
                                        c("sin").unsqueeze(1).broadcast_to([P, k, SEQ]), ALU.mult
                                        ).then_inc(free_of(f"r_{name}"), 1)
                        freed(v, f"r_{name}", l)
                        v.wait_ge(cos_ready, l * 5 + r + 1)
                        v.tensor_tensor(heads[name][:, 0:k], heads[name][:, 0:k], sq[:, 0:k], ALU.add
                                        ).then_inc(rope_ready, 1)
                        v.wait_ge(rope_ready, l * 5 + r + 1)
                    elif kind == "index_proj":
                        done_piece(v, N_MIX + w[1], l)
                        v.wait_ge(idx_raw, l + 1)
                        v.tensor_scalar(wi[:].rearrange("p t h -> p (t h)"), duo("p_idx")[:, 768:776], 0.5, None,
                                        ALU.mult).then_inc(free_of("p_idx"), 1)
                    elif kind == "scores":
                        u = w[1]
                        ukind, cc, qt, nk, _, _ = unit_aps(u)
                        v.wait_ge(scores_done, l * N_UNITS + u + 1)
                        if u >= 3:
                            v.wait_ge(probsT_done, l * N_UNITS + u - 2)
                        s, d = probs[:, u % 3, :, 0:nk], view(duo(f"u_{u}"), 0, 2, 512)[:, :, 0:nk]
                        if ukind == "X":
                            link(v.tensor_scalar(s, d, SCALE, None, ALU.mult))
                        else:
                            if ukind == "A":
                                add = win[:, 2 * cc:2 * cc + 2, nk - 1::-1] if nk == SEQ else win[:, 2 * cc:2 * cc + 2, nk - 1::-1]
                            elif ukind == "B":
                                add = c("mask")[:, SEQ - nk:SEQ].unsqueeze(1).broadcast_to([P, 2, nk])
                            else:
                                if u == 16:
                                    v.wait_ge(selneg_ready, l * 2 + 2)
                                add = selneg[:, qt, 0:nk].unsqueeze(1).broadcast_to([P, 2, nk])
                            link(v.scalar_tensor_tensor(s, d, SCALE, add, ALU.mult, ALU.add))
                        v.tensor_reduce(stat[:, u % 3, 0:2], s, AX.X, ALU.max, negate=True).then_inc(rowmax_ready, 1)
                    elif kind == "turn":
                        u = w[1]
                        ukind, cc, qt, nk, _, _ = unit_aps(u)
                        st = stat[:, u % 3]
                        v.wait_ge(exp_ready, l * N_UNITS + u + 1)
                        link(v.reciprocal(st[:, 4:6], st[:, 2:4]))
                        if ukind == "B":
                            link(v.tensor_tensor(st[:, 5:6], st[:, 5:6], lam[:, 2:3], ALU.mult))
                            link(v.tensor_scalar(probs[:, u % 3, 1, 0:nk], probs[:, u % 3, 1, 0:nk], st[:, 5:6], None, ALU.mult))
                            v.scalar_tensor_tensor(probs[:, u % 3, 0, 0:nk], probs[:, u % 3, 0, 0:nk], st[:, 4:5],
                                                   probs[:, u % 3, 1, 0:nk], ALU.mult, ALU.add).then_inc(probs_ready, 1)
                        else:
                            s = probs[:, u % 3, :, 0:nk]
                            v.tensor_tensor(s, s, st[:, 4:6].unsqueeze(2).broadcast_to([P, 2, nk]), ALU.mult
                                            ).then_inc(probs_ready, 1)
                    elif kind == "index":
                        t = w[1]
                        nk = P * (t + 1)
                        v.wait_ge(relu_ready, l * 2 + t + 1)
                        v.sem_inc(free_of(f"i_{t}"), 1)
                        sc = score[:, 0:nk]
                        for h in range(4):
                            add = c("mask")[:, SEQ - nk:SEQ] if h == 0 else sc
                            link(v.scalar_tensor_tensor(sc, relu[:, (h % 2) * 2 + h // 2, 0:nk], wi[:, t, h:h + 1], add,
                                                        ALU.mult, ALU.add))
                        for _ in range(TOPK // 8):
                            v.sem_inc(held, 1)
                            link(v.max(top8[:], sc))
                            v.sem_inc(held, 1)
                            link(v.match_replace(sc, top8[:], sc, TAKEN))
                        v.tensor_scalar(selneg[:, t, 0:nk], sc, TAKEN / 3, NEG, ALU.is_gt, ALU.mult).then_inc(selneg_ready, 1)
                        v.wait_ge(selneg_ready, l * 2 + t + 1)
                    elif kind == "subln":
                        v.wait_ge(std_ready, l * 4 + 7 + 2)
                        v.sem_inc(free_of("subln"), 1)
                        link(v.reciprocal(sq[:, 4:8], sq[:, 4:8]))
                        v.scalar_tensor_tensor(outs[:, 1], outs[:, 1], lam[:, 3:4], sq[:, 4:8], ALU.mult, ALU.mult
                                               ).then_inc(subln_ready, 1)
                    elif kind == "up":
                        b = w[2]
                        done_piece(v, N_MIX + w[1], l)
                        if b == 0:
                            v.wait_ge(gates_ready, l * 6 + 6)
                        for half in range(2):
                            name = f"up_{b}_{half}"
                            y = hT[:, half * 4:half * 4 + 4, :]
                            term = y if b == 0 else sq[:, half * 4:half * 4 + 4, :]
                            v.tensor_tensor(term, view(duo(name), 0, 4, SEQ),
                                            gates[:, 8 * b + 4 * half:8 * b + 4 * half + 4, :], ALU.mult
                                            ).then_inc(free_of(name), 1)
                            freed(v, name, l)
                            if b:
                                ins = v.tensor_tensor(y, y, term, ALU.add)
                                if b == 2 and half == 1:
                                    ins.then_inc(mixed_ready, 1)
                                else:
                                    link(ins)
                    elif kind in ("out", "cross_o"):
                        done_piece(v, N_MIX + w[1], l)
                        for half in ([w[2]] if kind == "out" else range(2)):
                            name = f"out_{half}" if kind == "out" else f"xo_{half}"
                            part = xT[:, half * 4:half * 4 + 4, :]
                            v.tensor_tensor(part, part, view(duo(name), 0, 4, SEQ), ALU.add).then_inc(free_of(name), 1)
                    elif kind == "gate_up":
                        i = w[2]
                        v.wait_ge(silu_ready, l * (KF // 2) + i + 1)
                        v.tensor_tensor(act[:, 2 * i:2 * i + 2, :], probs[:, i % 2], view(duo(f"gu_{i}"), 512, 2, SEQ),
                                        ALU.mult).then_inc(free_of(f"gu_{i}"), 1)
                    elif kind == "down":
                        done_piece(v, N_MIX + N_LAYER - 1, l)
                        v.tensor_tensor(xT[:, 0:4], xT[:, 0:4], view(duo("dn_0"), 0, 4, SEQ), ALU.add
                                        ).then_inc(free_of("dn_0"), 1)
                        freed(v, "dn_0", l)
                        v.tensor_tensor(xT[:, 4:8], xT[:, 4:8], view(duo("dn_1"), 0, 4, SEQ), ALU.add).then_inc(x_ready, 1)
                        v.wait_ge(x_ready, l + 2)
                        v.sem_inc(free_of("dn_1"), 1)
                assert linked[0] == LAYER_LINKS, linked

            link, linked = linker(v, last_chain)
            norm("n_last", 7 + 4 * LAYERS + 1, xT, g1("last_norm"), hT)

        @block.gpsimd
        def _(pool):
            pool.wait_ge(consts_in, 32)
            with pool.Fori(0, LAYERS) as l:
                for w in WORK:
                    kind = w[0]
                    if kind == "rope":
                        r, name = w[1], w[2]
                        k = 3 if name == "idx" else 4
                        pool.wait_ge(rot_done, l * 5 + r + 1)
                        pool.tensor_tensor(heads[name][:, 0:k], heads[name][:, 0:k],
                                           c("cos").unsqueeze(1).broadcast_to([P, k, SEQ]), ALU.mult).then_inc(cos_ready, 1)
                    elif kind == "gates" and w[3] == 3:
                        g = w[2]
                        freed(pool, f"g_{g}", l)
                        pool.sem_inc(held, 1)
                        part = gates[:, 4 * g:4 * g + 4, :]
                        pool.tensor_scalar(part, part, 0.5, 0.5, ALU.mult, ALU.add).then_inc(gates_ready, 1)


def constants():
    f = np.float32
    p = np.arange(P)
    out = {}
    out["ident"] = np.eye(P, dtype=f)
    out["mean_model"] = np.full((P, P), 1.0 / D, f)
    out["mean_mixb"] = np.full((P, P), 1.0 / D_A, f)
    out["mean_head"] = (p[:, None] // CH == p[None] // CH).astype(f) / CH
    out["mean_sub"] = np.full((P, P), 1.0 / (2 * CH), f)
    turn = np.zeros((P, P), f)
    for to in range(P):
        turn[to + 32 if to % CH < 32 else to - 32, to] = -1.0 if to % CH < 32 else 1.0
    out["rotate"] = turn
    out["before"] = (p[:, None] < p[None]).astype(f)
    out["ones"] = np.ones((P, P), f)
    inv = f(10000.0) ** (-np.arange(0, CH, 2, dtype=f) / f(CH))
    ang = (np.arange(SEQ, dtype=f)[None, :] * inv[p % 32][:, None]).astype(f)
    out["cos"], out["sin"] = np.cos(ang).astype(f), np.sin(ang).astype(f)
    mask = np.zeros((P, SEQ), f)
    mask[:CHUNK, SEQ - CHUNK:] = NEG
    out["mask"] = mask
    out["iota"] = np.broadcast_to(np.arange(SLOTS, dtype=f), (P, SLOTS))
    out["first"] = np.broadcast_to(np.arange(PER_GROUP, 0, -1).astype(f), (P, PER_GROUP))
    return np.ascontiguousarray(np.concatenate([out[n] for n in CONST], 1))


def kernel(x, norm_mix_g, w_in, conv_a_w, conv_b_w, conv_b_bias, ln_b_g, ln_b_b, beta_a, beta_b, w_out,
           norm_ffn_g, w_route_group, b_route_group, w_route_expert, b_route_expert, w1, w3, w2,
           norm_final_g, mem_2, norm_mix_2, w_in_2, rel_bias_a_2, lambda_vecs_2, subln_b_2, w_up_a_2,
           w_up_b_2, w_up_c_2, w_out_2, norm_cross_2, w_q_x_2, w_kv_x_2, w_o_x_2, norm_ffn_2, w_gu_2,
           w_down_2, mem_norm_2, final_norm_2):
    import concourse.bacc as bacc
    from concourse.bass_utils import run_bass_kernel_spmd as run

    def cols(a):
        a = np.asarray(a)
        a = a.reshape(-1, a.shape[-1] // P, P)
        return np.transpose(a, (2, 0, 1)).reshape(P, -1)

    def rows(a):
        a = np.asarray(a).reshape(1, -1)
        return np.broadcast_to(a, (P, a.shape[1]))

    wr = np.concatenate([np.asarray(w_route_group[0]), np.asarray(w_route_expert[0])], 1)
    wr = np.transpose(wr.reshape(KD, P, -1), (1, 0, 2)).reshape(P, -1)
    parts1 = {"norm_mix": cols(norm_mix_g[0]), "conv_a": cols(conv_a_w[0]), "conv_b": cols(conv_b_w[0]),
              "conv_bias": cols(conv_b_bias[0]), "ln_g": cols(ln_b_g[0]), "ln_b": cols(ln_b_b[0]),
              "beta": np.concatenate([cols(beta_a[0]), cols(beta_b[0])], 1), "norm_ffn": cols(norm_ffn_g[0]),
              "norm_final": cols(norm_final_g), "mem_norm": cols(mem_norm_2), "last_norm": cols(final_norm_2),
              "route_b": np.concatenate([rows(b_route_group[0]), rows(b_route_expert[0])], 1), "route_w": wr}
    vec1 = np.concatenate([parts1[n] for n in VEC1], 1)
    layers = []
    for l in range(LAYERS):
        init = 0.8 - 0.6 * float(np.exp(-0.3 * l))
        parts2 = {"norm_mix": cols(norm_mix_2[l]), "norm_cross": cols(norm_cross_2[l]), "norm_ffn": cols(norm_ffn_2[l]),
                  "subln": cols(subln_b_2[l]), "lam_init": np.full((P, 1), init, np.float32),
                  "one_less": np.full((P, 1), 1.0 - init, np.float32), "lambda": rows(lambda_vecs_2[l])}
        layers.append(np.concatenate([parts2[n] for n in VEC2], 1))
    rel = np.asarray(rel_bias_a_2)
    relpad = np.concatenate([np.zeros(rel.shape[:2] + (CHUNK,), rel.dtype), rel], 2)
    arrays = {"x": x, "mem": mem_2, "cst": constants(), "vec1": vec1, "vec2": np.stack(layers), "relpad": relpad,
              "w_in": w_in, "w_out": w_out, "w1": w1, "w3": w3, "w2": w2, "w_in_2": w_in_2, "w_up_a": w_up_a_2,
              "w_up_b": w_up_b_2, "w_up_c": w_up_c_2, "w_out_2": w_out_2, "w_q_x": w_q_x_2, "w_kv_x": w_kv_x_2,
              "w_o_x": w_o_x_2, "w_gu": w_gu_2, "w_down": w_down_2}
    arrays = {n: np.ascontiguousarray(a) for n, a in arrays.items()}
    nc = bacc.Bacc("TRN2", target_bir_lowering=False, num_devices=1, dynamic_dma_scratch_size=1024)
    args = [nc.dram_tensor(n, a.shape, mybir.dt.from_np(a.dtype), kind="ExternalInput").ap() for n, a in arrays.items()]
    out = nc.dram_tensor("out", (1, SEQ, D), F32, kind="ExternalOutput").ap()
    build(nc, *args, out)
    return run(nc, [arrays], core_ids=[0]).results[0]["out"]
```

```python
from contextlib import ExitStack

import numpy as np

import concourse.bass as bass
from concourse import mybir

F32 = mybir.dt.float32
F32R = mybir.dt.float32r
I32 = mybir.dt.int32
ALU = mybir.AluOpType
ACT = mybir.ActivationFunctionType
AX = mybir.AxisListType

P = 128
SEQ = 256
D = 1024
KD = D // P
TT = SEQ // P
HALF = 512
D_A = 512
CH = 64
TAPS_A, TAPS_B = 3, 31
PAD_A, PAD_B = 1, 15
EPS = 1e-6
N_GROUPS, PER_GROUP = 4, 8
N_EXPERTS = N_GROUPS * PER_GROUP
PAIRS = N_EXPERTS // 2
D_EXPERT = 512
SLOTS = 64
MAX_PASSES = SEQ // SLOTS
LAYERS = 2
CHUNK = 64
REL = 320
REL_ROW = CHUNK + REL
TOPK = min(256, SEQ // 4)
D_FF = 2816
KF = D_FF // P
SCALE = float(CH) ** -0.5
NEG = -1.0e30
LAYER_LINKS = 124
TAKEN = -3.0e38

RING = 6
RAW = 3
PARTS = 4
PIECE = 4096
DUOS = 4
DUO = 1024

CONST = {}
_at = 0
for _name, _width in (("ident", P), ("mean_model", P), ("mean_mixb", P), ("mean_head", P), ("mean_sub", P),
                      ("rotate", P), ("before", P), ("ones", P), ("cos", SEQ), ("sin", SEQ), ("mask", SEQ),
                      ("iota", SLOTS), ("first", PER_GROUP)):
    CONST[_name] = (_at, _at + _width)
    _at += _width
N_CONST = _at

VEC1 = {}
_at = 0
for _name, _width in (("norm_mix", KD), ("conv_a", 4 * TAPS_A), ("conv_b", 4 * TAPS_B), ("conv_bias", 4), ("ln_g", 4),
                      ("ln_b", 4), ("beta", 8), ("norm_ffn", KD), ("norm_final", KD), ("mem_norm", KD),
                      ("last_norm", KD), ("route_b", N_GROUPS + N_EXPERTS),
                      ("route_w", KD * (N_GROUPS + N_EXPERTS))):
    VEC1[_name] = (_at, _at + _width)
    _at += _width
N_VEC1 = _at

VEC2 = {}
_at = 0
for _name, _width in (("norm_mix", KD), ("norm_cross", KD), ("norm_ffn", KD), ("subln", 1), ("lam_init", 1),
                      ("one_less", 1), ("lambda", 4 * CH)):
    VEC2[_name] = (_at, _at + _width)
    _at += _width
N_VEC2 = _at

MIX_PIECES = [("w_in", c) for c in (3, 4, 0, 2, 1)] + [("w_out", 0), ("w_out", 1)]
Q_A, K_A, V_A, Q_B, K_B, V_B, Q_C, K_C, V_C = (("in", 512 * i, 512) for i in range(9))
IDX = ("in", 4608, 324)
GATES = [("in", 4932 + 512 * i, 512) for i in range(6)]
DOWN = [(0, 3), (3, 6), (6, 9), (9, 12), (12, 15), (15, 18), (18, 22)]
LAYER_PIECES = ([Q_A, K_A, V_A, Q_B, K_B, V_B, IDX] + GATES[:2] + [Q_C, K_C, V_C] + GATES[2:]
                + [("up", b) for b in range(3)] + [("out", 0), ("out", 1), ("q_x",), ("kv_x",), ("o_x",)]
                + [("gu", i) for i in range(KF // 2)] + [("down", i) for i in range(len(DOWN))])
N_MIX, N_LAYER = len(MIX_PIECES), len(LAYER_PIECES)
assert N_LAYER % RAW == 0


def is_split(piece):
    return piece[0] == "gu" or (piece[0] == "in" and piece[2] == HALF)


SPLIT_THROUGH = [4 * sum(is_split(p) for p in LAYER_PIECES[:i + 1]) for i in range(N_LAYER)]
DIRECT_THROUGH = [sum(not is_split(p) for p in LAYER_PIECES[:i + 1]) for i in range(N_LAYER)]
N_CHUNKS, N_DIRECT = SPLIT_THROUGH[-1], DIRECT_THROUGH[-1]
LOADS = [2 if p[0] == "gu" else 1 for p in LAYER_PIECES]

EARLY = (["mem0", "mem1", "x0", "x1", "n_mem", "n_mix"] + [f"win{i}" for i in range(5)]
         + ["ln_mean", "ln_var", "heads0", "heads1", "wout0", "wout1", "n_ffn", "tok0", "tok1", "logits", "rank"])
LATE = ["n_final"]
LAST = ["n_last", "out0", "out1"]

UNITS = ([("A", c, t) for c in range(4) for t in range(TT)] + [("B", c, t) for c in range(4) for t in range(TT)]
         + [("C", c, t) for c in range(4) for t in range(TT)] + [("X", c, t) for c in range(2) for t in range(TT)])
N_UNITS = len(UNITS)
ROPES = ["qb", "kb", "idx", "qc", "kc"]

def attention(first, last, extra):
    steps = []
    for s in range(first, last + 2):
        if s < last:
            steps.append(("scores", s))
        steps += extra.get(s, [])
        if first <= s - 1 < last:
            steps.append(("turn", s - 1))
        if first <= s - 2 < last:
            steps.append(("apply", s - 2))
    return steps


def gate_parts(starts, piece, gate):
    return {s + o: [("gates", piece + i, gate + i, o)] for i, s in enumerate(starts) for o in range(4)}


WORK = ([("norm", "mix"), ("lam",), ("proj", 0, "qa"), ("proj", 1, "ka"), ("proj_v", 2, "va"),
         ("proj", 3, "qb"), ("proj", 4, "kb"), ("rope", 0, "qb"), ("proj_v", 5, "vb"), ("rope", 1, "kb"),
         ("index_proj", 6)]
        + [("rope", 2, "idx")]
        + attention(0, 8, gate_parts((1, 5), 7, 0))
        + [("index", 0), ("index", 1), ("proj", 9, "qc"), ("proj", 10, "kc"), ("rope", 3, "qc"),
           ("proj_v", 11, "vc"), ("rope", 4, "kc")]
        + attention(8, 24, gate_parts((9, 13, 17, 21), 12, 2))
        + [("subln",)] + [("up", 16 + b, b) for b in range(3)]
        + [("out", 19, 0), ("out", 20, 1), ("norm", "cross"), ("cross_q", 21), ("cross_kv", 22)]
        + attention(24, 28, {}) + [("cross_o", 23), ("norm", "ffn")]
        + [("gate_up", 24 + i, i) for i in range(KF // 2)] + [("down",)])


def with_splits(work):
    out, split, used = [], 0, 0
    piece_of = [i for i, p in enumerate(LAYER_PIECES) if is_split(p) for _ in range(4)]
    direct_left = [i for i, p in enumerate(LAYER_PIECES) if not is_split(p)]
    for w in work:
        used += {"proj": 4, "proj_v": 4, "gate_up": 4, "gates": 1}.get(w[0], 0)
        if w[0] == "turn":
            out.append(w)
        while (w[0] not in ("gates", "scores", "apply") and split < N_CHUNKS and split < used + PARTS - 1
               and not (direct_left and direct_left[0] <= piece_of[split] - RAW)):
            out.append(("split", split))
            split += 1
        assert split >= used
        if w[0] != "turn":
            out.append(w)
        if direct_left and w[0] in ("index_proj", "up", "out", "cross_q", "cross_kv", "cross_o"):
            assert direct_left.pop(0) == w[1]
    assert split == used == N_CHUNKS
    return out


WORK_SPLIT = with_splits(WORK)
POOL_CHUNKS = range(SPLIT_THROUGH[8], SPLIT_THROUGH[11])


def low_parts(n, on_pool):
    return sum((j in POOL_CHUNKS) == on_pool for j in range(n + 1))


def tenants(work):
    names = []
    for w in work:
        kind = w[0]
        if kind == "norm":
            names.append(f"l_{w[1]}")
        elif kind in ("proj", "proj_v"):
            names.append(f"p_{w[2]}")
        elif kind == "rope":
            names.append(f"r_{w[2]}")
        elif kind == "index_proj":
            names.append("p_idx")
        elif kind == "index":
            names.append(f"i_{w[1]}")
        elif kind == "gates":
            names += [f"g_{w[2]}"] if w[3] == 0 else []
        elif kind == "scores":
            names.append(f"u_{w[1]}")
        elif kind == "subln":
            names.append("subln")
        elif kind == "up":
            names += [f"up_{w[2]}_0", f"up_{w[2]}_1"]
        elif kind == "out":
            names.append(f"out_{w[2]}")
        elif kind == "cross_q":
            names.append("xq")
        elif kind == "cross_kv":
            names.append("xkv")
        elif kind == "cross_o":
            names += ["xo_0", "xo_1"]
        elif kind == "gate_up":
            names.append(f"gu_{w[2]}")
        elif kind == "down":
            names += ["dn_0", "dn_1"]
    return names


def seat(names, before, at):
    units = others = 0
    for name in names:
        assert name not in at, name
        if name.startswith("u_"):
            d, units = units % 3, units + 1
        elif name.startswith("g_"):
            d = 3
        else:
            d, others = others % DUOS, others + 1
        at[name] = (d, before[d])
        before[d] += 1


def build(nc, x, mem, cst, vec1, vec2, relpad, w_in, w_out, w1, w3, w2, w_in_2, w_up_a, w_up_b, w_up_c,
          w_out_2, w_q_x, w_kv_x, w_o_x, w_gu, w_down, out):
    seats, tenancies = {}, [0] * DUOS
    seat(EARLY + LATE, tenancies, seats)
    start = list(tenancies)
    seat(tenants(WORK), tenancies, seats)
    layer_tenancies = [b - a for a, b in zip(start, tenancies)]
    for i, name in enumerate(LAST):
        d = i % DUOS
        seats[name] = (d, tenancies[d] + (LAYERS - 1) * layer_tenancies[d])

    with ExitStack() as ctx:
        def sb(name, shape, dt=F32):
            return ctx.enter_context(nc.sbuf_tensor(name, shape, dt))

        def sem(name):
            return ctx.enter_context(nc.semaphore(name))

        psum = ctx.enter_context(nc.psum_tensor("psum", [P, DUOS, DUO], F32))

        with ExitStack() as first_block:
            ring = first_block.enter_context(nc.sbuf_tensor("ring", [P, RING, PIECE], F32))
        raw = sb("raw", [P, RAW, PIECE])
        w_hi = sb("w_hi", [P, PARTS, KD * P], F32R)
        w_lo = sb("w_lo", [P, PARTS, KD * P], F32R)
        h_hi = sb("h_hi", [P, KD, SEQ], F32R)
        h_lo = sb("h_lo", [P, KD, SEQ], F32R)
        xT = sb("xT", [P, KD, SEQ])
        hT = sb("hT", [P, KD, SEQ])
        sq = sb("sq", [P, KD, SEQ])
        consts = sb("consts", [P, N_CONST])
        memT = sb("memT", [P, KD, SEQ])
        std = sb("std", [P, SEQ])
        rstd = sb("rstd", [P, SEQ])
        eps = sb("eps", [P, 1])
        v1 = sb("v1", [P, N_VEC1])
        v2 = sb("v2", [P, N_VEC2])
        big = sb("big", [P, 24 * SEQ])
        qk = sb("qk", [P, 16 * SEQ])
        vals = sb("vals", [P, 2, TT, HALF])
        outs = sb("outs", [P, 3, 4, SEQ])
        win = sb("win", [P, 8, SEQ])
        probs = sb("probs", [P, 3, 2, SEQ])
        probsT = sb("probsT", [P, 2, 2 * TT * P])
        stat = sb("stat", [P, 3, 6])
        qiT = sb("qiT", [P, 3, SEQ])
        wi = sb("wi", [P, TT, 4])
        score = sb("score", [P, SEQ])
        top8 = sb("top8", [P, 8])
        lam = sb("lam", [P, 8])
        route = vals[:, 0].rearrange("p t n -> p (t n)")
        passes = sb("passes", [P, 2], I32)

        def c(name):
            a, b = CONST[name]
            return consts[:, a:b]

        def g1(name):
            a, b = VEC1[name]
            return v1[:, a:b]

        def g2(name):
            a, b = VEC2[name]
            return v2[:, a:b]

        ident = c("ident")

        def view(t, at, *dims):
            n = int(np.prod(dims))
            ap = t[:, at:at + n]
            if len(dims) == 2:
                return ap.rearrange("p (a b) -> p a b", a=dims[0])
            if len(dims) == 3:
                return ap.rearrange("p (a b c) -> p a b c", a=dims[0], b=dims[1])
            return ap

        mtok = view(big, 0, TT, D)
        xtok = view(big, TT * D, TT, D)
        ua = view(qk, 0, 4, SEQ + 2 * PAD_A)
        ub = view(qk, 4 * (SEQ + 2 * PAD_A), 4, SEQ + 2 * PAD_B)
        ab = view(big, 4096, 4, SEQ)
        sg = view(big, 5120, 4, SEQ)
        cb = outs[:, 0]
        yT = view(big, 0, KD, SEQ)
        root_heads = view(big, 4096, KD, SEQ)
        htok = view(big, 0, TT, D)
        sel = view(big, 2048, TT, 2, SLOTS)
        selw = view(big, 2048 + 256, TT, 2, SLOTS)
        xs = view(big, 2048 + 512, KD, P)
        selwT = view(big, 2048 + 512 + 1024, SEQ)
        silu1 = view(big, 3840 + 256, D_EXPERT)
        hid = view(big, 3840 + 768, D_EXPERT)
        hidT = view(big, 3840 + 1280, 4, P)
        ysb = view(qk, 0, D)
        gates = view(big, 0, 24, SEQ)
        act = view(big, 0, KF, SEQ)
        heads = {n: view(qk, 4 * SEQ * i, 4, SEQ) for i, n in enumerate(("qa", "ka", "qb", "kb"))}
        heads["qc"], heads["kc"] = heads["qa"], heads["ka"]
        heads["idx"] = qiT
        values = {"va": vals[:, 0], "vb": vals[:, 1], "vc": vals[:, 0]}
        relu = [probs[:, 1].rearrange("p r (b n) -> p (r b) n", b=2), win[:, 0:4]]
        selneg = win[:, 4:6]
        qx, kx = heads["qb"][:, 0:2], heads["qb"][:, 2:4]
        vx = view(qk, 12 * SEQ, TT, SEQ)
        ox = outs[:, 0, 0:2]
        o_of = {"A": outs[:, 0], "B": outs[:, 1], "C": outs[:, 2], "X": ox}
        otok = view(big, 0, TT, D)

        used = [0]

        def small(*dims):
            n = int(np.prod(dims))
            at = used[0]
            used[0] += n
            assert used[0] <= 1024
            return view(route, at, *dims) if len(dims) > 1 else route[:, at:at + n]

        G, E = N_GROUPS, PER_GROUP
        logit = small(TT, G + N_EXPERTS)
        gmax, gsum, psel = small(TT, 1), small(TT, 1), small(TT, 1)
        gexp = small(TT, G)
        gc, gone = small(TT, G), small(TT, G)
        gcm = small(TT, 1)
        le4 = small(TT * G, E)
        le = small(TT, E)
        m1, m2, d12, e12, wa, wb = (small(TT, 1) for _ in range(6))
        f1, f2, fc, le2 = (small(TT, E) for _ in range(4))
        fm = small(TT, 1)
        wsum, fsum = small(TT, E), small(TT, E)
        member = small(TT * G, E)
        combine = small(TT * G, E)
        rank = small(TT, N_EXPERTS)
        count, most, more = small(1), small(1), small(3)

        ring_full = [sem(f"ring_full{i}") for i in range(RING)]
        moe_full = [sem(f"moe_full{i}") for i in range(RING)]
        duo_free = [sem(f"duo_free{i}") for i in range(DUOS)]
        piece_done = sem("piece_done")
        raw_full = [sem(f"raw_full{i}") for i in range(RAW)]
        (consts_in, mem_in, x_in, vec2_in, turned, sq_ready, sums_done, std_ready, h_ready, x_ready,
         dve_chain, act_chain, pad_ready, conv_a_ready, gate_b_ready, ub_ready, yb_raw, centred, silu_b, y_ready,
         logits_done, gexp_ready, gneg_ready, d12_ready, e12_ready, member_ready, ranks_done, passes_ready,
         credit_moe, sel_ready, gathered, xs_ready, w1_done, w3_done, silu1_ready, hid_ready, hidT_done, hidT_ready,
         w2_done, ysb_ready, scat_done, scat_added, moe_chain,
         lam_dot, lam_exp, rot_done, cos_ready, rope_ready, idx_raw, idx_done, relu_ready, selneg_ready,
         scores_done, rowmax_ready, exp_ready, probs_ready, probsT_done, probsT_ready, attn_done, subln_ready,
         direct_done, chunk_used, w_hi_ready, w_lo_ready, w_lo_pool_ready, h_half, h_hi_ready, h_lo_ready, gates_ready, held, conv_ready, shifted, kx_ready, mixed_ready, silu_ready, layer_chain, last_chain, otok_ready, out_done) = (sem(n) for n in (
            "consts_in mem_in x_in vec2_in turned sq_ready sums_done std_ready h_ready x_ready "
            "dve_chain act_chain pad_ready conv_a_ready gate_b_ready ub_ready yb_raw centred silu_b y_ready "
            "logits_done gexp_ready gneg_ready d12_ready e12_ready member_ready ranks_done passes_ready "
            "credit_moe sel_ready gathered xs_ready w1_done w3_done silu1_ready hid_ready hidT_done hidT_ready "
            "w2_done ysb_ready scat_done scat_added moe_chain "
            "lam_dot lam_exp rot_done cos_ready rope_ready idx_raw idx_done relu_ready selneg_ready "
            "scores_done rowmax_ready exp_ready probs_ready probsT_done probsT_ready attn_done subln_ready "
            "direct_done chunk_used w_hi_ready w_lo_ready w_lo_pool_ready h_half h_hi_ready h_lo_ready gates_ready held conv_ready shifted kx_ready mixed_ready silu_ready layer_chain last_chain otok_ready out_done").split())

        def duo(name):
            return psum[:, seats[name][0], :]

        def enter(eng, name, l=0):
            d, n = seats[name]
            eng.wait_ge(duo_free[d], l * layer_tenancies[d] + n + 1)

        def freed(eng, name, l=0):
            d, n = seats[name]
            eng.wait_ge(duo_free[d], l * layer_tenancies[d] + n + 2)

        def free_of(name):
            return duo_free[seats[name][0]]

        def slot_of(i):
            return ring[:, i % RING, :]

        def done_piece(eng, i):
            eng.wait_ge(piece_done, i + 1)

        def arrived(eng, i):
            eng.wait_ge(ring_full[i % RING], (i // RING + 1) * 16)

        def raw_of(i):
            return raw[:, i % RAW, :]

        def raw_arrived(eng, i, l):
            so_far = sum(LOADS[j] for j in range(i % RAW, i + 1, RAW))
            a_layer = sum(LOADS[j] for j in range(i % RAW, N_LAYER, RAW))
            eng.wait_ge(raw_full[i % RAW], (l * a_layer + so_far) * 16)

        def product_done(eng, i, l):
            if is_split(LAYER_PIECES[i]):
                eng.wait_ge(chunk_used, l * N_CHUNKS + SPLIT_THROUGH[i] + PARTS)
            else:
                eng.wait_ge(direct_done, l * N_DIRECT + DIRECT_THROUGH[i] + RAW)

        def parts_ready(eng, n, l):
            if n in POOL_CHUNKS:
                eng.wait_ge(w_lo_pool_ready, l * len(POOL_CHUNKS) + low_parts(n, True))
            else:
                eng.wait_ge(w_lo_ready, l * (N_CHUNKS - len(POOL_CHUNKS)) + low_parts(n, False))

        def low_part(eng, n, l):
            eng.wait_ge(w_hi_ready, l * N_CHUNKS + n + 1)
            if eng is nc.gpsimd:
                eng.sem_inc(held, 1)
            return eng.tensor_tensor(chunk_part(w_lo, n), chunk_raw(n), chunk_part(w_hi, n).bitcast(F32), ALU.subtract)

        def raw_free(eng, i, l):
            before, back = (i - RAW, 0) if i >= RAW else (i - RAW + N_LAYER, 1)
            if is_split(LAYER_PIECES[before]):
                assert not back
                parts_ready(eng, SPLIT_THROUGH[before] - 1, l)
            else:
                eng.wait_ge(direct_done, l * N_DIRECT + DIRECT_THROUGH[before] + RAW - back * N_DIRECT)

        def chunk_source(n):
            i = next(j for j in range(N_LAYER) if SPLIT_THROUGH[j] > n)
            return i, n - (SPLIT_THROUGH[i] - 4)

        def chunk_raw(n):
            i, o = chunk_source(n)
            whole = view(raw_of(i), 0, KD, HALF)
            return whole[:, 2 * o:2 * o + 2, :] if is_values(i) else whole[:, :, o * P:(o + 1) * P]

        def is_values(i):
            return LAYER_PIECES[i] in (V_A, V_B, V_C)

        def chunk_part(parts, n):
            i, _ = chunk_source(n)
            dims = (2, HALF) if is_values(i) else (KD, P)
            return view(parts[:, n % PARTS, :], 0, *dims)

        def linker(eng, chain, per=0, index=0):
            linked = [0]

            def link(ins):
                linked[0] += 1
                ins.then_inc(chain, 1)
                eng.wait_ge(chain, index * per + linked[0])

            return link, linked

        def moe_ap(w):
            return w.rearrange("l e (k p) n -> (l e) p k n", p=P)

        w1_v, w3_v, w2_v = moe_ap(w1), moe_ap(w3), moe_ap(w2)

        def expert_cols(ap, q):
            return ap[:, :, bass.ds(q * 2, 2)].unsqueeze(3).broadcast_to([P, TT, 2, SLOTS])

        def unit_aps(u):
            kind, cc, qt = UNITS[u]
            nk = SEQ if kind == "X" else P * (qt + 1)
            if kind == "X":
                q, k = qx, kx
            else:
                q, k = {"A": (heads["qa"], heads["ka"]), "B": (heads["qb"], heads["kb"]),
                        "C": (heads["qc"], heads["kc"])}[kind]
            return kind, cc, qt, nk, q, k

        block = ctx.enter_context(nc.Block())

        @block.sync
        def _(sp):
            sp.dma_start(consts[:], cst).then_inc(consts_in, 16)
            sp.dma_start(mtok, mem.rearrange("b (t p) d -> p (b t) d", p=P)).then_inc(mem_in, 16)
            sp.dma_start(xtok, x.rearrange("b (t p) d -> p (b t) d", p=P)).then_inc(x_in, 16)
            sp.dma_start(v1[:], vec1).then_inc(consts_in, 16)
            w_in_v = w_in.rearrange("l (k p) n -> p (l k) n", p=P)
            w_out_v = w_out.rearrange("l (k p) n -> p (l k) n", p=P)
            for i, (name, col) in enumerate(MIX_PIECES):
                if i >= RING:
                    done_piece(sp, i - RING)
                src = w_in_v if name == "w_in" else w_out_v
                sp.dma_start(view(ring[:, i % RING, :], 0, KD, HALF),
                             src[:, :, col * HALF:(col + 1) * HALF]).then_inc(ring_full[i % RING], 16)

            def load_pair(q, n):
                for at, done, src, k in ((0, w1_done, w1_v, KD), (2, w3_done, w3_v, KD), (4, w2_done, w2_v, 4)):
                    sp.wait_ge(done, n + 1)
                    for e in range(2):
                        sp.dma_start(view(ring[:, at + e, :], 0, k, PIECE // k),
                                     src[bass.ds(q * 2 + e, 1)].rearrange("a p k n -> (a p) k n")
                                     ).then_inc(moe_full[at + e], 16)

            done_piece(sp, N_MIX - 1)
            with sp.Fori(0, PAIRS) as q:
                load_pair(q, q)
            sp.wait_ge(passes_ready, 1)
            n_pass = sp.value_load(passes[0:1, 0:1], min_val=1, max_val=MAX_PASSES)
            n_more = sp.value_load(passes[0:1, 1:2], min_val=0, max_val=MAX_PASSES - 1)
            with sp.If(n_more):
                with sp.Fori(1, n_pass) as p:
                    with sp.Fori(0, PAIRS) as q:
                        load_pair(q, p * PAIRS + q)
            sp.wait_ge(w1_done, n_pass * PAIRS + 1)
            sp.sem_inc(held, 1)
            sp.wait_ge(w3_done, n_pass * PAIRS + 1)
            sp.sem_inc(held, 1)

            with sp.Fori(0, LAYERS) as l:
                for j, piece in enumerate(LAYER_PIECES):
                    if j == RAW:
                        sp.wait_ge(h_ready, l * 3 + 4)
                        sp.dma_start(v2[:], vec2[bass.ds(l, 1)].rearrange("a p n -> (a p) n")).then_inc(vec2_in, 16)
                        window = bass.AP(relpad.tensor, l * (8 * REL_ROW), [[1, P], [REL_ROW, 8], [1, SEQ]])
                        sp.dma_start(win[:], window).then_inc(vec2_in, 16)
                    raw_free(sp, j, l)
                    slot = raw_of(j)
                    kind = piece[0]

                    def rows(w, k):
                        return w[bass.ds(l, 1)].rearrange("a (k p) n -> (a p) k n", p=P)

                    if kind == "in":
                        _, at, n = piece
                        dst, src = view(slot, 0, KD, n), rows(w_in_2, KD)[:, :, at:at + n]
                    elif kind == "up":
                        w = (w_up_a, w_up_b, w_up_c)[piece[1]]
                        dst, src = view(slot, 0, 4, D), rows(w, 4)
                    elif kind == "out":
                        a = piece[1] * HALF
                        dst, src = view(slot, 0, KD, HALF), rows(w_out_2, KD)[:, :, a:a + HALF]
                    elif kind == "q_x":
                        dst, src = view(slot, 0, KD, SEQ), rows(w_q_x, KD)
                    elif kind == "kv_x":
                        dst, src = view(slot, 0, KD, HALF), rows(w_kv_x, KD)
                    elif kind == "o_x":
                        dst, src = view(slot, 0, 2, D), rows(w_o_x, 2)
                    elif kind == "gu":
                        a = piece[1] * 2 * P
                        dst = view(slot, 0, KD, 2, 2 * P)
                        src = w_gu[bass.ds(l, 1)].rearrange("a (k p) (g n) -> (a p) k g n", p=P, g=2)[:, :, :, a:a + 2 * P]
                        sp.dma_start(dst[:, :, 0, :], src[:, :, 0, :]).then_inc(raw_full[j % RAW], 16)
                        dst, src = dst[:, :, 1, :], src[:, :, 1, :]
                    else:
                        a, b = DOWN[piece[1]]
                        dst, src = view(slot, 0, b - a, D), rows(w_down, KF)[:, a:b, :]
                    sp.dma_start(dst, src).then_inc(raw_full[j % RAW], 16)

            sp.wait_ge(otok_ready, 2)
            sp.dma_start(out.rearrange("b (t p) d -> p (b t) d", p=P), otok).then_inc(out_done, 16)
            sp.wait_ge(out_done, 16)

        @block.tensor
        def _(pe):
            mm = pe.matmul

            def transpose_tokens(names, src):
                for half, name in enumerate(names):
                    enter(pe, name)
                    to = view(duo(name), 0, 4, SEQ)
                    for k in range(4):
                        for t in range(TT):
                            kk = half * 4 + k
                            last = pe.transpose(to[:, k, t * P:(t + 1) * P], src[:, t, kk * P:(kk + 1) * P], ident)
                    last.then_inc(turned, 1)

            def sums(name, mean, source, chunks, l=0):
                enter(pe, name, l)
                for k in range(chunks):
                    last = mm(duo(name)[:, 0:SEQ], mean, source[:, k, :], start=(k == 0), stop=(k == chunks - 1))
                last.then_inc(sums_done, 1)

            def project(w, name, rhs, done, l=0, chunks=4, k_chunks=KD, width=HALF):
                enter(pe, name, l)
                w = view(w, 0, k_chunks, width)
                to = view(duo(name), 0, 4, SEQ)
                for o in range(chunks):
                    for k in range(k_chunks):
                        last = mm(to[:, o, :], w[:, k, o * P:(o + 1) * P], rhs[:, k, :],
                                  start=(k == 0), stop=(k == k_chunks - 1))
                last.then_inc(done, 1)

            def split_chunk(i, o, to, l, first=None):
                n = SPLIT_THROUGH[i] - 4 + o
                parts_ready(pe, n, l)
                hi, lo = chunk_part(w_hi, n), chunk_part(w_lo, n)
                for k in range(KD):
                    if first is not None and k % 4 == 0:
                        pe.wait_ge(h_hi_ready, first + k // 4 + 1)
                    mm(to, hi[:, k, :], h_hi[:, k, :], start=(k == 0), stop=False)
                    mm(to, lo[:, k, :], h_hi[:, k, :], start=False, stop=False)
                for k in range(KD):
                    if first is not None and k % 4 == 0:
                        pe.wait_ge(h_lo_ready, first + k // 4 + 1)
                    last = mm(to, hi[:, k, :], h_lo[:, k, :], start=False, stop=(k == KD - 1))
                last.then_inc(chunk_used, 1)

            def split_project(i, name, l):
                enter(pe, name, l)
                for o in range(4):
                    halves = {0: l * 4, 24: l * 4 + 2}.get(i) if o == 0 else None
                    split_chunk(i, o, view(duo(name), 0, 4, SEQ)[:, o, :], l, halves)

            pe.wait_ge(consts_in, 32)
            pe.wait_ge(mem_in, 16)
            transpose_tokens(("mem0", "mem1"), mtok)
            pe.wait_ge(x_in, 16)
            transpose_tokens(("x0", "x1"), xtok)
            pe.wait_ge(sq_ready, 1)
            sums("n_mem", c("mean_model"), sq, KD)
            pe.wait_ge(sq_ready, 2)
            sums("n_mix", c("mean_model"), sq, KD)
            pe.wait_ge(h_ready, 2)
            for i in range(5):
                arrived(pe, i)
                project(slot_of(i), f"win{i}", hT, piece_done)
            pe.wait_ge(conv_ready, 1)
            sums("ln_mean", c("mean_mixb"), cb, 4)
            pe.wait_ge(sq_ready, 3)
            sums("ln_var", c("mean_mixb"), sq, 4)
            pe.wait_ge(sq_ready, 4)
            for half in range(2):
                name = f"heads{half}"
                enter(pe, name)
                for k in range(4):
                    last = mm(view(duo(name), 0, 4, SEQ)[:, k, :], c("mean_head"), sq[:, half * 4 + k, :],
                              start=True, stop=True)
                last.then_inc(sums_done, 1)
            pe.wait_ge(y_ready, 1)
            for i in range(2):
                arrived(pe, 5 + i)
                project(slot_of(5 + i), f"wout{i}", yT, piece_done)
            pe.wait_ge(sq_ready, 5)
            sums("n_ffn", c("mean_model"), sq, KD)
            pe.wait_ge(h_ready, 3)
            enter(pe, "tok0")
            enter(pe, "tok1")
            for half in range(2):
                to = duo(f"tok{half}")
                for k in range(KD):
                    last = pe.transpose(to[:, k * P:(k + 1) * P], hT[:, k, half * P:(half + 1) * P], ident)
                last.then_inc(turned, 1)
            enter(pe, "logits")
            wr = view(g1("route_w"), 0, KD, N_GROUPS + N_EXPERTS)
            for t in range(TT):
                for k in range(KD):
                    last = mm(view(duo("logits"), 0, TT, N_GROUPS + N_EXPERTS)[:, t, :], hT[:, k, t * P:(t + 1) * P],
                              wr[:, k, :], start=(k == 0), stop=(k == KD - 1))
            last.then_inc(logits_done, 1)
            pe.wait_ge(member_ready, 1)
            enter(pe, "rank")
            to = view(duo("rank"), 0, 3, N_EXPERTS)
            mem_t = member.rearrange("p (t g) e -> p t (g e)", t=TT)
            mm(to[:, 0, :], c("before"), mem_t[:, 0, :], start=True, stop=True)
            for o, (a, b) in ((1, ("ones", "before")), (2, ("ones", "ones"))):
                mm(to[:, o, :], c(a), mem_t[:, 0, :], start=True, stop=False)
                last = mm(to[:, o, :], c(b), mem_t[:, 1, :], start=False, stop=True)
            last.then_inc(ranks_done, 1)

            pe.wait_ge(passes_ready, 1)
            n_pass = pe.value_load(passes[0:1, 0:1], min_val=1, max_val=MAX_PASSES)
            for credit in (w1_done, w3_done, w2_done):
                pe.sem_inc(credit, 1)
            with pe.Fori(0, n_pass) as p:
                with pe.Fori(0, PAIRS) as q:
                    n = p * PAIRS + q
                    pe.wait_ge(sel_ready, n + 1)
                    pe.wait_ge(scat_added, n * 2 + 2)
                    g = view(psum[:, 0, :], 0, KD, P)
                    for k in range(KD):
                        for t in range(TT):
                            mm(g[:, k, :], htok[:, t, k * P:(k + 1) * P],
                               sel[:, t].rearrange("p e s -> p (e s)"), start=(t == 0), stop=(t == TT - 1))
                    for t in range(TT):
                        last = pe.transpose(psum[:, 3, t * P:(t + 1) * P], selw[:, t].rearrange("p e s -> p (e s)"), ident)
                    last.then_inc(gathered, 1)
                    pe.wait_ge(xs_ready, n * 2 + 2)
                    for at, bank, done in ((0, 0, w1_done), (2, 1, w3_done)):
                        for e in range(2):
                            pe.wait_ge(moe_full[at + e], n * 16 + 16)
                        for k in range(KD):
                            for e in range(2):
                                rows = slice(e * SLOTS, (e + 1) * SLOTS)
                                last = mm(psum[rows, 1, bank * 512:bank * 512 + 512], xs[:, k, rows],
                                          view(ring[:, at + e, :], 0, KD, D_EXPERT)[:, k, :],
                                          start=(k == 0), stop=(k == KD - 1), skip_group_check=True)
                        last.then_inc(done, 1)
                    pe.wait_ge(hid_ready, n + 1)
                    for f in range(4):
                        last = pe.transpose(psum[:, 3, 512 + f * P:512 + (f + 1) * P], hid[:, f * P:(f + 1) * P], ident)
                    last.then_inc(hidT_done, 1)
                    pe.wait_ge(hidT_ready, n + 1)
                    for e in range(2):
                        pe.wait_ge(moe_full[4 + e], n * 16 + 16)
                    for f in range(4):
                        for half in range(2):
                            for e in range(2):
                                rows = slice(e * SLOTS, (e + 1) * SLOTS)
                                last = mm(psum[rows, 2, half * 512:half * 512 + 512], hidT[:, f, rows],
                                          view(ring[:, 4 + e, :], 0, 4, D)[:, f, half * 512:half * 512 + 512],
                                          start=(f == 0), stop=(f == 3), skip_group_check=True)
                    last.then_inc(w2_done, 1)
                    pe.wait_ge(ysb_ready, n + 1)
                    for half, d in enumerate((0, 3)):
                        for k in range(4):
                            kk = half * 4 + k
                            last = mm(view(psum[:, d, :], 0, 4, SEQ)[:, k, :], ysb[:, kk * P:(kk + 1) * P], selwT,
                                      start=True, stop=True)
                        last.then_inc(scat_done, 1)
            pe.wait_ge(scat_added, n_pass * (2 * PAIRS) + 2)
            pe.wait_ge(sq_ready, 6)
            sums("n_final", c("mean_model"), sq, KD)

            pe.sem_inc(chunk_used, PARTS)
            pe.sem_inc(direct_done, RAW)
            with pe.Fori(0, LAYERS) as l:
                norm_no = 0
                for w in WORK:
                    kind = w[0]
                    if kind == "norm":
                        at = {"mix": 0, "cross": 2, "ffn": 3}[w[1]]
                        pe.wait_ge(sq_ready, l * 4 + 6 + at + 1)
                        sums(f"l_{w[1]}", c("mean_model"), sq, KD, l)
                        pe.wait_ge(h_ready, l * 3 + 4 + norm_no + 1)
                        norm_no += 1
                    elif kind == "proj":
                        split_project(w[1], f"p_{w[2]}", l)
                    elif kind == "proj_v":
                        i, name = w[1], f"p_{w[2]}"
                        enter(pe, name, l)
                        for o in range(4):
                            n = SPLIT_THROUGH[i] - 4 + o
                            parts_ready(pe, n, l)
                            hi, lo = chunk_part(w_hi, n), chunk_part(w_lo, n)
                            for t in range(TT):
                                to = duo(name)[:, t * 512:(t + 1) * 512]
                                for j in range(2):
                                    k = 2 * o + j
                                    tok = slice(t * P, (t + 1) * P)
                                    mm(to, h_hi[:, k, tok], hi[:, j, :], start=(k == 0), stop=False, skip_group_check=True)
                                    mm(to, h_hi[:, k, tok], lo[:, j, :], start=False, stop=False, skip_group_check=True)
                                    last = mm(to, h_lo[:, k, tok], hi[:, j, :], start=False, stop=(k == KD - 1),
                                              skip_group_check=True)
                            last.then_inc(chunk_used, 1)
                    elif kind == "index_proj":
                        i = w[1]
                        raw_arrived(pe, i, l)
                        enter(pe, "p_idx", l)
                        wx = view(raw_of(i), 0, KD, 324)
                        to = duo("p_idx")
                        for o in range(2):
                            for k in range(KD):
                                mm(to[:, o * SEQ:(o + 1) * SEQ], wx[:, k, o * P:(o + 1) * P], hT[:, k, :],
                                   start=(k == 0), stop=(k == KD - 1))
                        for half in range(2):
                            for k in range(KD):
                                mm(to[half * 64:half * 64 + 64, 512:512 + SEQ], wx[:, k, 256:320], hT[:, k, :],
                                   start=(k == 0), stop=(k == KD - 1))
                        for t in range(TT):
                            for k in range(KD):
                                last = mm(to[:, 768 + 4 * t:772 + 4 * t], hT[:, k, t * P:(t + 1) * P], wx[:, k, 320:324],
                                          start=(k == 0), stop=(k == KD - 1))
                        last.then_inc(direct_done, 1)
                    elif kind == "rope":
                        r, name = w[1], w[2]
                        freed(pe, f"p_{name}", l)
                        enter(pe, f"r_{name}", l)
                        to = view(duo(f"r_{name}"), 0, 4, SEQ)
                        for k in range(3 if name == "idx" else 4):
                            last = mm(to[:, k, :], c("rotate"), heads[name][:, k, :], start=True, stop=True)
                        last.then_inc(rot_done, 1)
                    elif kind == "index":
                        t = w[1]
                        nk = P * (t + 1)
                        name = f"i_{t}"
                        pe.wait_ge(rope_ready, l * 5 + 3)
                        enter(pe, name, l)
                        for h in range(4):
                            cc, r = h // 2, h % 2
                            rows = slice(64 * r, 64 * r + 64)
                            last = mm(duo(name)[:, r * 512 + cc * SEQ:r * 512 + cc * SEQ + nk],
                                      qiT[rows, cc, t * P:(t + 1) * P], qiT[rows, 2, 0:nk], start=True, stop=True)
                        last.then_inc(idx_done, 1)
                    elif kind == "gates":
                        i, name, o = w[1], f"g_{w[2]}", w[3]
                        if o == 0:
                            enter(pe, name, l)
                        split_chunk(i, o, duo(name)[:, o * SEQ:(o + 1) * SEQ], l)
                    elif kind == "scores":
                        u = w[1]
                        ukind, cc, qt, nk, qb, kb = unit_aps(u)
                        if u == 0:
                            freed(pe, "p_ka", l)
                        elif u == 8:
                            pe.wait_ge(rope_ready, l * 5 + 2)
                        elif u == 16:
                            pe.wait_ge(rope_ready, l * 5 + 5)
                        elif u == 24:
                            freed(pe, "xkv", l)
                        enter(pe, f"u_{u}", l)
                        for r in range(2):
                            rows = slice(64 * r, 64 * r + 64)
                            last = mm(duo(f"u_{u}")[:, r * 512:r * 512 + nk], qb[rows, cc, qt * P:(qt + 1) * P],
                                      kb[rows, cc, 0:nk], start=True, stop=True)
                        last.then_inc(scores_done, 1)
                    elif kind == "turn":
                        u = w[1]
                        ukind, cc, qt, nk, _, _ = unit_aps(u)
                        pe.wait_ge(probs_ready, l * N_UNITS + u + 1)
                        at = 0
                        for r in range(1 if ukind == "B" else 2):
                            for kt in range(nk // P):
                                last = pe.transpose(duo(f"u_{u}")[:, at * P:(at + 1) * P],
                                                    probs[:, u % 3, r, kt * P:(kt + 1) * P], ident)
                                at += 1
                        last.then_inc(probsT_done, 1)
                    elif kind == "apply":
                        u = w[1]
                        ukind, cc, qt, nk, _, _ = unit_aps(u)
                        pe.wait_ge(probsT_ready, l * N_UNITS + u + 1)
                        nt = nk // P
                        to = duo(f"u_{u}")
                        if ukind == "B":
                            for kt in range(nt):
                                last = mm(to[:, 512:512 + P], values["vb"][:, kt, cc * P:(cc + 1) * P],
                                          probsT[:, u % 2, kt * P:(kt + 1) * P], start=(kt == 0), stop=(kt == nt - 1))
                        else:
                            v = vx if ukind == "X" else vals[:, 0]
                            for r in range(2):
                                for kt in range(nt):
                                    at = r * nt + kt
                                    last = mm(to[64 * r:64 * r + 64, 512:512 + P],
                                              v[:, kt, (2 * cc + r) * CH:(2 * cc + r + 1) * CH],
                                              probsT[:, u % 2, at * P:(at + 1) * P],
                                              start=(kt == 0), stop=(kt == nt - 1))
                        last.then_inc(attn_done, 1)
                    elif kind == "subln":
                        pe.wait_ge(sq_ready, l * 4 + 6 + 2)
                        enter(pe, "subln", l)
                        for k in range(4):
                            last = mm(view(duo("subln"), 0, 4, SEQ)[:, k, :], c("mean_sub"), sq[:, k, :],
                                      start=True, stop=True)
                        last.then_inc(sums_done, 1)
                    elif kind == "up":
                        i, b = w[1], w[2]
                        if b == 0:
                            freed(pe, "u_7", l)
                        elif b == 1:
                            pe.wait_ge(subln_ready, l + 1)
                        else:
                            freed(pe, "u_23", l)
                        raw_arrived(pe, i, l)
                        wu = view(raw_of(i), 0, 4, D)
                        for half in range(2):
                            enter(pe, f"up_{b}_{half}", l)
                            to = view(duo(f"up_{b}_{half}"), 0, 4, SEQ)
                            for o in range(4):
                                oo = half * 4 + o
                                for k in range(4):
                                    last = mm(to[:, o, :], wu[:, k, oo * P:(oo + 1) * P], outs[:, b, k, :],
                                              start=(k == 0), stop=(k == 3))
                        last.then_inc(direct_done, 1)
                    elif kind == "out":
                        if w[2] == 0:
                            pe.wait_ge(mixed_ready, l + 1)
                        raw_arrived(pe, w[1], l)
                        project(raw_of(w[1]), f"out_{w[2]}", hT, direct_done, l)
                    elif kind == "cross_q":
                        raw_arrived(pe, w[1], l)
                        project(raw_of(w[1]), "xq", hT, direct_done, l, chunks=2, width=SEQ)
                    elif kind == "cross_kv":
                        i = w[1]
                        raw_arrived(pe, i, l)
                        enter(pe, "xkv", l)
                        wk = view(raw_of(i), 0, KD, HALF)
                        to = view(duo("xkv"), 0, 4, SEQ)
                        for o in range(2):
                            for k in range(KD):
                                mm(to[:, o, :], wk[:, k, o * P:(o + 1) * P], memT[:, k, :],
                                   start=(k == 0), stop=(k == KD - 1))
                        for t in range(TT):
                            for k in range(KD):
                                last = mm(to[:, 2 + t, :], memT[:, k, t * P:(t + 1) * P], wk[:, k, SEQ:2 * SEQ],
                                          start=(k == 0), stop=(k == KD - 1))
                        last.then_inc(direct_done, 1)
                    elif kind == "cross_o":
                        i = w[1]
                        raw_arrived(pe, i, l)
                        freed(pe, "u_27", l)
                        wo = view(raw_of(i), 0, 2, D)
                        for half in range(2):
                            enter(pe, f"xo_{half}", l)
                            to = view(duo(f"xo_{half}"), 0, 4, SEQ)
                            for o in range(4):
                                oo = half * 4 + o
                                for k in range(2):
                                    last = mm(to[:, o, :], wo[:, k, oo * P:(oo + 1) * P], ox[:, k, :],
                                              start=(k == 0), stop=(k == 1))
                        last.then_inc(direct_done, 1)
                    elif kind == "gate_up":
                        split_project(w[1], f"gu_{w[2]}", l)
                    elif kind == "down":
                        for half in range(2):
                            enter(pe, f"dn_{half}", l)
                        for j, (a, b) in enumerate(DOWN):
                            i = 35 + j
                            raw_arrived(pe, i, l)
                            wd = view(raw_of(i), 0, b - a, D)
                            for f in range(a, b):
                                freed(pe, f"gu_{f // 2}", l)
                                for oo in range(8):
                                    last = mm(view(duo(f"dn_{oo // 4}"), 0, 4, SEQ)[:, oo % 4, :],
                                              wd[:, f - a, oo * P:(oo + 1) * P], act[:, f, :],
                                              start=(f == 0 and oo % 2 == 0), stop=(f == KF - 1),
                                              skip_group_check=True)
                            last.then_inc(direct_done, 1)

            pe.wait_ge(sq_ready, 6 + 4 * LAYERS + 1)
            sums("n_last", c("mean_model"), sq, KD)
            pe.wait_ge(h_ready, 4 + 3 * LAYERS + 1)
            for t in range(TT):
                enter(pe, f"out{t}")
                for k in range(KD):
                    last = pe.transpose(duo(f"out{t}")[:, k * P:(k + 1) * P], hT[:, k, t * P:(t + 1) * P], ident)
                last.then_inc(turned, 1)

        @block.scalar
        def _(act_e):
            nca = nc.scalar

            def f(out_ap, in_ap, func, **kw):
                return nca.activation(out_ap, in_ap, func, **kw)

            def copy(out_ap, in_ap):
                return nca.activation(out_ap, in_ap, ACT.Copy)

            def root(name, sums_no, l=0, per=0):
                act_e.wait_ge(sums_done, l * per + sums_no)
                return f(std[:], duo(name)[:, 0:SEQ], ACT.Sqrt, bias=eps[:])

            for d in range(DUOS):
                act_e.sem_inc(duo_free[d], 1)
            for half in range(2):
                act_e.wait_ge(turned, half + 1)
                copy(hT[:, half * 4:half * 4 + 4, :], view(duo(f"mem{half}"), 0, 4, SEQ)).then_inc(free_of(f"mem{half}"), 1)
            freed(act_e, "mem0")
            freed(act_e, "mem1")
            f(sq[:], hT[:], ACT.Square).then_inc(sq_ready, 1)
            for half in range(2):
                act_e.wait_ge(turned, half + 3)
                copy(xT[:, half * 4:half * 4 + 4, :], view(duo(f"x{half}"), 0, 4, SEQ)).then_inc(free_of(f"x{half}"), 1)
            act_e.wait_ge(pad_ready, 3)
            root("n_mem", 1).then_inc(std_ready, 1)
            freed(act_e, "x0")
            freed(act_e, "x1")
            f(sq[:], xT[:], ACT.Square).then_inc(sq_ready, 1)
            act_e.wait_ge(h_ready, 1)
            root("n_mix", 2).then_inc(std_ready, 1)

            done_piece(act_e, 0)
            copy(ub[:, :, PAD_B:PAD_B + SEQ], view(duo("win0"), 0, 4, SEQ)).then_inc(free_of("win0"), 1)
            done_piece(act_e, 1)
            f(sg, view(duo("win1"), 0, 4, SEQ), ACT.Sigmoid).then_inc(free_of("win1"), 1)
            done_piece(act_e, 2)
            copy(ua[:, :, PAD_A:PAD_A + SEQ], view(duo("win2"), 0, 4, SEQ)).then_inc(free_of("win2"), 1)
            done_piece(act_e, 4)
            copy(ab, view(duo("win4"), 0, 4, SEQ)).then_inc(free_of("win4"), 1)
            act_e.wait_ge(centred, 1)
            f(sq[:, 0:4], cb, ACT.Square).then_inc(sq_ready, 1)
            root("ln_var", 4).then_inc(std_ready, 1)
            act_e.wait_ge(yb_raw, 1)
            for k in range(4):
                last = f(yT[:, 4 + k, :], cb[:, k, :], ACT.Silu, bias=g1("ln_b")[:, k:k + 1])
            last.then_inc(silu_b, 1)
            act_e.wait_ge(silu_b, 1)
            act_e.wait_ge(conv_a_ready, 1)
            f(sq[:], yT, ACT.Square).then_inc(sq_ready, 1)
            for half in range(2):
                act_e.wait_ge(sums_done, 5 + half)
                f(root_heads[:, half * 4:half * 4 + 4, :], view(duo(f"heads{half}"), 0, 4, SEQ), ACT.Sqrt,
                  bias=eps[:]).then_inc(std_ready, 1)
            freed(act_e, "wout0")
            freed(act_e, "wout1")
            f(sq[:], xT[:], ACT.Square).then_inc(sq_ready, 1)
            root("n_ffn", 7).then_inc(std_ready, 1)
            for t in range(TT):
                act_e.wait_ge(turned, 5 + t)
                copy(htok[:, t, :], duo(f"tok{t}")).then_inc(free_of(f"tok{t}"), 1)
            act_e.wait_ge(gneg_ready, 1)
            f(gexp, gexp, ACT.Exp).then_inc(gexp_ready, 1)
            act_e.wait_ge(d12_ready, 1)
            f(e12, d12, ACT.Exp).then_inc(e12_ready, 1)

            act_e.wait_ge(passes_ready, 1)
            n_pass = act_e.value_load(passes[0:1, 0:1], min_val=1, max_val=MAX_PASSES)
            with act_e.Fori(0, n_pass) as p:
                with act_e.Fori(0, PAIRS) as q:
                    n = p * PAIRS + q
                    act_e.wait_ge(gathered, n + 1)
                    copy(xs, view(psum[:, 0, :], 0, KD, P)).then_inc(xs_ready, 1)
                    copy(selwT, psum[:, 3, 0:SEQ]).then_inc(xs_ready, 1)
                    act_e.wait_ge(w1_done, n + 2)
                    f(silu1, psum[:, 1, 0:512], ACT.Silu).then_inc(silu1_ready, 1)
                    act_e.wait_ge(hidT_done, n + 1)
                    copy(hidT, view(psum[:, 3, 512:1024], 0, 4, P)).then_inc(hidT_ready, 1)
                    act_e.wait_ge(w2_done, n + 2)
                    copy(ysb, psum[:, 2, :]).then_inc(ysb_ready, 1)
            act_e.wait_ge(scat_added, n_pass * (2 * PAIRS) + 2)
            f(sq[:], xT[:], ACT.Square).then_inc(sq_ready, 1)
            root("n_final", 8).then_inc(std_ready, 1)

            with act_e.Fori(0, LAYERS) as l:
                norm_no = 0
                for w in WORK_SPLIT:
                    kind = w[0]
                    if kind == "split":
                        n = w[1]
                        i, o = chunk_source(n)
                        if o == 0:
                            raw_arrived(act_e, i, l)
                        act_e.wait_ge(chunk_used, l * N_CHUNKS + n + 1)
                        copy(chunk_part(w_hi, n), chunk_raw(n)).then_inc(w_hi_ready, 1)
                    elif kind == "norm":
                        name = f"l_{w[1]}"
                        if w[1] == "mix":
                            act_e.wait_ge(x_ready, l + 1)
                        elif w[1] == "cross":
                            freed(act_e, "out_0", l)
                            freed(act_e, "out_1", l)
                        else:
                            freed(act_e, "xo_0", l)
                            freed(act_e, "xo_1", l)
                        f(sq[:], xT[:], ACT.Square).then_inc(sq_ready, 1)
                        act_e.wait_ge(h_ready, l * 3 + 4 + norm_no)
                        norm_no += 1
                        root(name, 8 + {"mix": 0, "cross": 2, "ffn": 3}[w[1]] + 1, l, 4).then_inc(std_ready, 1)
                        if w[1] != "cross":
                            for half in range(2):
                                if half == 0:
                                    act_e.wait_ge(h_half, l * 2 + (1 if w[1] == "mix" else 2))
                                else:
                                    act_e.wait_ge(h_ready, l * 3 + 4 + norm_no)
                                copy(h_hi[:, half * 4:half * 4 + 4, :], hT[:, half * 4:half * 4 + 4, :]
                                     ).then_inc(h_hi_ready, 1)
                    elif kind == "lam":
                        act_e.wait_ge(lam_dot, l + 1)
                        f(lam[:, 0:2], lam[:, 0:2], ACT.Exp).then_inc(lam_exp, 1)
                    elif kind == "proj":
                        product_done(act_e, w[1], l)
                        name = w[2]
                        copy(heads[name], view(duo(f"p_{name}"), 0, 4, SEQ)).then_inc(free_of(f"p_{name}"), 1)
                    elif kind == "proj_v":
                        product_done(act_e, w[1], l)
                        name = w[2]
                        copy(values[name], view(duo(f"p_{name}"), 0, TT, HALF)).then_inc(free_of(f"p_{name}"), 1)
                    elif kind == "index_proj":
                        product_done(act_e, w[1], l)
                        copy(qiT[:], view(duo("p_idx"), 0, 3, SEQ)).then_inc(idx_raw, 1)
                    elif kind == "gates":
                        if w[3] == 3:
                            product_done(act_e, w[1], l)
                            g = w[2]
                            f(gates[:, 4 * g:4 * g + 4, :], view(duo(f"g_{g}"), 0, 4, SEQ), ACT.Tanh, scale=0.5
                              ).then_inc(free_of(f"g_{g}"), 1)
                    elif kind == "scores":
                        u = w[1]
                        _, _, _, nk, _, _ = unit_aps(u)
                        act_e.wait_ge(rowmax_ready, l * N_UNITS + u + 1)
                        for r in range(2):
                            last = f(probs[:, u % 3, r, 0:nk], probs[:, u % 3, r, 0:nk], ACT.Exp,
                                     bias=stat[:, u % 3, r:r + 1], accum_out=stat[:, u % 3, 2 + r:3 + r])
                        last.then_inc(exp_ready, 1)
                    elif kind == "turn":
                        u = w[1]
                        ukind, _, _, nk, _, _ = unit_aps(u)
                        n = nk * (1 if ukind == "B" else 2)
                        act_e.wait_ge(probsT_done, l * N_UNITS + u + 1)
                        copy(probsT[:, u % 2, 0:n], duo(f"u_{u}")[:, 0:n]).then_inc(probsT_ready, 1)
                    elif kind == "apply":
                        u = w[1]
                        ukind, cc, qt, nk, _, _ = unit_aps(u)
                        act_e.wait_ge(attn_done, l * N_UNITS + u + 1)
                        copy(o_of[ukind][:, cc, qt * P:(qt + 1) * P], duo(f"u_{u}")[:, 512:512 + P]
                             ).then_inc(free_of(f"u_{u}"), 1)
                    elif kind == "index":
                        t = w[1]
                        nk = P * (t + 1)
                        act_e.wait_ge(idx_done, l * 2 + t + 1)
                        f(relu[t][:, :, 0:nk], view(duo(f"i_{t}"), 0, 4, SEQ)[:, :, 0:nk], ACT.Relu, scale=SCALE
                          ).then_inc(relu_ready, 1)
                    elif kind == "subln":
                        freed(act_e, "u_15", l)
                        act_e.wait_ge(rope_ready, l * 5 + 5)
                        f(sq[:, 0:4], outs[:, 1], ACT.Square).then_inc(sq_ready, 1)
                        act_e.wait_ge(sums_done, l * 4 + 8 + 2)
                        f(sq[:, 4:8], view(duo("subln"), 0, 4, SEQ), ACT.Sqrt, bias=eps[:]).then_inc(std_ready, 1)
                    elif kind == "cross_q":
                        product_done(act_e, w[1], l)
                        copy(qx, view(duo("xq"), 0, 2, SEQ)).then_inc(free_of("xq"), 1)
                    elif kind == "cross_kv":
                        product_done(act_e, w[1], l)
                        copy(kx, view(duo("xkv"), 0, 2, SEQ)).then_inc(kx_ready, 1)
                        copy(vx, view(duo("xkv"), 512, TT, SEQ)).then_inc(free_of("xkv"), 1)
                    elif kind == "gate_up":
                        i = w[2]
                        product_done(act_e, w[1], l)
                        if i >= 2:
                            freed(act_e, f"gu_{i - 2}", l)
                        f(probs[:, i % 2], view(duo(f"gu_{i}"), 0, 2, SEQ), ACT.Silu).then_inc(silu_ready, 1)

            act_e.wait_ge(x_ready, LAYERS + 1)
            f(sq[:], xT[:], ACT.Square).then_inc(sq_ready, 1)
            root("n_last", 8 + 4 * LAYERS + 1).then_inc(std_ready, 1)
            for t in range(TT):
                act_e.wait_ge(turned, 7 + t)
                copy(otok[:, t, :], duo(f"out{t}")).then_inc(otok_ready, 1)

        @block.vector
        def _(v):
            link, linked = linker(v, dve_chain)

            def wide(ap, shape):
                return ap.broadcast_to(shape)

            def norm(name, std_no, src, gain, dst, l=0, per=0, halves=False):
                v.wait_ge(std_ready, l * per + std_no)
                link(v.reciprocal(rstd[:], std[:]))
                for k in range(KD):
                    last = v.scalar_tensor_tensor(dst[:, k, :], src[:, k, :], gain[:, k:k + 1], rstd[:], ALU.mult, ALU.mult)
                    if k == 0:
                        last.then_inc(free_of(name), 1)
                    if k == 3 and halves:
                        last.then_inc(h_half, 1)
                last.then_inc(h_ready, 1)

            v.memset(eps[:], EPS).then_inc(pad_ready, 1)
            v.memset(ua, 0.0).then_inc(pad_ready, 1)
            v.memset(ub, 0.0).then_inc(pad_ready, 1)
            v.wait_ge(consts_in, 32)
            norm("n_mem", 1, hT, g1("mem_norm"), memT)
            norm("n_mix", 2, xT, g1("norm_mix"), hT)

            freed(v, "win0")
            freed(v, "win1")
            ub_mid = ub[:, :, PAD_B:PAD_B + SEQ]
            link(v.tensor_tensor(ub_mid, ub_mid, sg, ALU.mult))

            def convolve(dst, src, taps, weight, bias, count):
                for j in range(taps):
                    for k in range(4):
                        if j:
                            v.wait_ge(dve_chain, linked[0] - 3)
                        tap = weight[:, j * 4 + k:j * 4 + k + 1]
                        if j == 0:
                            ins = v.tensor_scalar(dst[:, k, :], src[:, k, 0:SEQ], tap, bias[:, k:k + 1] if bias is not None else 0.0,
                                                  ALU.mult, ALU.add)
                        else:
                            ins = v.scalar_tensor_tensor(dst[:, k, :], src[:, k, j:j + SEQ], tap, dst[:, k, :],
                                                         ALU.mult, ALU.add)
                        linked[0] += 1
                        ins.then_inc(dve_chain, 1)
                v.wait_ge(dve_chain, linked[0])

            convolve(cb, ub, TAPS_B, g1("conv_b"), g1("conv_bias"), 4)
            v.sem_inc(conv_ready, 1)
            done_piece(v, 3)
            freed(v, "win2")
            ua_mid = ua[:, :, PAD_A:PAD_A + SEQ]
            v.tensor_tensor(ua_mid, view(duo("win3"), 0, 4, SEQ), ua_mid, ALU.mult).then_inc(free_of("win3"), 1)
            freed(v, "win3")
            convolve(yT[:, 0:4], ua, TAPS_A, g1("conv_a"), None, 4)
            freed(v, "win4")
            v.tensor_tensor(yT[:, 0:4], yT[:, 0:4], ab, ALU.mult).then_inc(conv_a_ready, 1)
            v.wait_ge(sums_done, 3)
            v.tensor_tensor(cb, cb, duo("ln_mean")[:, 0:SEQ].unsqueeze(1).broadcast_to([P, 4, SEQ]),
                            ALU.subtract).then_inc(centred, 1)
            v.wait_ge(centred, 1)
            v.sem_inc(free_of("ln_mean"), 1)
            v.wait_ge(std_ready, 3)
            link(v.reciprocal(rstd[:], std[:]))
            for k in range(4):
                last = v.scalar_tensor_tensor(cb[:, k, :], cb[:, k, :], g1("ln_g")[:, k:k + 1], rstd[:], ALU.mult, ALU.mult)
                if k == 0:
                    last.then_inc(free_of("ln_var"), 1)
            last.then_inc(yb_raw, 1)
            for half in range(2):
                v.wait_ge(std_ready, 4 + half)
                part = root_heads[:, half * 4:half * 4 + 4, :]
                link(v.reciprocal(part, part))
                for k in range(4):
                    kk = half * 4 + k
                    last = v.scalar_tensor_tensor(yT[:, kk, :], yT[:, kk, :], g1("beta")[:, kk:kk + 1],
                                                  root_heads[:, kk, :], ALU.mult, ALU.mult)
                    if k == 0:
                        last.then_inc(free_of(f"heads{half}"), 1)
            last.then_inc(y_ready, 1)
            for half in range(2):
                done_piece(v, 5 + half)
                part = xT[:, half * 4:half * 4 + 4, :]
                v.tensor_tensor(part, part, view(duo(f"wout{half}"), 0, 4, SEQ), ALU.add).then_inc(free_of(f"wout{half}"), 1)
            norm("n_ffn", 6, xT, g1("norm_ffn"), hT)

            v.wait_ge(logits_done, 1)
            nl = G + N_EXPERTS
            v.tensor_tensor(logit, view(duo("logits"), 0, TT, nl),
                            g1("route_b").unsqueeze(1).broadcast_to([P, TT, nl]), ALU.add).then_inc(free_of("logits"), 1)
            freed(v, "logits")
            lg, lex = logit[:, :, 0:G], logit[:, :, G:nl]

            def bc(ap, n):
                return ap.broadcast_to([P, TT, n])

            def first_of(dst, values_ap, peak, tmp, tmp_max, n):
                order = c("first")[:, 0:n].unsqueeze(1).broadcast_to([P, TT, n])
                link(v.tensor_tensor(tmp, values_ap, bc(peak, n), ALU.is_equal))
                link(v.tensor_tensor(tmp, tmp, order, ALU.mult))
                link(v.tensor_reduce(tmp_max, tmp, AX.X, ALU.max))
                link(v.tensor_tensor(dst, tmp, bc(tmp_max, n), ALU.is_equal))

            link(v.tensor_reduce(gmax, lg, AX.X, ALU.max))
            v.tensor_tensor(gexp, lg, bc(gmax, G), ALU.subtract).then_inc(gneg_ready, 1)
            first_of(gone, lg, gmax, gc, gcm, G)
            gone8 = gone.rearrange("p t g -> p (t g)").unsqueeze(2).broadcast_to([P, TT * G, E])
            for t in range(TT):
                link(v.tensor_tensor(le4[:, t * G:(t + 1) * G, :], lex[:, t, :].rearrange("p (g e) -> p g e", g=G),
                                     gone8[:, t * G:(t + 1) * G, :], ALU.mult))
                link(v.tensor_reduce(le[:, t, :], le4[:, t * G:(t + 1) * G, :].rearrange("p g e -> p e g"), AX.X, ALU.add))
            link(v.tensor_reduce(m1, le, AX.X, ALU.max))
            first_of(f1, le, m1, fc, fm, E)
            link(v.scalar_tensor_tensor(le2, f1, NEG, le, ALU.mult, ALU.add))
            link(v.tensor_reduce(m2, le2, AX.X, ALU.max))
            v.tensor_tensor(d12, m2, m1, ALU.subtract).then_inc(d12_ready, 1)
            first_of(f2, le2, m2, fc, fm, E)
            v.wait_ge(gexp_ready, 1)
            link(v.tensor_reduce(gsum, gexp, AX.X, ALU.add))
            link(v.reciprocal(psel, gsum))
            v.wait_ge(e12_ready, 1)
            link(v.tensor_scalar(wa, e12, 1.0, None, ALU.add))
            link(v.reciprocal(wa, wa))
            link(v.tensor_tensor(wa, wa, psel, ALU.mult))
            link(v.tensor_tensor(wb, e12, wa, ALU.mult))
            link(v.tensor_tensor(wsum, f1, bc(wa, E), ALU.mult))
            link(v.tensor_tensor(fc, f2, bc(wb, E), ALU.mult))
            link(v.tensor_tensor(wsum, wsum, fc, ALU.add))
            link(v.tensor_tensor(fsum, f1, f2, ALU.add))
            for t in range(TT):
                g8 = gone8[:, t * G:(t + 1) * G, :]
                link(v.tensor_tensor(combine[:, t * G:(t + 1) * G, :], g8,
                                     wsum[:, t, :].unsqueeze(1).broadcast_to([P, G, E]), ALU.mult))
                link(v.tensor_tensor(member[:, t * G:(t + 1) * G, :], g8,
                                     fsum[:, t, :].unsqueeze(1).broadcast_to([P, G, E]), ALU.mult))
            v.sem_inc(member_ready, 1)
            member2 = member.rearrange("p (t g) e -> p t (g e)", t=TT)
            combine2 = combine.rearrange("p (t g) e -> p t (g e)", t=TT)
            link(v.tensor_scalar(rank, member2, -4096.0, 4096.0, ALU.mult, ALU.add))
            v.wait_ge(ranks_done, 1)
            placed = view(duo("rank"), 0, 3, N_EXPERTS)
            link(v.tensor_tensor(rank, rank, placed[:, 0:2, :], ALU.add))
            link(v.tensor_reduce(most, placed[:, 2, :], AX.X, ALU.max))
            v.sem_inc(free_of("rank"), 1)
            for i in range(3):
                link(v.tensor_scalar(more[:, i:i + 1], most, float((i + 1) * SLOTS), None, ALU.is_gt))
            link(v.tensor_reduce(count, more, AX.X, ALU.add))
            link(v.tensor_scalar(passes[:, 0:1], count, 1.0, None, ALU.add))
            v.tensor_copy(passes[:, 1:2], count).then_inc(passes_ready, 1)
            v.wait_ge(passes_ready, 1)

            n_pass = v.value_load(passes[0:1, 0:1], min_val=1, max_val=MAX_PASSES)
            v.sem_inc(scat_added, 2)
            slots = c("iota").unsqueeze(1).unsqueeze(1).broadcast_to([P, TT, 2, SLOTS])
            with v.Fori(0, n_pass) as p:
                with v.Fori(0, PAIRS) as q:
                    n = p * PAIRS + q
                    v.tensor_tensor(sel, slots, expert_cols(rank, q), ALU.is_equal).then_inc(moe_chain, 1)
                    v.wait_ge(moe_chain, n + 1)
                    v.tensor_tensor(selw, sel, expert_cols(combine2, q), ALU.mult).then_inc(sel_ready, 1)
                    v.wait_ge(silu1_ready, n + 1)
                    v.wait_ge(w3_done, n + 2)
                    v.tensor_tensor(hid, silu1, psum[:, 1, 512:1024], ALU.mult).then_inc(hid_ready, 1)
                    for half, d in enumerate((0, 3)):
                        v.wait_ge(scat_done, n * 2 + half + 1)
                        part = xT[:, half * 4:half * 4 + 4, :]
                        v.tensor_tensor(part, part, view(psum[:, d, :], 0, 4, SEQ), ALU.add).then_inc(scat_added, 1)
                v.tensor_scalar(rank, rank, -float(SLOTS), None, ALU.add).then_inc(shifted, 1)
                v.wait_ge(shifted, p + 1)
            v.wait_ge(scat_added, n_pass * (2 * PAIRS) + 2)
            norm("n_final", 7, xT, g1("norm_final"), xT)
            v.wait_ge(h_ready, 4)
            v.sem_inc(x_ready, 1)

            with v.Fori(0, LAYERS) as l:
                link, linked = linker(v, layer_chain, LAYER_LINKS, l)
                for w in WORK_SPLIT:
                    kind = w[0]
                    if kind == "split":
                        if w[1] not in POOL_CHUNKS:
                            low_part(v, w[1], l).then_inc(w_lo_ready, 1)
                    elif kind == "norm":
                        if w[1] == "mix":
                            v.wait_ge(vec2_in, l * 32 + 32)
                        norm(f"l_{w[1]}", 7 + {"mix": 0, "cross": 2, "ffn": 3}[w[1]] + 1, xT, g2(f"norm_{w[1]}"), hT, l, 4,
                             halves=w[1] != "cross")
                        if w[1] != "cross":
                            for half in range(2):
                                part = slice(half * 4, half * 4 + 4)
                                v.wait_ge(h_hi_ready, l * 4 + (0 if w[1] == "mix" else 2) + half + 1)
                                v.tensor_tensor(h_lo[:, part, :], hT[:, part, :], h_hi[:, part, :].bitcast(F32),
                                                ALU.subtract).then_inc(h_lo_ready, 1)
                    elif kind == "lam":
                        lv = view(g2("lambda"), 0, 2, 2, CH)
                        dots = view(score, 0, 2, CH)
                        link(v.tensor_tensor(dots, lv[:, :, 0, :], lv[:, :, 1, :], ALU.mult))
                        v.tensor_reduce(lam[:, 0:2], dots, AX.X, ALU.add).then_inc(lam_dot, 1)
                        link(v.memset(win[0:CHUNK, :, 0:CHUNK], NEG))
                        link(v.tensor_tensor(lam[:, 3:4], g2("subln"), g2("one_less"), ALU.mult))
                        v.wait_ge(lam_exp, l + 1)
                        link(v.tensor_tensor(lam[:, 2:3], lam[:, 1:2], lam[:, 0:1], ALU.subtract))
                        link(v.tensor_tensor(lam[:, 2:3], lam[:, 2:3], g2("lam_init"), ALU.subtract))
                    elif kind == "rope":
                        r, name = w[1], w[2]
                        k = 3 if name == "idx" else 4
                        v.wait_ge(rot_done, l * 5 + r + 1)
                        v.tensor_tensor(sq[:, 0:k], view(duo(f"r_{name}"), 0, 4, SEQ)[:, 0:k],
                                        c("sin").unsqueeze(1).broadcast_to([P, k, SEQ]), ALU.mult
                                        ).then_inc(free_of(f"r_{name}"), 1)
                        freed(v, f"r_{name}", l)
                        v.wait_ge(cos_ready, l * 5 + r + 1)
                        v.tensor_tensor(heads[name][:, 0:k], heads[name][:, 0:k], sq[:, 0:k], ALU.add
                                        ).then_inc(rope_ready, 1)
                        v.wait_ge(rope_ready, l * 5 + r + 1)
                    elif kind == "index_proj":
                        product_done(v, w[1], l)
                        v.wait_ge(idx_raw, l + 1)
                        v.tensor_scalar(wi[:].rearrange("p t h -> p (t h)"), duo("p_idx")[:, 768:776], 0.5, None,
                                        ALU.mult).then_inc(free_of("p_idx"), 1)
                    elif kind == "scores":
                        u = w[1]
                        ukind, cc, qt, nk, _, _ = unit_aps(u)
                        v.wait_ge(scores_done, l * N_UNITS + u + 1)
                        if u >= 3:
                            v.wait_ge(probsT_done, l * N_UNITS + u - 2)
                        s, d = probs[:, u % 3, :, 0:nk], view(duo(f"u_{u}"), 0, 2, 512)[:, :, 0:nk]
                        if ukind == "X":
                            link(v.tensor_scalar(s, d, SCALE, None, ALU.mult))
                        else:
                            if ukind == "A":
                                add = win[:, 2 * cc:2 * cc + 2, nk - 1::-1] if nk == SEQ else win[:, 2 * cc:2 * cc + 2, nk - 1::-1]
                            elif ukind == "B":
                                add = c("mask")[:, SEQ - nk:SEQ].unsqueeze(1).broadcast_to([P, 2, nk])
                            else:
                                if u == 16:
                                    v.wait_ge(selneg_ready, l * 2 + 2)
                                add = selneg[:, qt, 0:nk].unsqueeze(1).broadcast_to([P, 2, nk])
                            link(v.scalar_tensor_tensor(s, d, SCALE, add, ALU.mult, ALU.add))
                        v.tensor_reduce(stat[:, u % 3, 0:2], s, AX.X, ALU.max, negate=True).then_inc(rowmax_ready, 1)
                    elif kind == "turn":
                        u = w[1]
                        ukind, cc, qt, nk, _, _ = unit_aps(u)
                        st = stat[:, u % 3]
                        v.wait_ge(exp_ready, l * N_UNITS + u + 1)
                        link(v.reciprocal(st[:, 4:6], st[:, 2:4]))
                        if ukind == "B":
                            link(v.tensor_tensor(st[:, 5:6], st[:, 5:6], lam[:, 2:3], ALU.mult))
                            link(v.tensor_scalar(probs[:, u % 3, 1, 0:nk], probs[:, u % 3, 1, 0:nk], st[:, 5:6], None, ALU.mult))
                            v.scalar_tensor_tensor(probs[:, u % 3, 0, 0:nk], probs[:, u % 3, 0, 0:nk], st[:, 4:5],
                                                   probs[:, u % 3, 1, 0:nk], ALU.mult, ALU.add).then_inc(probs_ready, 1)
                        else:
                            s = probs[:, u % 3, :, 0:nk]
                            v.tensor_tensor(s, s, st[:, 4:6].unsqueeze(2).broadcast_to([P, 2, nk]), ALU.mult
                                            ).then_inc(probs_ready, 1)
                    elif kind == "index":
                        t = w[1]
                        nk = P * (t + 1)
                        v.wait_ge(relu_ready, l * 2 + t + 1)
                        v.sem_inc(free_of(f"i_{t}"), 1)
                        sc = score[:, 0:nk]
                        for h in range(4):
                            add = c("mask")[:, SEQ - nk:SEQ] if h == 0 else sc
                            link(v.scalar_tensor_tensor(sc, relu[t][:, (h % 2) * 2 + h // 2, 0:nk], wi[:, t, h:h + 1], add,
                                                        ALU.mult, ALU.add))
                        for _ in range(TOPK // 8):
                            v.sem_inc(held, 1)
                            link(v.max(top8[:], sc))
                            v.sem_inc(held, 1)
                            link(v.match_replace(sc, top8[:], sc, TAKEN))
                        v.tensor_scalar(selneg[:, t, 0:nk], sc, TAKEN / 3, NEG, ALU.is_gt, ALU.mult).then_inc(selneg_ready, 1)
                        v.wait_ge(selneg_ready, l * 2 + t + 1)
                    elif kind == "subln":
                        v.wait_ge(std_ready, l * 4 + 7 + 2)
                        v.sem_inc(free_of("subln"), 1)
                        link(v.reciprocal(sq[:, 4:8], sq[:, 4:8]))
                        v.scalar_tensor_tensor(outs[:, 1], outs[:, 1], lam[:, 3:4], sq[:, 4:8], ALU.mult, ALU.mult
                                               ).then_inc(subln_ready, 1)
                    elif kind == "up":
                        b = w[2]
                        product_done(v, w[1], l)
                        if b == 0:
                            v.wait_ge(gates_ready, l * 6 + 6)
                        for half in range(2):
                            name = f"up_{b}_{half}"
                            y = hT[:, half * 4:half * 4 + 4, :]
                            term = y if b == 0 else sq[:, half * 4:half * 4 + 4, :]
                            v.tensor_tensor(term, view(duo(name), 0, 4, SEQ),
                                            gates[:, 8 * b + 4 * half:8 * b + 4 * half + 4, :], ALU.mult
                                            ).then_inc(free_of(name), 1)
                            freed(v, name, l)
                            if b:
                                ins = v.tensor_tensor(y, y, term, ALU.add)
                                if b == 2 and half == 1:
                                    ins.then_inc(mixed_ready, 1)
                                else:
                                    link(ins)
                    elif kind in ("out", "cross_o"):
                        product_done(v, w[1], l)
                        for half in ([w[2]] if kind == "out" else range(2)):
                            name = f"out_{half}" if kind == "out" else f"xo_{half}"
                            part = xT[:, half * 4:half * 4 + 4, :]
                            v.tensor_tensor(part, part, view(duo(name), 0, 4, SEQ), ALU.add).then_inc(free_of(name), 1)
                    elif kind == "gate_up":
                        i = w[2]
                        v.wait_ge(silu_ready, l * (KF // 2) + i + 1)
                        v.tensor_tensor(act[:, 2 * i:2 * i + 2, :], probs[:, i % 2], view(duo(f"gu_{i}"), 512, 2, SEQ),
                                        ALU.mult).then_inc(free_of(f"gu_{i}"), 1)
                    elif kind == "down":
                        product_done(v, N_LAYER - 1, l)
                        v.tensor_tensor(xT[:, 0:4], xT[:, 0:4], view(duo("dn_0"), 0, 4, SEQ), ALU.add
                                        ).then_inc(free_of("dn_0"), 1)
                        freed(v, "dn_0", l)
                        v.tensor_tensor(xT[:, 4:8], xT[:, 4:8], view(duo("dn_1"), 0, 4, SEQ), ALU.add).then_inc(x_ready, 1)
                        v.wait_ge(x_ready, l + 2)
                        v.sem_inc(free_of("dn_1"), 1)
                assert linked[0] == LAYER_LINKS, linked

            link, linked = linker(v, last_chain)
            norm("n_last", 7 + 4 * LAYERS + 1, xT, g1("last_norm"), hT)

        @block.gpsimd
        def _(pool):
            pool.wait_ge(consts_in, 32)
            with pool.Fori(0, LAYERS) as l:
                for w in WORK_SPLIT:
                    kind = w[0]
                    if kind == "split":
                        if w[1] in POOL_CHUNKS:
                            low_part(pool, w[1], l).then_inc(w_lo_pool_ready, 1)
                    elif kind == "rope":
                        r, name = w[1], w[2]
                        k = 3 if name == "idx" else 4
                        pool.wait_ge(rot_done, l * 5 + r + 1)
                        pool.tensor_tensor(heads[name][:, 0:k], heads[name][:, 0:k],
                                           c("cos").unsqueeze(1).broadcast_to([P, k, SEQ]), ALU.mult).then_inc(cos_ready, 1)
                    elif kind == "gates" and w[3] == 3:
                        g = w[2]
                        freed(pool, f"g_{g}", l)
                        pool.sem_inc(held, 1)
                        part = gates[:, 4 * g:4 * g + 4, :]
                        pool.tensor_scalar(part, part, 0.5, 0.5, ALU.mult, ALU.add).then_inc(gates_ready, 1)


def constants():
    f = np.float32
    p = np.arange(P)
    out = {}
    out["ident"] = np.eye(P, dtype=f)
    out["mean_model"] = np.full((P, P), 1.0 / D, f)
    out["mean_mixb"] = np.full((P, P), 1.0 / D_A, f)
    out["mean_head"] = (p[:, None] // CH == p[None] // CH).astype(f) / CH
    out["mean_sub"] = np.full((P, P), 1.0 / (2 * CH), f)
    turn = np.zeros((P, P), f)
    for to in range(P):
        turn[to + 32 if to % CH < 32 else to - 32, to] = -1.0 if to % CH < 32 else 1.0
    out["rotate"] = turn
    out["before"] = (p[:, None] < p[None]).astype(f)
    out["ones"] = np.ones((P, P), f)
    inv = f(10000.0) ** (-np.arange(0, CH, 2, dtype=f) / f(CH))
    ang = (np.arange(SEQ, dtype=f)[None, :] * inv[p % 32][:, None]).astype(f)
    out["cos"], out["sin"] = np.cos(ang).astype(f), np.sin(ang).astype(f)
    mask = np.zeros((P, SEQ), f)
    mask[:CHUNK, SEQ - CHUNK:] = NEG
    out["mask"] = mask
    out["iota"] = np.broadcast_to(np.arange(SLOTS, dtype=f), (P, SLOTS))
    out["first"] = np.broadcast_to(np.arange(PER_GROUP, 0, -1).astype(f), (P, PER_GROUP))
    return np.ascontiguousarray(np.concatenate([out[n] for n in CONST], 1))


def kernel(x, norm_mix_g, w_in, conv_a_w, conv_b_w, conv_b_bias, ln_b_g, ln_b_b, beta_a, beta_b, w_out,
           norm_ffn_g, w_route_group, b_route_group, w_route_expert, b_route_expert, w1, w3, w2,
           norm_final_g, mem_2, norm_mix_2, w_in_2, rel_bias_a_2, lambda_vecs_2, subln_b_2, w_up_a_2,
           w_up_b_2, w_up_c_2, w_out_2, norm_cross_2, w_q_x_2, w_kv_x_2, w_o_x_2, norm_ffn_2, w_gu_2,
           w_down_2, mem_norm_2, final_norm_2):
    import concourse.bacc as bacc
    from concourse.bass_utils import run_bass_kernel_spmd as run

    def cols(a):
        a = np.asarray(a)
        a = a.reshape(-1, a.shape[-1] // P, P)
        return np.transpose(a, (2, 0, 1)).reshape(P, -1)

    def rows(a):
        a = np.asarray(a).reshape(1, -1)
        return np.broadcast_to(a, (P, a.shape[1]))

    wr = np.concatenate([np.asarray(w_route_group[0]), np.asarray(w_route_expert[0])], 1)
    wr = np.transpose(wr.reshape(KD, P, -1), (1, 0, 2)).reshape(P, -1)
    parts1 = {"norm_mix": cols(norm_mix_g[0]), "conv_a": cols(conv_a_w[0]), "conv_b": cols(conv_b_w[0]),
              "conv_bias": cols(conv_b_bias[0]), "ln_g": cols(ln_b_g[0]), "ln_b": cols(ln_b_b[0]),
              "beta": np.concatenate([cols(beta_a[0]), cols(beta_b[0])], 1), "norm_ffn": cols(norm_ffn_g[0]),
              "norm_final": cols(norm_final_g), "mem_norm": cols(mem_norm_2), "last_norm": cols(final_norm_2),
              "route_b": np.concatenate([rows(b_route_group[0]), rows(b_route_expert[0])], 1), "route_w": wr}
    vec1 = np.concatenate([parts1[n] for n in VEC1], 1)
    layers = []
    for l in range(LAYERS):
        init = 0.8 - 0.6 * float(np.exp(-0.3 * l))
        parts2 = {"norm_mix": cols(norm_mix_2[l]), "norm_cross": cols(norm_cross_2[l]), "norm_ffn": cols(norm_ffn_2[l]),
                  "subln": cols(subln_b_2[l]), "lam_init": np.full((P, 1), init, np.float32),
                  "one_less": np.full((P, 1), 1.0 - init, np.float32), "lambda": rows(lambda_vecs_2[l])}
        layers.append(np.concatenate([parts2[n] for n in VEC2], 1))
    rel = np.asarray(rel_bias_a_2)
    relpad = np.concatenate([np.zeros(rel.shape[:2] + (CHUNK,), rel.dtype), rel], 2)
    arrays = {"x": x, "mem": mem_2, "cst": constants(), "vec1": vec1, "vec2": np.stack(layers), "relpad": relpad,
              "w_in": w_in, "w_out": w_out, "w1": w1, "w3": w3, "w2": w2, "w_in_2": w_in_2, "w_up_a": w_up_a_2,
              "w_up_b": w_up_b_2, "w_up_c": w_up_c_2, "w_out_2": w_out_2, "w_q_x": w_q_x_2, "w_kv_x": w_kv_x_2,
              "w_o_x": w_o_x_2, "w_gu": w_gu_2, "w_down": w_down_2}
    arrays = {n: np.ascontiguousarray(a) for n, a in arrays.items()}
    nc = bacc.Bacc("TRN2", target_bir_lowering=False, num_devices=1, dynamic_dma_scratch_size=1024)
    args = [nc.dram_tensor(n, a.shape, mybir.dt.from_np(a.dtype), kind="ExternalInput").ap() for n, a in arrays.items()]
    out = nc.dram_tensor("out", (1, SEQ, D), F32, kind="ExternalOutput").ap()
    build(nc, *args, out)
    return run(nc, [arrays], core_ids=[0]).results[0]["out"]
```

```python
from contextlib import ExitStack

import numpy as np

import concourse.bass as bass
from concourse import mybir

F32 = mybir.dt.float32
F32R = mybir.dt.float32r
I32 = mybir.dt.int32
ALU = mybir.AluOpType
ACT = mybir.ActivationFunctionType
AX = mybir.AxisListType

P = 128
SEQ = 256
D = 1024
KD = D // P
TT = SEQ // P
HALF = 512
D_A = 512
CH = 64
TAPS_A, TAPS_B = 3, 31
PAD_A, PAD_B = 1, 15
EPS = 1e-6
N_GROUPS, PER_GROUP = 4, 8
N_EXPERTS = N_GROUPS * PER_GROUP
PAIRS = N_EXPERTS // 2
D_EXPERT = 512
SLOTS = 64
MAX_PASSES = SEQ // SLOTS
LAYERS = 2
CHUNK = 64
REL = 320
REL_ROW = CHUNK + REL
TOPK = min(256, SEQ // 4)
D_FF = 2816
KF = D_FF // P
SCALE = float(CH) ** -0.5
NEG = -1.0e30
LAYER_LINKS = 123
TAKEN = -3.0e38

RING = 6
RAW = 3
PARTS = 4
PIECE = 4096
DUOS = 4
DUO = 1024

CONST = {}
_at = 0
for _name, _width in (("ident", P), ("mean_model", P), ("mean_mixb", P), ("mean_head", P), ("mean_sub", P),
                      ("rotate", P), ("before", P), ("ones", P), ("cos", SEQ), ("sin", SEQ), ("mask", SEQ),
                      ("iota", SLOTS), ("first", PER_GROUP)):
    CONST[_name] = (_at, _at + _width)
    _at += _width
N_CONST = _at

VEC1 = {}
_at = 0
for _name, _width in (("norm_mix", KD), ("conv_a", 4 * TAPS_A), ("conv_b", 4 * TAPS_B), ("conv_bias", 4), ("ln_g", 4),
                      ("ln_b", 4), ("beta", 8), ("norm_ffn", KD), ("norm_final", KD), ("mem_norm", KD),
                      ("last_norm", KD), ("route_b", N_GROUPS + N_EXPERTS),
                      ("route_w", KD * (N_GROUPS + N_EXPERTS))):
    VEC1[_name] = (_at, _at + _width)
    _at += _width
N_VEC1 = _at

VEC2 = {}
_at = 0
for _name, _width in (("norm_mix", KD), ("norm_cross", KD), ("norm_ffn", KD), ("subln", 1), ("lam_init", 1),
                      ("one_less", 1), ("lambda", 4 * CH)):
    VEC2[_name] = (_at, _at + _width)
    _at += _width
N_VEC2 = _at

MIX_PIECES = [("w_in", c) for c in (3, 4, 0, 2, 1)] + [("w_out", 0), ("w_out", 1)]
MIX_SLOTS = [0, 1, 2, 3, 4, 5, 4]
Q_A, K_A, V_A, Q_B, K_B, V_B, Q_C, K_C, V_C = (("in", 512 * i, 512) for i in range(9))
IDX = ("in", 4608, 324)
GATES = [("in", 4932 + 512 * i, 512) for i in range(6)]
DOWN = [(0, 3), (3, 6), (6, 9), (9, 12), (12, 15), (15, 18), (18, 22)]
LAYER_PIECES = ([Q_A, K_A, V_A, Q_B, K_B, V_B, IDX] + GATES[:2] + [Q_C, K_C, V_C] + GATES[2:]
                + [("up", b) for b in range(3)] + [("out", 0), ("out", 1), ("kv_x",), ("q_x",), ("o_x",)]
                + [("gu", i) for i in range(KF // 2)] + [("down", i) for i in range(len(DOWN))])
N_MIX, N_LAYER = len(MIX_PIECES), len(LAYER_PIECES)
assert N_LAYER % RAW == 0


def is_split(piece):
    return piece[0] in ("out", "gu", "down") or (piece[0] == "in" and piece[2] == HALF)


def chunks_of(piece):
    if not is_split(piece):
        return 0
    return DOWN[piece[1]][1] - DOWN[piece[1]][0] if piece[0] == "down" else 4


SPLIT_THROUGH = [sum(chunks_of(p) for p in LAYER_PIECES[:i + 1]) for i in range(N_LAYER)]
DIRECT_THROUGH = [sum(not is_split(p) for p in LAYER_PIECES[:i + 1]) for i in range(N_LAYER)]
N_CHUNKS, N_DIRECT = SPLIT_THROUGH[-1], DIRECT_THROUGH[-1]
LAST_CHUNKS = N_CHUNKS - SPLIT_THROUGH[N_LAYER - RAW - 1]
LOADS = [2 if p[0] == "gu" else 1 for p in LAYER_PIECES]

EARLY = (["x0", "x1", "n_mix"] + [f"win{i}" for i in range(5)] + ["mem0", "mem1", "n_mem"]
         + ["ln_mean", "ln_var", "heads0", "heads1", "wout0", "wout1", "n_ffn", "tok0", "tok1", "logits", "rank"])
LATE = ["n_final"]
LAST = ["n_last", "out0", "out1"]

UNITS = ([("A", c, t) for c in range(4) for t in range(TT)] + [("B", c, t) for c in range(4) for t in range(TT)]
         + [("C", c, t) for c in range(4) for t in range(TT)] + [("X", c, t) for c in range(2) for t in range(TT)])
N_UNITS = len(UNITS)
ROPES = ["qb", "kb", "idx", "qc", "kc"]


def attention(first, last, extra):
    steps = []
    for s in range(first, last + 2):
        if first <= s - 1 < last:
            steps.append(("probs", s - 1))
        steps += extra.get(s, [])
        if s < last:
            steps.append(("scores", s))
        if first <= s - 1 < last:
            steps.append(("turn", s - 1))
        if first <= s - 2 < last:
            steps.append(("apply", s - 2))
    return steps


def gate_parts(starts, piece, gate):
    return {s + o: [("gates", piece + i, gate + i, o)] for i, s in enumerate(starts) for o in range(4)}


WORK = ([("norm", "mix"), ("lam",), ("proj", 0, "qa"), ("proj", 1, "ka"), ("proj_v", 2, "va"),
         ("proj", 3, "qb"), ("proj", 4, "kb"), ("rope", 0, "qb"), ("proj_v", 5, "vb"), ("rope", 1, "kb"),
         ("index_proj", 6)]
        + [("rope", 2, "idx")]
        + attention(0, 8, gate_parts((1, 5), 7, 0))
        + [("index", 0), ("index", 1), ("proj", 9, "qc"), ("proj", 10, "kc"), ("rope", 3, "qc"),
           ("proj_v", 11, "vc"), ("rope", 4, "kc")]
        + attention(8, 24, {**gate_parts((9, 13, 17, 21), 12, 2), 25: [("square_b",)]})
        + [("subln",)] + [("up", 16 + b, b) for b in range(3)]
        + [("out", 19, 0), ("out", 20, 1), ("cross_k", 21), ("norm", "cross"), ("cross_v", 21), ("cross_q", 22)]
        + attention(24, 28, {}) + [("cross_o", 23), ("norm", "ffn")]
        + [("gate_up", 24 + i, i) for i in range(KF // 2)] + [("down", k) for k in range(KF)] + [("down_add",)])


def with_splits(work):
    out, split, used = [], 0, 0
    piece_of = [i for i, p in enumerate(LAYER_PIECES) for _ in range(chunks_of(p))]
    direct_left = [i for i, p in enumerate(LAYER_PIECES) if not is_split(p)]
    low = []
    for w in work:
        used += {"proj": 4, "proj_v": 4, "out": 4, "gate_up": 4, "gates": 1, "down": 1}.get(w[0], 0)
        unit = w[0] in ("scores", "probs", "turn", "apply", "gates")
        if unit:
            out.append(w)
        if w[0] == "probs" or not unit:
            out += low
            low = []
        held = w[0] in ("gates", "probs", "turn", "apply", "cross_q") or (w[0] == "scores" and w[1] >= 24)
        while (not held and split < N_CHUNKS and split < used + PARTS - 1
               and not (direct_left and direct_left[0] <= piece_of[split] - RAW)):
            out.append(("split", split))
            if unit:
                low.append(("low", split))
            else:
                out.append(("low", split))
            split += 1
        assert split >= used
        if not unit:
            out.append(w)
        if direct_left and w[0] in ("index_proj", "up", "cross_v", "cross_q", "cross_o"):
            assert direct_left.pop(0) == w[1]
    assert split == used == N_CHUNKS
    return out


WORK_SPLIT = with_splits(WORK)
POOL_CHUNKS = range(SPLIT_THROUGH[8], SPLIT_THROUGH[11])


def low_parts(n, on_pool):
    return sum((j in POOL_CHUNKS) == on_pool for j in range(n + 1))


def tenants(work):
    names = []
    for w in work:
        kind = w[0]
        if kind == "norm":
            names.append(f"l_{w[1]}")
        elif kind in ("proj", "proj_v"):
            names.append(f"p_{w[2]}")
        elif kind == "rope":
            names.append(f"r_{w[2]}")
        elif kind == "index_proj":
            names.append("p_idx")
        elif kind == "index":
            names.append(f"i_{w[1]}")
        elif kind == "gates":
            names += [f"g_{w[2]}"] if w[3] == 0 else []
        elif kind == "scores":
            names.append(f"u_{w[1]}")
        elif kind == "subln":
            names.append("subln")
        elif kind == "up":
            names += [f"up_{w[2]}_0", f"up_{w[2]}_1"]
        elif kind == "out":
            names.append(f"out_{w[2]}")
        elif kind == "cross_q":
            names.append("xq")
        elif kind == "cross_k":
            names.append("xkv")
        elif kind == "cross_o":
            names += ["xo_0", "xo_1"]
        elif kind == "gate_up":
            names.append(f"gu_{w[2]}")
        elif kind == "down":
            names += ["dn_0", "dn_1"] if w[1] == 0 else []
    return names


def seat(names, before, at):
    units = others = 0
    for name in names:
        assert name not in at, name
        if name.startswith("u_"):
            d, units = units % 3, units + 1
        elif name.startswith("g_"):
            d = 3
        else:
            d, others = others % DUOS, others + 1
        at[name] = (d, before[d])
        before[d] += 1


def build(nc, x, mem, cst, vec1, vec2, relpad, w_in, w_out, w1, w3, w2, w_in_2, w_up_a, w_up_b, w_up_c,
          w_out_2, w_q_x, w_kv_x, w_o_x, w_gu, w_down, out):
    seats, tenancies = {}, [0] * DUOS
    seat(EARLY + LATE, tenancies, seats)
    start = list(tenancies)
    seat(tenants(WORK), tenancies, seats)
    layer_tenancies = [b - a for a, b in zip(start, tenancies)]
    for i, name in enumerate(LAST):
        d = i % DUOS
        seats[name] = (d, tenancies[d] + (LAYERS - 1) * layer_tenancies[d])

    with ExitStack() as ctx:
        def sb(name, shape, dt=F32):
            return ctx.enter_context(nc.sbuf_tensor(name, shape, dt))

        def sem(name):
            return ctx.enter_context(nc.semaphore(name))

        psum = ctx.enter_context(nc.psum_tensor("psum", [P, DUOS, DUO], F32))

        with ExitStack() as first_block:
            ring = first_block.enter_context(nc.sbuf_tensor("ring", [P, RING, PIECE], F32))
        raw = sb("raw", [P, RAW, PIECE])
        w_hi = sb("w_hi", [P, PARTS, KD * P], F32R)
        w_lo = sb("w_lo", [P, PARTS, KD * P], F32R)
        h_hi = sb("h_hi", [P, KD, SEQ], F32R)
        h_lo = sb("h_lo", [P, KD, SEQ], F32R)
        xT = sb("xT", [P, KD, SEQ])
        hT = sb("hT", [P, KD, SEQ])
        sq = sb("sq", [P, KD, SEQ])
        consts = sb("consts", [P, N_CONST])
        memT = sb("memT", [P, KD, SEQ])
        std = sb("std", [P, SEQ])
        rstd = sb("rstd", [P, SEQ])
        eps = sb("eps", [P, 1])
        v1 = sb("v1", [P, N_VEC1])
        v2 = sb("v2", [P, N_VEC2])
        with ExitStack() as feed_forward:
            act_parts = feed_forward.enter_context(nc.sbuf_tensor("act_parts", [P, 2, 24, SEQ], F32R))
        act_hi, act_lo = act_parts[:, 0], act_parts[:, 1]
        big = sb("big", [P, 24 * SEQ])
        qk = sb("qk", [P, 16 * SEQ])
        vals = sb("vals", [P, 2, TT, HALF])
        outs = sb("outs", [P, 3, 4, SEQ])
        win = sb("win", [P, 8, SEQ])
        probs = sb("probs", [P, 3, 2, SEQ])
        probsT = sb("probsT", [P, 2, 2 * TT * P])
        stat = sb("stat", [P, 3, 6])
        qiT = sb("qiT", [P, 3, SEQ])
        wi = sb("wi", [P, TT, 4])
        score = sb("score", [P, SEQ])
        top8 = sb("top8", [P, 8])
        lam = sb("lam", [P, 8])
        route = vals[:, 0].rearrange("p t n -> p (t n)")
        passes = sb("passes", [P, 2], I32)

        def c(name):
            a, b = CONST[name]
            return consts[:, a:b]

        def g1(name):
            a, b = VEC1[name]
            return v1[:, a:b]

        def g2(name):
            a, b = VEC2[name]
            return v2[:, a:b]

        ident = c("ident")

        def view(t, at, *dims):
            n = int(np.prod(dims))
            ap = t[:, at:at + n]
            if len(dims) == 2:
                return ap.rearrange("p (a b) -> p a b", a=dims[0])
            if len(dims) == 3:
                return ap.rearrange("p (a b c) -> p a b c", a=dims[0], b=dims[1])
            return ap

        xtok = view(big, 0, TT, D)
        mtok = view(big, TT * D, TT, D)
        ua = view(qk, 0, 4, SEQ + 2 * PAD_A)
        ub = view(qk, 4 * (SEQ + 2 * PAD_A), 4, SEQ + 2 * PAD_B)
        ab = view(big, 4096, 4, SEQ)
        sg = view(big, 5120, 4, SEQ)
        cb = outs[:, 0]
        yT = view(big, 0, KD, SEQ)
        mem_std = score[:]
        root_heads = view(big, 4096, KD, SEQ)
        htok = view(big, 0, TT, D)
        sel = view(big, 2048, TT, 2, SLOTS)
        selw = view(big, 2048 + 256, TT, 2, SLOTS)
        xs = view(big, 2048 + 512, KD, P)
        selwT = view(big, 2048 + 512 + 1024, SEQ)
        silu1 = view(big, 3840 + 256, D_EXPERT)
        hid = view(big, 3840 + 768, D_EXPERT)
        hidT = view(big, 3840 + 1280, 4, P)
        ysb = view(qk, 0, D)
        gates = view(big, 0, 24, SEQ)
        heads = {n: view(qk, 4 * SEQ * i, 4, SEQ) for i, n in enumerate(("qa", "ka", "qb", "kb"))}
        heads["qc"], heads["kc"] = heads["qa"], heads["ka"]
        heads["idx"] = qiT
        values = {"va": vals[:, 0], "vb": vals[:, 1], "vc": vals[:, 0]}
        relu = [probs[:, 1].rearrange("p r (b n) -> p (r b) n", b=2), win[:, 0:4]]
        selneg = win[:, 4:6]
        qx, kx = heads["qb"][:, 0:2], heads["qb"][:, 2:4]
        vx = view(qk, 12 * SEQ, TT, SEQ)
        ox = outs[:, 0, 0:2]
        o_of = {"A": outs[:, 0], "B": outs[:, 1], "C": outs[:, 2], "X": ox}
        otok = view(big, 0, TT, D)

        used = [0]

        def small(*dims):
            n = int(np.prod(dims))
            at = used[0]
            used[0] += n
            assert used[0] <= 1024
            return view(route, at, *dims) if len(dims) > 1 else route[:, at:at + n]

        G, E = N_GROUPS, PER_GROUP
        logit = small(TT, G + N_EXPERTS)
        gmax, gsum, psel = small(TT, 1), small(TT, 1), small(TT, 1)
        gexp = small(TT, G)
        gc, gone = small(TT, G), small(TT, G)
        gcm = small(TT, 1)
        le4 = small(TT * G, E)
        le = small(TT, E)
        m1, m2, d12, e12, wa, wb = (small(TT, 1) for _ in range(6))
        f1, f2, fc, le2 = (small(TT, E) for _ in range(4))
        fm = small(TT, 1)
        wsum, fsum = small(TT, E), small(TT, E)
        member = small(TT * G, E)
        combine = small(TT * G, E)
        rank = small(TT, N_EXPERTS)
        count, most, more = small(1), small(1), small(3)

        ring_full = [sem(f"ring_full{i}") for i in range(RING)]
        moe_full = [sem(f"moe_full{i}") for i in range(RING)]
        duo_free = [sem(f"duo_free{i}") for i in range(DUOS)]
        piece_done = sem("piece_done")
        raw_full = [sem(f"raw_full{i}") for i in range(RAW)]
        (ident_in, up_half, consts_in, mem_in, squares_a, x_in, vec2_in, turned, sq_ready, sums_done, std_ready, h_ready, x_ready,
         dve_chain, pad_ready, conv_a_ready, yb_raw, centred, silu_b, y_ready,
         logits_done, gexp_ready, gneg_ready, d12_ready, e12_ready, member_ready, ranks_done, passes_ready,
         sel_ready, gathered, xs_ready, selwT_ready, w1_done, w3_done, silu1_ready, hid_ready, hidT_done, hidT_ready,
         w2_done, ysb_ready, scat_done, scat_added, moe_chain,
         lam_dot, lam_exp, rot_done, cos_ready, rope_ready, idx_raw, idx_done, relu_ready, selneg_ready,
         scores_done, rowmax_ready, exp_ready, probs_ready, probsT_done, probsT_ready, attn_done, subln_ready,
         direct_done, chunk_used, w_hi_ready, w_lo_ready, w_lo_pool_ready, act_hi_ready, act_lo_ready, h_half,
         h_hi_ready, h_lo_ready, gates_ready, held, conv_ready, shifted, kx_ready, mixed_ready, silu_ready,
         layer_chain, last_chain, otok_ready, out_done) = (sem(n) for n in (
            "ident_in up_half consts_in mem_in squares_a x_in vec2_in turned sq_ready sums_done std_ready h_ready x_ready "
            "dve_chain pad_ready conv_a_ready yb_raw centred silu_b y_ready "
            "logits_done gexp_ready gneg_ready d12_ready e12_ready member_ready ranks_done passes_ready "
            "sel_ready gathered xs_ready selwT_ready w1_done w3_done silu1_ready hid_ready hidT_done hidT_ready "
            "w2_done ysb_ready scat_done scat_added moe_chain "
            "lam_dot lam_exp rot_done cos_ready rope_ready idx_raw idx_done relu_ready selneg_ready "
            "scores_done rowmax_ready exp_ready probs_ready probsT_done probsT_ready attn_done subln_ready "
            "direct_done chunk_used w_hi_ready w_lo_ready w_lo_pool_ready act_hi_ready act_lo_ready h_half "
            "h_hi_ready h_lo_ready gates_ready held conv_ready shifted kx_ready mixed_ready silu_ready "
            "layer_chain last_chain otok_ready out_done").split())

        def duo(name):
            return psum[:, seats[name][0], :]

        def enter(eng, name, l=0):
            d, n = seats[name]
            eng.wait_ge(duo_free[d], l * layer_tenancies[d] + n + 1)

        def freed(eng, name, l=0):
            d, n = seats[name]
            eng.wait_ge(duo_free[d], l * layer_tenancies[d] + n + 2)

        def free_of(name):
            return duo_free[seats[name][0]]

        def slot_of(i):
            return ring[:, MIX_SLOTS[i], :]

        def done_piece(eng, i):
            eng.wait_ge(piece_done, i + 1)

        def arrived(eng, i):
            eng.wait_ge(ring_full[MIX_SLOTS[i]], MIX_SLOTS[:i + 1].count(MIX_SLOTS[i]) * 16)

        def raw_of(i):
            return raw[:, i % RAW, :]

        def raw_arrived(eng, i, l):
            so_far = sum(LOADS[j] for j in range(i % RAW, i + 1, RAW))
            a_layer = sum(LOADS[j] for j in range(i % RAW, N_LAYER, RAW))
            eng.wait_ge(raw_full[i % RAW], (l * a_layer + so_far) * 16)

        def product_done(eng, i, l):
            if is_split(LAYER_PIECES[i]):
                eng.wait_ge(chunk_used, l * N_CHUNKS + SPLIT_THROUGH[i] + PARTS)
            else:
                eng.wait_ge(direct_done, l * N_DIRECT + DIRECT_THROUGH[i])

        def parts_ready(eng, n, l, before=0):
            if n in POOL_CHUNKS:
                eng.wait_ge(w_lo_pool_ready, l * len(POOL_CHUNKS) + low_parts(n, True))
            else:
                eng.wait_ge(w_lo_ready, (l - before) * (N_CHUNKS - len(POOL_CHUNKS)) + low_parts(n, False) + LAST_CHUNKS)

        def low_part(eng, n, l):
            eng.wait_ge(w_hi_ready, l * N_CHUNKS + n + 1)
            if eng is nc.gpsimd:
                eng.sem_inc(held, 1)
            return eng.tensor_tensor(chunk_part(w_lo, n), chunk_raw(n), chunk_part(w_hi, n).bitcast(F32), ALU.subtract)

        def raw_free(eng, i, l):
            before = (i - RAW) % N_LAYER
            if is_split(LAYER_PIECES[before]):
                parts_ready(eng, SPLIT_THROUGH[before] - 1, l, int(i < RAW))
            else:
                assert i >= RAW
                eng.wait_ge(direct_done, l * N_DIRECT + DIRECT_THROUGH[before])

        def chunk_source(n):
            i = next(j for j in range(N_LAYER) if SPLIT_THROUGH[j] > n)
            return i, n - (SPLIT_THROUGH[i] - chunks_of(LAYER_PIECES[i]))

        def chunk_raw(n):
            i, o = chunk_source(n)
            if LAYER_PIECES[i][0] == "down":
                return view(raw_of(i), o * D, KD, P)
            whole = view(raw_of(i), 0, KD, HALF)
            return whole[:, 2 * o:2 * o + 2, :] if is_values(i) else whole[:, :, o * P:(o + 1) * P]

        def is_values(i):
            return LAYER_PIECES[i] in (V_A, V_B, V_C)

        def buffer_user(n):
            if n >= PARTS:
                return n - PARTS
            return next(j for j in range(N_CHUNKS - PARTS, N_CHUNKS) if j % PARTS == n) - N_CHUNKS

        def chunk_part(parts, n):
            i, _ = chunk_source(n)
            dims = (2, HALF) if is_values(i) else (KD, P)
            return view(parts[:, n % PARTS, :], 0, *dims)

        def linker(eng, chain, per=0, index=0):
            linked = [0]

            def link(ins):
                linked[0] += 1
                ins.then_inc(chain, 1)
                eng.wait_ge(chain, index * per + linked[0])

            return link, linked

        def moe_ap(w):
            return w.rearrange("l e (k p) n -> (l e) p k n", p=P)

        w1_v, w3_v, w2_v = moe_ap(w1), moe_ap(w3), moe_ap(w2)

        def expert_cols(ap, q):
            return ap[:, :, bass.ds(q * 2, 2)].unsqueeze(3).broadcast_to([P, TT, 2, SLOTS])

        def unit_aps(u):
            kind, cc, qt = UNITS[u]
            nk = SEQ if kind == "X" else P * (qt + 1)
            if kind == "X":
                q, k = qx, kx
            else:
                q, k = {"A": (heads["qa"], heads["ka"]), "B": (heads["qb"], heads["kb"]),
                        "C": (heads["qc"], heads["kc"])}[kind]
            return kind, cc, qt, nk, q, k

        block = ctx.enter_context(nc.Block())

        @block.sync
        def _(sp):
            sp.dma_start(ident, cst[:, 0:P]).then_inc(ident_in, 16)
            sp.dma_start(xtok, x.rearrange("b (t p) d -> p (b t) d", p=P)).then_inc(x_in, 16)
            sp.dma_start(consts[:, P:N_CONST], cst[:, P:N_CONST]).then_inc(consts_in, 16)
            sp.dma_start(v1[:], vec1).then_inc(consts_in, 16)
            w_in_v = w_in.rearrange("l (k p) n -> p (l k) n", p=P)
            w_out_v = w_out.rearrange("l (k p) n -> p (l k) n", p=P)
            for i, (name, col) in enumerate(MIX_PIECES):
                slot = MIX_SLOTS[i]
                if slot in MIX_SLOTS[:i]:
                    done_piece(sp, MIX_SLOTS.index(slot))
                src = w_in_v if name == "w_in" else w_out_v
                sp.dma_start(view(ring[:, slot, :], 0, KD, HALF),
                             src[:, :, col * HALF:(col + 1) * HALF]).then_inc(ring_full[slot], 16)
                if i == 2:
                    sp.dma_start(mtok, mem.rearrange("b (t p) d -> p (b t) d", p=P)).then_inc(mem_in, 16)

            def load_pair(q, n):
                for at, done, src, k, last in ((0, w1_done, w1_v, KD, 1), (2, w3_done, w3_v, KD, 3),
                                               (4, w2_done, w2_v, 4, N_MIX - 1)):
                    if n is None:
                        done_piece(sp, last)
                    else:
                        sp.wait_ge(done, n + 1)
                    for e in range(2):
                        sp.dma_start(view(ring[:, at + e, :], 0, k, PIECE // k),
                                     src[bass.ds(q * 2 + e, 1)].rearrange("a p k n -> (a p) k n")
                                     ).then_inc(moe_full[at + e], 16)

            load_pair(0, None)
            with sp.Fori(1, PAIRS) as q:
                load_pair(q, q)
            sp.wait_ge(passes_ready, 1)
            n_pass = sp.value_load(passes[0:1, 0:1], min_val=1, max_val=MAX_PASSES)
            n_more = sp.value_load(passes[0:1, 1:2], min_val=0, max_val=MAX_PASSES - 1)
            with sp.If(n_more):
                with sp.Fori(1, n_pass) as p:
                    with sp.Fori(0, PAIRS) as q:
                        load_pair(q, p * PAIRS + q)
            sp.wait_ge(w1_done, n_pass * PAIRS + 1)
            sp.sem_inc(held, 1)
            sp.wait_ge(w3_done, n_pass * PAIRS + 1)
            sp.sem_inc(held, 1)

            with sp.Fori(0, LAYERS) as l:
                for j, piece in enumerate(LAYER_PIECES):
                    if j == RAW:
                        sp.wait_ge(h_ready, l * 3 + 4)
                        sp.dma_start(v2[:], vec2[bass.ds(l, 1)].rearrange("a p n -> (a p) n")).then_inc(vec2_in, 16)
                        window = bass.AP(relpad.tensor, l * (8 * REL_ROW), [[1, P], [REL_ROW, 8], [1, SEQ]])
                        sp.dma_start(win[:], window).then_inc(vec2_in, 16)
                    raw_free(sp, j, l)
                    slot = raw_of(j)
                    kind = piece[0]

                    def rows(w, k):
                        return w[bass.ds(l, 1)].rearrange("a (k p) n -> (a p) k n", p=P)

                    if kind == "in":
                        _, at, n = piece
                        dst, src = view(slot, 0, KD, n), rows(w_in_2, KD)[:, :, at:at + n]
                    elif kind == "up":
                        w = (w_up_a, w_up_b, w_up_c)[piece[1]]
                        dst, src = view(slot, 0, 4, D), rows(w, 4)
                    elif kind == "out":
                        a = piece[1] * HALF
                        dst, src = view(slot, 0, KD, HALF), rows(w_out_2, KD)[:, :, a:a + HALF]
                    elif kind == "q_x":
                        dst, src = view(slot, 0, KD, SEQ), rows(w_q_x, KD)
                    elif kind == "kv_x":
                        dst, src = view(slot, 0, KD, HALF), rows(w_kv_x, KD)
                    elif kind == "o_x":
                        dst, src = view(slot, 0, 2, D), rows(w_o_x, 2)
                    elif kind == "gu":
                        a = piece[1] * 2 * P
                        dst = view(slot, 0, KD, 2, 2 * P)
                        src = w_gu[bass.ds(l, 1)].rearrange("a (k p) (g n) -> (a p) k g n", p=P, g=2)[:, :, :, a:a + 2 * P]
                        sp.dma_start(dst[:, :, 0, :], src[:, :, 0, :]).then_inc(raw_full[j % RAW], 16)
                        dst, src = dst[:, :, 1, :], src[:, :, 1, :]
                    else:
                        a, b = DOWN[piece[1]]
                        dst, src = view(slot, 0, b - a, D), rows(w_down, KF)[:, a:b, :]
                    sp.dma_start(dst, src).then_inc(raw_full[j % RAW], 16)

            sp.wait_ge(otok_ready, 2)
            sp.dma_start(out.rearrange("b (t p) d -> p (b t) d", p=P), otok).then_inc(out_done, 16)
            sp.wait_ge(out_done, 16)

        @block.tensor
        def _(pe):
            mm = pe.matmul

            def transpose_tokens(names, src):
                for half, name in enumerate(names):
                    enter(pe, name)
                    to = view(duo(name), 0, 4, SEQ)
                    for k in range(4):
                        for t in range(TT):
                            kk = half * 4 + k
                            last = pe.transpose(to[:, k, t * P:(t + 1) * P], src[:, t, kk * P:(kk + 1) * P], ident)
                    last.then_inc(turned, 1)

            def sums(name, mean, source, chunks, l=0):
                enter(pe, name, l)
                for k in range(chunks):
                    last = mm(duo(name)[:, 0:SEQ], mean, source[:, k, :], start=(k == 0), stop=(k == chunks - 1))
                last.then_inc(sums_done, 1)

            def project(w, name, rhs, done, l=0, chunks=4, k_chunks=KD, width=HALF):
                enter(pe, name, l)
                w = view(w, 0, k_chunks, width)
                to = view(duo(name), 0, 4, SEQ)
                for o in range(chunks):
                    for k in range(k_chunks):
                        last = mm(to[:, o, :], w[:, k, o * P:(o + 1) * P], rhs[:, k, :],
                                  start=(k == 0), stop=(k == k_chunks - 1))
                last.then_inc(done, 1)

            def split_chunk(i, o, to, l, first=None):
                n = SPLIT_THROUGH[i] - 4 + o
                parts_ready(pe, n, l)
                hi, lo = chunk_part(w_hi, n), chunk_part(w_lo, n)
                for k in range(KD):
                    if first is not None and k % 4 == 0:
                        pe.wait_ge(h_hi_ready, first + k // 4 + 1)
                    mm(to, hi[:, k, :], h_hi[:, k, :], start=(k == 0), stop=False)
                    mm(to, lo[:, k, :], h_hi[:, k, :], start=False, stop=False)
                for k in range(KD):
                    if first is not None and k % 4 == 0:
                        pe.wait_ge(h_lo_ready, first + k // 4 + 1)
                    last = mm(to, hi[:, k, :], h_lo[:, k, :], start=False, stop=(k == KD - 1))
                last.then_inc(chunk_used, 1)

            def split_project(i, name, l):
                enter(pe, name, l)
                for o in range(4):
                    halves = {0: l * 6, 19: l * 6 + 2, 24: l * 6 + 4}.get(i) if o == 0 else None
                    split_chunk(i, o, view(duo(name), 0, 4, SEQ)[:, o, :], l, halves)

            pe.wait_ge(ident_in, 16)
            pe.wait_ge(x_in, 16)
            transpose_tokens(("x0", "x1"), xtok)
            pe.wait_ge(consts_in, 32)
            pe.wait_ge(sq_ready, 1)
            sums("n_mix", c("mean_model"), sq, KD)
            pe.wait_ge(h_ready, 1)
            for i in range(5):
                arrived(pe, i)
                project(slot_of(i), f"win{i}", hT, piece_done)
            pe.wait_ge(mem_in, 16)
            transpose_tokens(("mem0", "mem1"), mtok)
            pe.wait_ge(sq_ready, 2)
            sums("n_mem", c("mean_model"), sq, KD)
            pe.wait_ge(conv_ready, 1)
            sums("ln_mean", c("mean_mixb"), cb, 4)
            pe.wait_ge(sq_ready, 3)
            sums("ln_var", c("mean_mixb"), sq, 4)
            for half, (squares, count) in enumerate(((squares_a, 1), (sq_ready, 4))):
                name = f"heads{half}"
                pe.wait_ge(squares, count)
                enter(pe, name)
                for k in range(4):
                    last = mm(view(duo(name), 0, 4, SEQ)[:, k, :], c("mean_head"), sq[:, (1 - half) * 4 + k, :],
                              start=True, stop=True)
                last.then_inc(sums_done, 1)
            pe.wait_ge(y_ready, 1)
            for i in range(2):
                arrived(pe, 5 + i)
                project(slot_of(5 + i), f"wout{i}", yT, piece_done)
            pe.wait_ge(sq_ready, 5)
            sums("n_ffn", c("mean_model"), sq, KD)
            pe.wait_ge(h_ready, 3)
            enter(pe, "tok0")
            enter(pe, "tok1")
            for half in range(2):
                to = duo(f"tok{half}")
                for k in range(KD):
                    last = pe.transpose(to[:, k * P:(k + 1) * P], hT[:, k, half * P:(half + 1) * P], ident)
                last.then_inc(turned, 1)
            enter(pe, "logits")
            wr = view(g1("route_w"), 0, KD, N_GROUPS + N_EXPERTS)
            for t in range(TT):
                for k in range(KD):
                    last = mm(view(duo("logits"), 0, TT, N_GROUPS + N_EXPERTS)[:, t, :], hT[:, k, t * P:(t + 1) * P],
                              wr[:, k, :], start=(k == 0), stop=(k == KD - 1))
            last.then_inc(logits_done, 1)
            pe.wait_ge(member_ready, 1)
            enter(pe, "rank")
            to = view(duo("rank"), 0, 3, N_EXPERTS)
            mem_t = member.rearrange("p (t g) e -> p t (g e)", t=TT)
            mm(to[:, 0, :], c("before"), mem_t[:, 0, :], start=True, stop=True)
            for o, (a, b) in ((1, ("ones", "before")), (2, ("ones", "ones"))):
                mm(to[:, o, :], c(a), mem_t[:, 0, :], start=True, stop=False)
                last = mm(to[:, o, :], c(b), mem_t[:, 1, :], start=False, stop=True)
            last.then_inc(ranks_done, 1)

            pe.wait_ge(passes_ready, 1)
            n_pass = pe.value_load(passes[0:1, 0:1], min_val=1, max_val=MAX_PASSES)
            for credit in (w1_done, w3_done, w2_done):
                pe.sem_inc(credit, 1)

            def gather(n, follows):
                pe.wait_ge(sel_ready, n + 1)
                g = view(psum[:, 1, :], 0, KD, P)
                for k in range(KD):
                    for t in range(TT):
                        mm(g[:, k, :], htok[:, t, k * P:(k + 1) * P],
                           sel[:, t].rearrange("p e s -> p (e s)"), start=(t == 0), stop=(t == TT - 1))
                if follows:
                    pe.wait_ge(ysb_ready, n)
                for t in range(TT):
                    last = pe.transpose(psum[:, 2, t * P:(t + 1) * P], selw[:, t].rearrange("p e s -> p (e s)"), ident)
                last.then_inc(gathered, 1)

            def turn(n, more_follow):
                pe.wait_ge(xs_ready, n + 1)
                for at, bank, done in ((0, 0, w1_done), (2, 1, w3_done)):
                    for e in range(2):
                        pe.wait_ge(moe_full[at + e], n * 16 + 16)
                    for k in range(KD):
                        for e in range(2):
                            rows = slice(e * SLOTS, (e + 1) * SLOTS)
                            last = mm(psum[rows, 1, bank * 512:bank * 512 + 512], xs[:, k, rows],
                                      view(ring[:, at + e, :], 0, KD, D_EXPERT)[:, k, :],
                                      start=(k == 0), stop=(k == KD - 1), skip_group_check=True)
                    last.then_inc(done, 1)
                pe.wait_ge(hid_ready, n + 1)
                pe.wait_ge(scat_added, n * 2 + 2)
                for f in range(4):
                    last = pe.transpose(psum[:, 3, 512 + f * P:512 + (f + 1) * P], hid[:, f * P:(f + 1) * P], ident)
                last.then_inc(hidT_done, 1)
                pe.wait_ge(hidT_ready, n + 1)
                pe.wait_ge(selwT_ready, n + 1)
                for e in range(2):
                    pe.wait_ge(moe_full[4 + e], n * 16 + 16)
                for f in range(4):
                    for half in range(2):
                        for e in range(2):
                            rows = slice(e * SLOTS, (e + 1) * SLOTS)
                            last = mm(psum[rows, 2, half * 512:half * 512 + 512], hidT[:, f, rows],
                                      view(ring[:, 4 + e, :], 0, 4, D)[:, f, half * 512:half * 512 + 512],
                                      start=(f == 0), stop=(f == 3), skip_group_check=True)
                last.then_inc(w2_done, 1)
                if more_follow:
                    gather(n + 1, True)
                pe.wait_ge(ysb_ready, n + 1)
                for half, d in enumerate((0, 3)):
                    for k in range(4):
                        kk = half * 4 + k
                        last = mm(view(psum[:, d, :], 0, 4, SEQ)[:, k, :], ysb[:, kk * P:(kk + 1) * P], selwT,
                                  start=True, stop=True)
                    last.then_inc(scat_done, 1)

            with pe.Fori(0, n_pass) as p:
                gather(p * PAIRS, False)
                with pe.Fori(0, PAIRS - 1) as q:
                    turn(p * PAIRS + q, True)
                turn(p * PAIRS + (PAIRS - 1), False)
            pe.wait_ge(scat_added, n_pass * (2 * PAIRS) + 2)
            pe.wait_ge(sq_ready, 6)
            sums("n_final", c("mean_model"), sq, KD)

            pe.sem_inc(chunk_used, PARTS)
            with pe.Fori(0, LAYERS) as l:
                norm_no = 0
                for w in WORK:
                    kind = w[0]
                    if kind == "norm":
                        at = {"mix": 0, "cross": 2, "ffn": 3}[w[1]]
                        pe.wait_ge(sq_ready, l * 4 + 6 + at + 1)
                        sums(f"l_{w[1]}", c("mean_model"), sq, KD, l)
                        if w[1] != "cross":
                            pe.wait_ge(h_ready, l * 3 + 4 + norm_no + 1)
                        norm_no += 1
                    elif kind == "proj":
                        split_project(w[1], f"p_{w[2]}", l)
                    elif kind == "proj_v":
                        i, name = w[1], f"p_{w[2]}"
                        enter(pe, name, l)
                        for o in range(4):
                            n = SPLIT_THROUGH[i] - 4 + o
                            parts_ready(pe, n, l)
                            hi, lo = chunk_part(w_hi, n), chunk_part(w_lo, n)
                            for t in range(TT):
                                to = duo(name)[:, t * 512:(t + 1) * 512]
                                for j in range(2):
                                    k = 2 * o + j
                                    tok = slice(t * P, (t + 1) * P)
                                    mm(to, h_hi[:, k, tok], hi[:, j, :], start=(k == 0), stop=False, skip_group_check=True)
                                    mm(to, h_hi[:, k, tok], lo[:, j, :], start=False, stop=False, skip_group_check=True)
                                    last = mm(to, h_lo[:, k, tok], hi[:, j, :], start=False, stop=(k == KD - 1),
                                              skip_group_check=True)
                            last.then_inc(chunk_used, 1)
                    elif kind == "index_proj":
                        i = w[1]
                        raw_arrived(pe, i, l)
                        enter(pe, "p_idx", l)
                        wx = view(raw_of(i), 0, KD, 324)
                        to = duo("p_idx")
                        for o in range(2):
                            for k in range(KD):
                                mm(to[:, o * SEQ:(o + 1) * SEQ], wx[:, k, o * P:(o + 1) * P], hT[:, k, :],
                                   start=(k == 0), stop=(k == KD - 1))
                        for half in range(2):
                            for k in range(KD):
                                mm(to[half * 64:half * 64 + 64, 512:512 + SEQ], wx[:, k, 256:320], hT[:, k, :],
                                   start=(k == 0), stop=(k == KD - 1))
                        for t in range(TT):
                            for k in range(KD):
                                last = mm(to[:, 768 + 4 * t:772 + 4 * t], hT[:, k, t * P:(t + 1) * P], wx[:, k, 320:324],
                                          start=(k == 0), stop=(k == KD - 1))
                        last.then_inc(direct_done, 1)
                    elif kind == "rope":
                        r, name = w[1], w[2]
                        freed(pe, f"p_{name}", l)
                        enter(pe, f"r_{name}", l)
                        to = view(duo(f"r_{name}"), 0, 4, SEQ)
                        for k in range(3 if name == "idx" else 4):
                            last = mm(to[:, k, :], c("rotate"), heads[name][:, k, :], start=True, stop=True)
                        last.then_inc(rot_done, 1)
                    elif kind == "index":
                        t = w[1]
                        nk = P * (t + 1)
                        name = f"i_{t}"
                        pe.wait_ge(rope_ready, l * 5 + 3)
                        enter(pe, name, l)
                        for h in range(4):
                            cc, r = h // 2, h % 2
                            rows = slice(64 * r, 64 * r + 64)
                            last = mm(duo(name)[:, r * 512 + cc * SEQ:r * 512 + cc * SEQ + nk],
                                      qiT[rows, cc, t * P:(t + 1) * P], qiT[rows, 2, 0:nk], start=True, stop=True)
                        last.then_inc(idx_done, 1)
                    elif kind == "gates":
                        i, name, o = w[1], f"g_{w[2]}", w[3]
                        if o == 0:
                            enter(pe, name, l)
                        split_chunk(i, o, duo(name)[:, o * SEQ:(o + 1) * SEQ], l)
                    elif kind == "scores":
                        u = w[1]
                        ukind, cc, qt, nk, qb, kb = unit_aps(u)
                        if u == 0:
                            freed(pe, "p_ka", l)
                        elif u == 8:
                            pe.wait_ge(rope_ready, l * 5 + 2)
                        elif u == 16:
                            pe.wait_ge(rope_ready, l * 5 + 5)
                        elif u == 24:
                            freed(pe, "xkv", l)
                            freed(pe, "xq", l)
                        enter(pe, f"u_{u}", l)
                        for r in range(2):
                            rows = slice(64 * r, 64 * r + 64)
                            last = mm(duo(f"u_{u}")[:, r * 512:r * 512 + nk], qb[rows, cc, qt * P:(qt + 1) * P],
                                      kb[rows, cc, 0:nk], start=True, stop=True)
                        last.then_inc(scores_done, 1)
                    elif kind == "turn":
                        u = w[1]
                        ukind, cc, qt, nk, _, _ = unit_aps(u)
                        pe.wait_ge(probs_ready, l * N_UNITS + u + 1)
                        at = 0
                        for r in range(1 if ukind == "B" else 2):
                            for kt in range(nk // P):
                                last = pe.transpose(duo(f"u_{u}")[:, at * P:(at + 1) * P],
                                                    probs[:, u % 3, r, kt * P:(kt + 1) * P], ident)
                                at += 1
                        last.then_inc(probsT_done, 1)
                    elif kind == "apply":
                        u = w[1]
                        ukind, cc, qt, nk, _, _ = unit_aps(u)
                        pe.wait_ge(probsT_ready, l * N_UNITS + u + 1)
                        nt = nk // P
                        to = duo(f"u_{u}")
                        if ukind == "B":
                            for kt in range(nt):
                                last = mm(to[:, 512:512 + P], values["vb"][:, kt, cc * P:(cc + 1) * P],
                                          probsT[:, u % 2, kt * P:(kt + 1) * P], start=(kt == 0), stop=(kt == nt - 1))
                        else:
                            v = vx if ukind == "X" else vals[:, 0]
                            for r in range(2):
                                for kt in range(nt):
                                    at = r * nt + kt
                                    last = mm(to[64 * r:64 * r + 64, 512:512 + P],
                                              v[:, kt, (2 * cc + r) * CH:(2 * cc + r + 1) * CH],
                                              probsT[:, u % 2, at * P:(at + 1) * P],
                                              start=(kt == 0), stop=(kt == nt - 1))
                        last.then_inc(attn_done, 1)
                    elif kind == "subln":
                        pe.wait_ge(sq_ready, l * 4 + 6 + 2)
                        enter(pe, "subln", l)
                        for k in range(4):
                            last = mm(view(duo("subln"), 0, 4, SEQ)[:, k, :], c("mean_sub"), sq[:, k, :],
                                      start=True, stop=True)
                        last.then_inc(sums_done, 1)
                    elif kind == "up":
                        i, b = w[1], w[2]
                        if b == 0:
                            freed(pe, "u_7", l)
                        elif b == 1:
                            pe.wait_ge(subln_ready, l + 1)
                        else:
                            freed(pe, "u_23", l)
                        raw_arrived(pe, i, l)
                        wu = view(raw_of(i), 0, 4, D)
                        for half in range(2):
                            enter(pe, f"up_{b}_{half}", l)
                            to = view(duo(f"up_{b}_{half}"), 0, 4, SEQ)
                            for o in range(4):
                                oo = half * 4 + o
                                for k in range(4):
                                    last = mm(to[:, o, :], wu[:, k, oo * P:(oo + 1) * P], outs[:, b, k, :],
                                              start=(k == 0), stop=(k == 3))
                            if half == 0:
                                last.then_inc(up_half, 1)
                        last.then_inc(direct_done, 1)
                    elif kind == "out":
                        split_project(w[1], f"out_{w[2]}", l)
                    elif kind == "cross_q":
                        raw_arrived(pe, w[1], l)
                        pe.wait_ge(h_ready, l * 3 + 4 + 2)
                        project(raw_of(w[1]), "xq", hT, direct_done, l, chunks=2, width=SEQ)
                    elif kind == "cross_k":
                        i = w[1]
                        raw_arrived(pe, i, l)
                        enter(pe, "xkv", l)
                        wk = view(raw_of(i), 0, KD, HALF)
                        to = view(duo("xkv"), 0, 4, SEQ)
                        for o in range(2):
                            for k in range(KD):
                                mm(to[:, o, :], wk[:, k, o * P:(o + 1) * P], memT[:, k, :],
                                   start=(k == 0), stop=(k == KD - 1))
                    elif kind == "cross_v":
                        for t in range(TT):
                            for k in range(KD):
                                last = mm(to[:, 2 + t, :], memT[:, k, t * P:(t + 1) * P], wk[:, k, SEQ:2 * SEQ],
                                          start=(k == 0), stop=(k == KD - 1))
                        last.then_inc(direct_done, 1)
                    elif kind == "cross_o":
                        i = w[1]
                        raw_arrived(pe, i, l)
                        freed(pe, "u_27", l)
                        wo = view(raw_of(i), 0, 2, D)
                        for half in range(2):
                            enter(pe, f"xo_{half}", l)
                            to = view(duo(f"xo_{half}"), 0, 4, SEQ)
                            for o in range(4):
                                oo = half * 4 + o
                                for k in range(2):
                                    last = mm(to[:, o, :], wo[:, k, oo * P:(oo + 1) * P], ox[:, k, :],
                                              start=(k == 0), stop=(k == 1))
                        last.then_inc(direct_done, 1)
                    elif kind == "gate_up":
                        split_project(w[1], f"gu_{w[2]}", l)
                    elif kind == "down":
                        k = w[1]
                        n = SPLIT_THROUGH[34] + k
                        if k == 0:
                            enter(pe, "dn_0", l)
                            enter(pe, "dn_1", l)
                        if k % 2 == 0:
                            pe.wait_ge(act_lo_ready, l * (KF // 2) + k // 2 + 1)
                        parts_ready(pe, n, l)
                        hi, lo = chunk_part(w_hi, n), chunk_part(w_lo, n)
                        for o in range(KD):
                            to = view(duo(f"dn_{o // 4}"), 0, 4, SEQ)[:, o % 4, :]
                            mm(to, hi[:, o, :], act_hi[:, k, :], start=(k == 0 and o % 2 == 0), stop=False,
                               skip_group_check=True)
                            mm(to, hi[:, o, :], act_lo[:, k, :], start=False, stop=False, skip_group_check=True)
                            last = mm(to, lo[:, o, :], act_hi[:, k, :], start=False, stop=(k == KF - 1),
                                      skip_group_check=True)
                        last.then_inc(chunk_used, 1)

            pe.wait_ge(sq_ready, 6 + 4 * LAYERS + 1)
            sums("n_last", c("mean_model"), sq, KD)
            pe.wait_ge(h_ready, 4 + 3 * LAYERS + 1)
            for t in range(TT):
                enter(pe, f"out{t}")
                for k in range(KD):
                    last = pe.transpose(duo(f"out{t}")[:, k * P:(k + 1) * P], hT[:, k, t * P:(t + 1) * P], ident)
                last.then_inc(turned, 1)

        @block.scalar
        def _(act_e):
            nca = nc.scalar

            def f(out_ap, in_ap, func, **kw):
                return nca.activation(out_ap, in_ap, func, **kw)

            def copy(out_ap, in_ap):
                return nca.activation(out_ap, in_ap, ACT.Copy)

            def root(name, sums_no, l=0, per=0):
                act_e.wait_ge(sums_done, l * per + sums_no)
                return f(std[:], duo(name)[:, 0:SEQ], ACT.Sqrt, bias=eps[:])

            for d in range(DUOS):
                act_e.sem_inc(duo_free[d], 1)
            for half in range(2):
                act_e.wait_ge(turned, half + 1)
                copy(xT[:, half * 4:half * 4 + 4, :], view(duo(f"x{half}"), 0, 4, SEQ)).then_inc(free_of(f"x{half}"), 1)
            freed(act_e, "x0")
            freed(act_e, "x1")
            f(sq[:], xT[:], ACT.Square).then_inc(sq_ready, 1)
            act_e.wait_ge(pad_ready, 3)
            root("n_mix", 1).then_inc(std_ready, 1)

            done_piece(act_e, 0)
            copy(ub[:, :, PAD_B:PAD_B + SEQ], view(duo("win0"), 0, 4, SEQ)).then_inc(free_of("win0"), 1)
            done_piece(act_e, 1)
            f(sg, view(duo("win1"), 0, 4, SEQ), ACT.Sigmoid).then_inc(free_of("win1"), 1)
            done_piece(act_e, 2)
            copy(ua[:, :, PAD_A:PAD_A + SEQ], view(duo("win2"), 0, 4, SEQ)).then_inc(free_of("win2"), 1)
            done_piece(act_e, 4)
            copy(ab, view(duo("win4"), 0, 4, SEQ)).then_inc(free_of("win4"), 1)
            for half in range(2):
                act_e.wait_ge(turned, half + 3)
                copy(hT[:, half * 4:half * 4 + 4, :], view(duo(f"mem{half}"), 0, 4, SEQ)).then_inc(free_of(f"mem{half}"), 1)
            freed(act_e, "mem0")
            freed(act_e, "mem1")
            f(sq[:], hT[:], ACT.Square).then_inc(sq_ready, 1)
            act_e.wait_ge(sums_done, 2)
            f(mem_std, duo("n_mem")[:, 0:SEQ], ACT.Sqrt, bias=eps[:]).then_inc(free_of("n_mem"), 1)
            act_e.wait_ge(centred, 1)
            f(sq[:, 0:4], cb, ACT.Square).then_inc(sq_ready, 1)
            root("ln_var", 4).then_inc(std_ready, 1)
            act_e.wait_ge(conv_a_ready, 1)
            f(sq[:, 4:8], yT[:, 0:4], ACT.Square).then_inc(squares_a, 1)
            act_e.wait_ge(sums_done, 5)
            f(root_heads[:, 0:4], view(duo("heads0"), 0, 4, SEQ), ACT.Sqrt, bias=eps[:]).then_inc(std_ready, 1)
            act_e.wait_ge(yb_raw, 1)
            for k in range(4):
                last = f(yT[:, 4 + k, :], cb[:, k, :], ACT.Silu, bias=g1("ln_b")[:, k:k + 1])
            last.then_inc(silu_b, 1)
            act_e.wait_ge(silu_b, 1)
            f(sq[:, 0:4], yT[:, 4:8], ACT.Square).then_inc(sq_ready, 1)
            act_e.wait_ge(sums_done, 6)
            f(root_heads[:, 4:8], view(duo("heads1"), 0, 4, SEQ), ACT.Sqrt, bias=eps[:]).then_inc(std_ready, 1)
            freed(act_e, "wout0")
            freed(act_e, "wout1")
            f(sq[:], xT[:], ACT.Square).then_inc(sq_ready, 1)
            root("n_ffn", 7).then_inc(std_ready, 1)
            for t in range(TT):
                act_e.wait_ge(turned, 5 + t)
                copy(htok[:, t, :], duo(f"tok{t}")).then_inc(free_of(f"tok{t}"), 1)
            act_e.wait_ge(gneg_ready, 1)
            f(gexp, gexp, ACT.Exp).then_inc(gexp_ready, 1)
            act_e.wait_ge(d12_ready, 1)
            f(e12, d12, ACT.Exp).then_inc(e12_ready, 1)

            act_e.wait_ge(passes_ready, 1)
            n_pass = act_e.value_load(passes[0:1, 0:1], min_val=1, max_val=MAX_PASSES)

            def gathered_tokens(n):
                act_e.wait_ge(gathered, n + 1)
                copy(xs, view(psum[:, 1, :], 0, KD, P)).then_inc(xs_ready, 1)

            def combination():
                copy(selwT, psum[:, 2, 0:SEQ]).then_inc(selwT_ready, 1)

            def turn(n, more_follow):
                act_e.wait_ge(w1_done, n + 2)
                f(silu1, psum[:, 1, 0:512], ACT.Silu).then_inc(silu1_ready, 1)
                act_e.wait_ge(hidT_done, n + 1)
                copy(hidT, view(psum[:, 3, 512:1024], 0, 4, P)).then_inc(hidT_ready, 1)
                act_e.wait_ge(w2_done, n + 2)
                copy(ysb, psum[:, 2, :]).then_inc(ysb_ready, 1)
                if more_follow:
                    gathered_tokens(n + 1)
                act_e.wait_ge(scat_done, n * 2 + 2)
                if more_follow:
                    combination()

            with act_e.Fori(0, n_pass) as p:
                gathered_tokens(p * PAIRS)
                combination()
                with act_e.Fori(0, PAIRS - 1) as q:
                    turn(p * PAIRS + q, True)
                turn(p * PAIRS + (PAIRS - 1), False)
            act_e.wait_ge(scat_added, n_pass * (2 * PAIRS) + 2)
            f(sq[:], xT[:], ACT.Square).then_inc(sq_ready, 1)
            root("n_final", 8).then_inc(std_ready, 1)

            with act_e.Fori(0, LAYERS) as l:
                norm_no = 0
                for w in WORK_SPLIT:
                    kind = w[0]
                    if kind == "split":
                        n = w[1]
                        i, o = chunk_source(n)
                        if o == 0:
                            raw_arrived(act_e, i, l)
                        act_e.wait_ge(chunk_used, l * N_CHUNKS + PARTS + buffer_user(n) + 1)
                        copy(chunk_part(w_hi, n), chunk_raw(n)).then_inc(w_hi_ready, 1)
                    elif kind == "norm":
                        name = f"l_{w[1]}"
                        if w[1] == "mix":
                            act_e.wait_ge(x_ready, l + 1)
                        elif w[1] == "cross":
                            freed(act_e, "out_0", l)
                            freed(act_e, "out_1", l)
                        else:
                            freed(act_e, "xo_0", l)
                            freed(act_e, "xo_1", l)
                        f(sq[:], xT[:], ACT.Square).then_inc(sq_ready, 1)
                        act_e.wait_ge(h_ready, l * 3 + 4 + norm_no)
                        norm_no += 1
                        root(name, 8 + {"mix": 0, "cross": 2, "ffn": 3}[w[1]] + 1, l, 4).then_inc(std_ready, 1)
                        if w[1] != "cross":
                            for half in range(2):
                                if half == 0:
                                    act_e.wait_ge(h_half, l * 2 + (1 if w[1] == "mix" else 2))
                                else:
                                    act_e.wait_ge(h_ready, l * 3 + 4 + norm_no)
                                copy(h_hi[:, half * 4:half * 4 + 4, :], hT[:, half * 4:half * 4 + 4, :]
                                     ).then_inc(h_hi_ready, 1)
                    elif kind == "lam":
                        act_e.wait_ge(lam_dot, l + 1)
                        f(lam[:, 0:2], lam[:, 0:2], ACT.Exp).then_inc(lam_exp, 1)
                    elif kind == "proj":
                        product_done(act_e, w[1], l)
                        name = w[2]
                        copy(heads[name], view(duo(f"p_{name}"), 0, 4, SEQ)).then_inc(free_of(f"p_{name}"), 1)
                    elif kind == "proj_v":
                        product_done(act_e, w[1], l)
                        name = w[2]
                        copy(values[name], view(duo(f"p_{name}"), 0, TT, HALF)).then_inc(free_of(f"p_{name}"), 1)
                    elif kind == "index_proj":
                        product_done(act_e, w[1], l)
                        copy(qiT[:], view(duo("p_idx"), 0, 3, SEQ)).then_inc(idx_raw, 1)
                    elif kind == "gates":
                        if w[3] == 3:
                            product_done(act_e, w[1], l)
                            g = w[2]
                            f(gates[:, 4 * g:4 * g + 4, :], view(duo(f"g_{g}"), 0, 4, SEQ), ACT.Tanh, scale=0.5
                              ).then_inc(free_of(f"g_{g}"), 1)
                    elif kind == "scores":
                        u = w[1]
                        _, _, _, nk, _, _ = unit_aps(u)
                        act_e.wait_ge(rowmax_ready, l * N_UNITS + u + 1)
                        for r in range(2):
                            last = f(probs[:, u % 3, r, 0:nk], probs[:, u % 3, r, 0:nk], ACT.Exp,
                                     bias=stat[:, u % 3, r:r + 1], accum_out=stat[:, u % 3, 2 + r:3 + r])
                        last.then_inc(exp_ready, 1)
                    elif kind == "turn":
                        u = w[1]
                        ukind, _, _, nk, _, _ = unit_aps(u)
                        n = nk * (1 if ukind == "B" else 2)
                        act_e.wait_ge(probsT_done, l * N_UNITS + u + 1)
                        copy(probsT[:, u % 2, 0:n], duo(f"u_{u}")[:, 0:n]).then_inc(probsT_ready, 1)
                    elif kind == "apply":
                        u = w[1]
                        ukind, cc, qt, nk, _, _ = unit_aps(u)
                        act_e.wait_ge(attn_done, l * N_UNITS + u + 1)
                        copy(o_of[ukind][:, cc, qt * P:(qt + 1) * P], duo(f"u_{u}")[:, 512:512 + P]
                             ).then_inc(free_of(f"u_{u}"), 1)
                    elif kind == "index":
                        t = w[1]
                        nk = P * (t + 1)
                        act_e.wait_ge(idx_done, l * 2 + t + 1)
                        f(relu[t][:, :, 0:nk], view(duo(f"i_{t}"), 0, 4, SEQ)[:, :, 0:nk], ACT.Relu, scale=SCALE
                          ).then_inc(relu_ready, 1)
                    elif kind == "square_b":
                        freed(act_e, "u_15", l)
                        act_e.wait_ge(rope_ready, l * 5 + 5)
                        f(sq[:, 0:4], outs[:, 1], ACT.Square).then_inc(sq_ready, 1)
                    elif kind == "subln":
                        act_e.wait_ge(sums_done, l * 4 + 8 + 2)
                        f(sq[:, 4:8], view(duo("subln"), 0, 4, SEQ), ACT.Sqrt, bias=eps[:]).then_inc(std_ready, 1)
                    elif kind == "cross_q":
                        product_done(act_e, w[1], l)
                        copy(qx, view(duo("xq"), 0, 2, SEQ)).then_inc(free_of("xq"), 1)
                    elif kind == "up" and w[2] == 2:
                        for half in range(2):
                            act_e.wait_ge(mixed_ready, l * 2 + half + 1)
                            copy(h_hi[:, half * 4:half * 4 + 4, :], hT[:, half * 4:half * 4 + 4, :]
                                 ).then_inc(h_hi_ready, 1)
                    elif kind == "cross_v":
                        product_done(act_e, w[1], l)
                        copy(kx, view(duo("xkv"), 0, 2, SEQ)).then_inc(kx_ready, 1)
                        copy(vx, view(duo("xkv"), 512, TT, SEQ)).then_inc(free_of("xkv"), 1)
                    elif kind == "gate_up":
                        i = w[2]
                        product_done(act_e, w[1], l)
                        if i >= 2:
                            act_e.wait_ge(act_lo_ready, l * (KF // 2) + i - 1)
                        f(probs[:, i % 2], view(duo(f"gu_{i}"), 0, 2, SEQ), ACT.Silu).then_inc(silu_ready, 1)
                        freed(act_e, f"gu_{i}", l)
                        copy(act_hi[:, 2 * i:2 * i + 2, :], probs[:, i % 2]).then_inc(act_hi_ready, 1)

            act_e.wait_ge(x_ready, LAYERS + 1)
            f(sq[:], xT[:], ACT.Square).then_inc(sq_ready, 1)
            root("n_last", 8 + 4 * LAYERS + 1).then_inc(std_ready, 1)
            for t in range(TT):
                act_e.wait_ge(turned, 7 + t)
                copy(otok[:, t, :], duo(f"out{t}")).then_inc(otok_ready, 1)

        @block.vector
        def _(v):
            link, linked = linker(v, dve_chain)

            def wide(ap, shape):
                return ap.broadcast_to(shape)

            def norm(name, std_no, src, gain, dst, l=0, per=0, halves=False):
                v.wait_ge(std_ready, l * per + std_no)
                link(v.reciprocal(rstd[:], std[:]))
                for k in range(KD):
                    last = v.scalar_tensor_tensor(dst[:, k, :], src[:, k, :], gain[:, k:k + 1], rstd[:], ALU.mult, ALU.mult)
                    if k == 0:
                        last.then_inc(free_of(name), 1)
                    if k == 3 and halves:
                        last.then_inc(h_half, 1)
                last.then_inc(h_ready, 1)

            v.sem_inc(w_lo_ready, LAST_CHUNKS)
            v.memset(eps[:], EPS).then_inc(pad_ready, 1)
            v.memset(ua, 0.0).then_inc(pad_ready, 1)
            v.memset(ub, 0.0).then_inc(pad_ready, 1)
            v.wait_ge(consts_in, 32)
            norm("n_mix", 1, xT, g1("norm_mix"), hT)

            freed(v, "win0")
            freed(v, "win1")
            ub_mid = ub[:, :, PAD_B:PAD_B + SEQ]
            link(v.tensor_tensor(ub_mid, ub_mid, sg, ALU.mult))

            def convolve(dst, src, taps, weight, bias):
                for j in taps:
                    for k in range(4):
                        if j:
                            v.wait_ge(dve_chain, linked[0] - 3)
                        tap = weight[:, j * 4 + k:j * 4 + k + 1]
                        if j == 0:
                            ins = v.tensor_scalar(dst[:, k, :], src[:, k, 0:SEQ], tap, bias[:, k:k + 1] if bias is not None else 0.0,
                                                  ALU.mult, ALU.add)
                        else:
                            ins = v.scalar_tensor_tensor(dst[:, k, :], src[:, k, j:j + SEQ], tap, dst[:, k, :],
                                                         ALU.mult, ALU.add)
                        linked[0] += 1
                        ins.then_inc(dve_chain, 1)
                v.wait_ge(dve_chain, linked[0])

            convolve(cb, ub, range(TAPS_B - 6), g1("conv_b"), g1("conv_bias"))
            done_piece(v, 3)
            freed(v, "win2")
            ua_mid = ua[:, :, PAD_A:PAD_A + SEQ]
            v.tensor_tensor(ua_mid, view(duo("win3"), 0, 4, SEQ), ua_mid, ALU.mult).then_inc(free_of("win3"), 1)
            convolve(cb, ub, range(TAPS_B - 6, TAPS_B), g1("conv_b"), g1("conv_bias"))
            v.sem_inc(conv_ready, 1)
            v.wait_ge(sums_done, 3)
            v.tensor_tensor(cb, cb, duo("ln_mean")[:, 0:SEQ].unsqueeze(1).broadcast_to([P, 4, SEQ]),
                            ALU.subtract).then_inc(centred, 1)
            v.wait_ge(centred, 1)
            v.sem_inc(free_of("ln_mean"), 1)
            freed(v, "win3")
            convolve(yT[:, 0:4], ua, range(TAPS_A), g1("conv_a"), None)
            freed(v, "win4")
            v.tensor_tensor(yT[:, 0:4], yT[:, 0:4], ab, ALU.mult).then_inc(conv_a_ready, 1)
            v.wait_ge(std_ready, 2)
            link(v.reciprocal(rstd[:], std[:]))
            for k in range(4):
                last = v.scalar_tensor_tensor(cb[:, k, :], cb[:, k, :], g1("ln_g")[:, k:k + 1], rstd[:], ALU.mult, ALU.mult)
                if k == 0:
                    last.then_inc(free_of("ln_var"), 1)
            last.then_inc(yb_raw, 1)
            for half in range(2):
                v.wait_ge(std_ready, 3 + half)
                part = root_heads[:, half * 4:half * 4 + 4, :]
                link(v.reciprocal(part, part))
                for k in range(4):
                    kk = half * 4 + k
                    last = v.scalar_tensor_tensor(yT[:, kk, :], yT[:, kk, :], g1("beta")[:, kk:kk + 1],
                                                  root_heads[:, kk, :], ALU.mult, ALU.mult)
                    if k == 0:
                        last.then_inc(free_of(f"heads{half}"), 1)
            last.then_inc(y_ready, 1)
            freed(v, "n_mem")
            link(v.reciprocal(rstd[:], mem_std))
            for k in range(KD):
                last = v.scalar_tensor_tensor(memT[:, k, :], hT[:, k, :], g1("mem_norm")[:, k:k + 1], rstd[:],
                                              ALU.mult, ALU.mult)
            last.then_inc(h_ready, 1)
            v.wait_ge(h_ready, 2)
            for half in range(2):
                done_piece(v, 5 + half)
                part = xT[:, half * 4:half * 4 + 4, :]
                v.tensor_tensor(part, part, view(duo(f"wout{half}"), 0, 4, SEQ), ALU.add).then_inc(free_of(f"wout{half}"), 1)
            norm("n_ffn", 5, xT, g1("norm_ffn"), hT)

            v.wait_ge(logits_done, 1)
            nl = G + N_EXPERTS
            v.tensor_tensor(logit, view(duo("logits"), 0, TT, nl),
                            g1("route_b").unsqueeze(1).broadcast_to([P, TT, nl]), ALU.add).then_inc(free_of("logits"), 1)
            freed(v, "logits")
            lg, lex = logit[:, :, 0:G], logit[:, :, G:nl]

            def bc(ap, n):
                return ap.broadcast_to([P, TT, n])

            def first_of(dst, values_ap, peak, tmp, tmp_max, n):
                order = c("first")[:, 0:n].unsqueeze(1).broadcast_to([P, TT, n])
                link(v.tensor_tensor(tmp, values_ap, bc(peak, n), ALU.is_equal))
                link(v.tensor_tensor(tmp, tmp, order, ALU.mult))
                link(v.tensor_reduce(tmp_max, tmp, AX.X, ALU.max))
                link(v.tensor_tensor(dst, tmp, bc(tmp_max, n), ALU.is_equal))

            link(v.tensor_reduce(gmax, lg, AX.X, ALU.max))
            v.tensor_tensor(gexp, lg, bc(gmax, G), ALU.subtract).then_inc(gneg_ready, 1)
            first_of(gone, lg, gmax, gc, gcm, G)
            gone8 = gone.rearrange("p t g -> p (t g)").unsqueeze(2).broadcast_to([P, TT * G, E])
            for t in range(TT):
                link(v.tensor_tensor(le4[:, t * G:(t + 1) * G, :], lex[:, t, :].rearrange("p (g e) -> p g e", g=G),
                                     gone8[:, t * G:(t + 1) * G, :], ALU.mult))
                link(v.tensor_reduce(le[:, t, :], le4[:, t * G:(t + 1) * G, :].rearrange("p g e -> p e g"), AX.X, ALU.add))
            link(v.tensor_reduce(m1, le, AX.X, ALU.max))
            first_of(f1, le, m1, fc, fm, E)
            link(v.scalar_tensor_tensor(le2, f1, NEG, le, ALU.mult, ALU.add))
            link(v.tensor_reduce(m2, le2, AX.X, ALU.max))
            v.tensor_tensor(d12, m2, m1, ALU.subtract).then_inc(d12_ready, 1)
            first_of(f2, le2, m2, fc, fm, E)
            v.wait_ge(gexp_ready, 1)
            link(v.tensor_reduce(gsum, gexp, AX.X, ALU.add))
            link(v.reciprocal(psel, gsum))
            v.wait_ge(e12_ready, 1)
            link(v.tensor_scalar(wa, e12, 1.0, None, ALU.add))
            link(v.reciprocal(wa, wa))
            link(v.tensor_tensor(wa, wa, psel, ALU.mult))
            link(v.tensor_tensor(wb, e12, wa, ALU.mult))
            link(v.tensor_tensor(wsum, f1, bc(wa, E), ALU.mult))
            link(v.tensor_tensor(fc, f2, bc(wb, E), ALU.mult))
            link(v.tensor_tensor(wsum, wsum, fc, ALU.add))
            link(v.tensor_tensor(fsum, f1, f2, ALU.add))
            for t in range(TT):
                g8 = gone8[:, t * G:(t + 1) * G, :]
                link(v.tensor_tensor(combine[:, t * G:(t + 1) * G, :], g8,
                                     wsum[:, t, :].unsqueeze(1).broadcast_to([P, G, E]), ALU.mult))
                link(v.tensor_tensor(member[:, t * G:(t + 1) * G, :], g8,
                                     fsum[:, t, :].unsqueeze(1).broadcast_to([P, G, E]), ALU.mult))
            v.sem_inc(member_ready, 1)
            member2 = member.rearrange("p (t g) e -> p t (g e)", t=TT)
            combine2 = combine.rearrange("p (t g) e -> p t (g e)", t=TT)
            link(v.tensor_scalar(rank, member2, -4096.0, 4096.0, ALU.mult, ALU.add))
            v.wait_ge(ranks_done, 1)
            placed = view(duo("rank"), 0, 3, N_EXPERTS)
            link(v.tensor_tensor(rank, rank, placed[:, 0:2, :], ALU.add))
            link(v.tensor_reduce(most, placed[:, 2, :], AX.X, ALU.max))
            v.sem_inc(free_of("rank"), 1)
            for i in range(3):
                link(v.tensor_scalar(more[:, i:i + 1], most, float((i + 1) * SLOTS), None, ALU.is_gt))
            link(v.tensor_reduce(count, more, AX.X, ALU.add))
            link(v.tensor_scalar(passes[:, 0:1], count, 1.0, None, ALU.add))
            v.tensor_copy(passes[:, 1:2], count).then_inc(passes_ready, 1)
            v.wait_ge(passes_ready, 1)

            n_pass = v.value_load(passes[0:1, 0:1], min_val=1, max_val=MAX_PASSES)
            v.sem_inc(scat_added, 2)
            slots = c("iota").unsqueeze(1).unsqueeze(1).broadcast_to([P, TT, 2, SLOTS])

            def choose(q, n):
                v.tensor_tensor(sel, slots, expert_cols(rank, q), ALU.is_equal).then_inc(moe_chain, 1)
                v.wait_ge(moe_chain, n + 1)
                v.tensor_tensor(selw, sel, expert_cols(combine2, q), ALU.mult).then_inc(sel_ready, 1)

            def turn(q, n, more_follow):
                v.wait_ge(silu1_ready, n + 1)
                v.wait_ge(w3_done, n + 2)
                v.tensor_tensor(hid, silu1, psum[:, 1, 512:1024], ALU.mult).then_inc(hid_ready, 1)
                if more_follow:
                    choose(q + 1, n + 1)
                for half, d in enumerate((0, 3)):
                    v.wait_ge(scat_done, n * 2 + half + 1)
                    part = xT[:, half * 4:half * 4 + 4, :]
                    v.tensor_tensor(part, part, view(psum[:, d, :], 0, 4, SEQ), ALU.add).then_inc(scat_added, 1)

            with v.Fori(0, n_pass) as p:
                choose(0, p * PAIRS)
                with v.Fori(0, PAIRS - 1) as q:
                    turn(q, p * PAIRS + q, True)
                turn(PAIRS - 1, p * PAIRS + (PAIRS - 1), False)
                v.tensor_scalar(rank, rank, -float(SLOTS), None, ALU.add).then_inc(shifted, 1)
                v.wait_ge(shifted, p + 1)
            v.wait_ge(scat_added, n_pass * (2 * PAIRS) + 2)
            norm("n_final", 6, xT, g1("norm_final"), xT)
            v.wait_ge(h_ready, 4)
            v.sem_inc(x_ready, 1)

            with v.Fori(0, LAYERS) as l:
                link, linked = linker(v, layer_chain, LAYER_LINKS, l)
                for w in WORK_SPLIT:
                    kind = w[0]
                    if kind == "low":
                        if w[1] not in POOL_CHUNKS:
                            low_part(v, w[1], l).then_inc(w_lo_ready, 1)
                    elif kind == "norm":
                        if w[1] == "mix":
                            v.wait_ge(vec2_in, l * 32 + 32)
                        norm(f"l_{w[1]}", 6 + {"mix": 0, "cross": 2, "ffn": 3}[w[1]] + 1, xT, g2(f"norm_{w[1]}"), hT, l, 4,
                             halves=w[1] != "cross")
                        if w[1] != "cross":
                            for half in range(2):
                                part = slice(half * 4, half * 4 + 4)
                                v.wait_ge(h_hi_ready, l * 6 + (0 if w[1] == "mix" else 4) + half + 1)
                                v.tensor_tensor(h_lo[:, part, :], hT[:, part, :], h_hi[:, part, :].bitcast(F32),
                                                ALU.subtract).then_inc(h_lo_ready, 1)
                    elif kind == "lam":
                        lv = view(g2("lambda"), 0, 2, 2, CH)
                        dots = view(score, 0, 2, CH)
                        link(v.tensor_tensor(dots, lv[:, :, 0, :], lv[:, :, 1, :], ALU.mult))
                        v.tensor_reduce(lam[:, 0:2], dots, AX.X, ALU.add).then_inc(lam_dot, 1)
                        link(v.memset(win[0:CHUNK, :, 0:CHUNK], NEG))
                        link(v.tensor_tensor(lam[:, 3:4], g2("subln"), g2("one_less"), ALU.mult))
                        v.wait_ge(lam_exp, l + 1)
                        link(v.tensor_tensor(lam[:, 2:3], lam[:, 1:2], lam[:, 0:1], ALU.subtract))
                        link(v.tensor_tensor(lam[:, 2:3], lam[:, 2:3], g2("lam_init"), ALU.subtract))
                    elif kind == "rope":
                        r, name = w[1], w[2]
                        k = 3 if name == "idx" else 4
                        v.wait_ge(rot_done, l * 5 + r + 1)
                        v.tensor_tensor(sq[:, 0:k], view(duo(f"r_{name}"), 0, 4, SEQ)[:, 0:k],
                                        c("sin").unsqueeze(1).broadcast_to([P, k, SEQ]), ALU.mult
                                        ).then_inc(free_of(f"r_{name}"), 1)
                        freed(v, f"r_{name}", l)
                        v.wait_ge(cos_ready, l * 5 + r + 1)
                        v.tensor_tensor(heads[name][:, 0:k], heads[name][:, 0:k], sq[:, 0:k], ALU.add
                                        ).then_inc(rope_ready, 1)
                        v.wait_ge(rope_ready, l * 5 + r + 1)
                    elif kind == "index_proj":
                        product_done(v, w[1], l)
                        v.wait_ge(idx_raw, l + 1)
                        v.tensor_scalar(wi[:].rearrange("p t h -> p (t h)"), duo("p_idx")[:, 768:776], 0.5, None,
                                        ALU.mult).then_inc(free_of("p_idx"), 1)
                    elif kind == "scores":
                        u = w[1]
                        ukind, cc, qt, nk, _, _ = unit_aps(u)
                        v.wait_ge(scores_done, l * N_UNITS + u + 1)
                        if u >= 3:
                            v.wait_ge(probsT_done, l * N_UNITS + u - 2)
                        s, d = probs[:, u % 3, :, 0:nk], view(duo(f"u_{u}"), 0, 2, 512)[:, :, 0:nk]
                        if ukind == "X":
                            link(v.tensor_scalar(s, d, SCALE, None, ALU.mult))
                        else:
                            if ukind == "A":
                                add = win[:, 2 * cc:2 * cc + 2, nk - 1::-1]
                            elif ukind == "B":
                                add = c("mask")[:, SEQ - nk:SEQ].unsqueeze(1).broadcast_to([P, 2, nk])
                            else:
                                if u == 16:
                                    v.wait_ge(selneg_ready, l * 2 + 2)
                                add = selneg[:, qt, 0:nk].unsqueeze(1).broadcast_to([P, 2, nk])
                            link(v.scalar_tensor_tensor(s, d, SCALE, add, ALU.mult, ALU.add))
                        v.tensor_reduce(stat[:, u % 3, 0:2], s, AX.X, ALU.max, negate=True).then_inc(rowmax_ready, 1)
                    elif kind == "probs":
                        u = w[1]
                        ukind, cc, qt, nk, _, _ = unit_aps(u)
                        st = stat[:, u % 3]
                        v.wait_ge(exp_ready, l * N_UNITS + u + 1)
                        link(v.reciprocal(st[:, 4:6], st[:, 2:4]))
                        if ukind == "B":
                            link(v.tensor_tensor(st[:, 5:6], st[:, 5:6], lam[:, 2:3], ALU.mult))
                            link(v.tensor_scalar(probs[:, u % 3, 1, 0:nk], probs[:, u % 3, 1, 0:nk], st[:, 5:6], None, ALU.mult))
                            v.scalar_tensor_tensor(probs[:, u % 3, 0, 0:nk], probs[:, u % 3, 0, 0:nk], st[:, 4:5],
                                                   probs[:, u % 3, 1, 0:nk], ALU.mult, ALU.add).then_inc(probs_ready, 1)
                        else:
                            s = probs[:, u % 3, :, 0:nk]
                            v.tensor_tensor(s, s, st[:, 4:6].unsqueeze(2).broadcast_to([P, 2, nk]), ALU.mult
                                            ).then_inc(probs_ready, 1)
                    elif kind == "index":
                        t = w[1]
                        nk = P * (t + 1)
                        v.wait_ge(relu_ready, l * 2 + t + 1)
                        v.sem_inc(free_of(f"i_{t}"), 1)
                        sc = score[:, 0:nk]
                        for h in range(4):
                            add = c("mask")[:, SEQ - nk:SEQ] if h == 0 else sc
                            link(v.scalar_tensor_tensor(sc, relu[t][:, (h % 2) * 2 + h // 2, 0:nk], wi[:, t, h:h + 1], add,
                                                        ALU.mult, ALU.add))
                        for _ in range(TOPK // 8):
                            v.sem_inc(held, 1)
                            link(v.max(top8[:], sc))
                            v.sem_inc(held, 1)
                            link(v.match_replace(sc, top8[:], sc, TAKEN))
                        v.tensor_scalar(selneg[:, t, 0:nk], sc, TAKEN / 3, NEG, ALU.is_gt, ALU.mult).then_inc(selneg_ready, 1)
                        v.wait_ge(selneg_ready, l * 2 + t + 1)
                    elif kind == "subln":
                        v.wait_ge(std_ready, l * 4 + 6 + 2)
                        v.sem_inc(free_of("subln"), 1)
                        link(v.reciprocal(sq[:, 4:8], sq[:, 4:8]))
                        v.scalar_tensor_tensor(outs[:, 1], outs[:, 1], lam[:, 3:4], sq[:, 4:8], ALU.mult, ALU.mult
                                               ).then_inc(subln_ready, 1)
                    elif kind == "up":
                        b = w[2]
                        if b == 0:
                            v.wait_ge(gates_ready, l * 6 + 6)
                        for half in range(2):
                            name = f"up_{b}_{half}"
                            if half == 0:
                                v.wait_ge(up_half, l * 3 + b + 1)
                            else:
                                product_done(v, w[1], l)
                            y = hT[:, half * 4:half * 4 + 4, :]
                            term = y if b == 0 else sq[:, half * 4:half * 4 + 4, :]
                            v.tensor_tensor(term, view(duo(name), 0, 4, SEQ),
                                            gates[:, 8 * b + 4 * half:8 * b + 4 * half + 4, :], ALU.mult
                                            ).then_inc(free_of(name), 1)
                            freed(v, name, l)
                            if b:
                                ins = v.tensor_tensor(y, y, term, ALU.add)
                                if b == 2:
                                    ins.then_inc(mixed_ready, 1)
                                else:
                                    link(ins)
                        if b == 2:
                            for half in range(2):
                                part = slice(half * 4, half * 4 + 4)
                                v.wait_ge(h_hi_ready, l * 6 + 2 + half + 1)
                                v.tensor_tensor(h_lo[:, part, :], hT[:, part, :], h_hi[:, part, :].bitcast(F32),
                                                ALU.subtract).then_inc(h_lo_ready, 1)
                    elif kind in ("out", "cross_o"):
                        product_done(v, w[1], l)
                        for half in ([w[2]] if kind == "out" else range(2)):
                            name = f"out_{half}" if kind == "out" else f"xo_{half}"
                            part = xT[:, half * 4:half * 4 + 4, :]
                            v.tensor_tensor(part, part, view(duo(name), 0, 4, SEQ), ALU.add).then_inc(free_of(name), 1)
                    elif kind == "gate_up":
                        i = w[2]
                        v.wait_ge(silu_ready, l * (KF // 2) + i + 1)
                        v.tensor_tensor(probs[:, i % 2], probs[:, i % 2], view(duo(f"gu_{i}"), 512, 2, SEQ),
                                        ALU.mult).then_inc(free_of(f"gu_{i}"), 1)
                        v.wait_ge(act_hi_ready, l * (KF // 2) + i + 1)
                        v.tensor_tensor(act_lo[:, 2 * i:2 * i + 2, :], probs[:, i % 2],
                                        act_hi[:, 2 * i:2 * i + 2, :].bitcast(F32), ALU.subtract).then_inc(act_lo_ready, 1)
                    elif kind == "down_add":
                        product_done(v, N_LAYER - 1, l)
                        v.tensor_tensor(xT[:, 0:4], xT[:, 0:4], view(duo("dn_0"), 0, 4, SEQ), ALU.add
                                        ).then_inc(free_of("dn_0"), 1)
                        freed(v, "dn_0", l)
                        v.tensor_tensor(xT[:, 4:8], xT[:, 4:8], view(duo("dn_1"), 0, 4, SEQ), ALU.add).then_inc(x_ready, 1)
                        v.wait_ge(x_ready, l + 2)
                        v.sem_inc(free_of("dn_1"), 1)
                assert linked[0] == LAYER_LINKS, linked

            link, linked = linker(v, last_chain)
            norm("n_last", 6 + 4 * LAYERS + 1, xT, g1("last_norm"), hT)

        @block.gpsimd
        def _(pool):
            pool.wait_ge(consts_in, 32)
            with pool.Fori(0, LAYERS) as l:
                for w in WORK_SPLIT:
                    kind = w[0]
                    if kind == "low":
                        if w[1] in POOL_CHUNKS:
                            low_part(pool, w[1], l).then_inc(w_lo_pool_ready, 1)
                    elif kind == "rope":
                        r, name = w[1], w[2]
                        k = 3 if name == "idx" else 4
                        pool.wait_ge(rot_done, l * 5 + r + 1)
                        pool.tensor_tensor(heads[name][:, 0:k], heads[name][:, 0:k],
                                           c("cos").unsqueeze(1).broadcast_to([P, k, SEQ]), ALU.mult).then_inc(cos_ready, 1)
                    elif kind == "gates" and w[3] == 3:
                        g = w[2]
                        freed(pool, f"g_{g}", l)
                        pool.sem_inc(held, 1)
                        part = gates[:, 4 * g:4 * g + 4, :]
                        pool.tensor_scalar(part, part, 0.5, 0.5, ALU.mult, ALU.add).then_inc(gates_ready, 1)


def constants():
    f = np.float32
    p = np.arange(P)
    out = {}
    out["ident"] = np.eye(P, dtype=f)
    out["mean_model"] = np.full((P, P), 1.0 / D, f)
    out["mean_mixb"] = np.full((P, P), 1.0 / D_A, f)
    out["mean_head"] = (p[:, None] // CH == p[None] // CH).astype(f) / CH
    out["mean_sub"] = np.full((P, P), 1.0 / (2 * CH), f)
    turn = np.zeros((P, P), f)
    for to in range(P):
        turn[to + 32 if to % CH < 32 else to - 32, to] = -1.0 if to % CH < 32 else 1.0
    out["rotate"] = turn
    out["before"] = (p[:, None] < p[None]).astype(f)
    out["ones"] = np.ones((P, P), f)
    inv = f(10000.0) ** (-np.arange(0, CH, 2, dtype=f) / f(CH))
    ang = (np.arange(SEQ, dtype=f)[None, :] * inv[p % 32][:, None]).astype(f)
    out["cos"], out["sin"] = np.cos(ang).astype(f), np.sin(ang).astype(f)
    mask = np.zeros((P, SEQ), f)
    mask[:CHUNK, SEQ - CHUNK:] = NEG
    out["mask"] = mask
    out["iota"] = np.broadcast_to(np.arange(SLOTS, dtype=f), (P, SLOTS))
    out["first"] = np.broadcast_to(np.arange(PER_GROUP, 0, -1).astype(f), (P, PER_GROUP))
    return np.ascontiguousarray(np.concatenate([out[n] for n in CONST], 1))


def kernel(x, norm_mix_g, w_in, conv_a_w, conv_b_w, conv_b_bias, ln_b_g, ln_b_b, beta_a, beta_b, w_out,
           norm_ffn_g, w_route_group, b_route_group, w_route_expert, b_route_expert, w1, w3, w2,
           norm_final_g, mem_2, norm_mix_2, w_in_2, rel_bias_a_2, lambda_vecs_2, subln_b_2, w_up_a_2,
           w_up_b_2, w_up_c_2, w_out_2, norm_cross_2, w_q_x_2, w_kv_x_2, w_o_x_2, norm_ffn_2, w_gu_2,
           w_down_2, mem_norm_2, final_norm_2):
    import concourse.bacc as bacc
    from concourse.bass_utils import run_bass_kernel_spmd as run

    def cols(a):
        a = np.asarray(a)
        a = a.reshape(-1, a.shape[-1] // P, P)
        return np.transpose(a, (2, 0, 1)).reshape(P, -1)

    def rows(a):
        a = np.asarray(a).reshape(1, -1)
        return np.broadcast_to(a, (P, a.shape[1]))

    wr = np.concatenate([np.asarray(w_route_group[0]), np.asarray(w_route_expert[0])], 1)
    wr = np.transpose(wr.reshape(KD, P, -1), (1, 0, 2)).reshape(P, -1)
    parts1 = {"norm_mix": cols(norm_mix_g[0]), "conv_a": cols(conv_a_w[0]), "conv_b": cols(conv_b_w[0]),
              "conv_bias": cols(conv_b_bias[0]), "ln_g": cols(ln_b_g[0]), "ln_b": cols(ln_b_b[0]),
              "beta": np.concatenate([cols(beta_a[0]), cols(beta_b[0])], 1), "norm_ffn": cols(norm_ffn_g[0]),
              "norm_final": cols(norm_final_g), "mem_norm": cols(mem_norm_2), "last_norm": cols(final_norm_2),
              "route_b": np.concatenate([rows(b_route_group[0]), rows(b_route_expert[0])], 1), "route_w": wr}
    vec1 = np.concatenate([parts1[n] for n in VEC1], 1)
    layers = []
    for l in range(LAYERS):
        init = 0.8 - 0.6 * float(np.exp(-0.3 * l))
        parts2 = {"norm_mix": cols(norm_mix_2[l]), "norm_cross": cols(norm_cross_2[l]), "norm_ffn": cols(norm_ffn_2[l]),
                  "subln": cols(subln_b_2[l]), "lam_init": np.full((P, 1), init, np.float32),
                  "one_less": np.full((P, 1), 1.0 - init, np.float32), "lambda": rows(lambda_vecs_2[l])}
        layers.append(np.concatenate([parts2[n] for n in VEC2], 1))
    rel = np.asarray(rel_bias_a_2)
    relpad = np.concatenate([np.zeros(rel.shape[:2] + (CHUNK,), rel.dtype), rel], 2)
    arrays = {"x": x, "mem": mem_2, "cst": constants(), "vec1": vec1, "vec2": np.stack(layers), "relpad": relpad,
              "w_in": w_in, "w_out": w_out, "w1": w1, "w3": w3, "w2": w2, "w_in_2": w_in_2, "w_up_a": w_up_a_2,
              "w_up_b": w_up_b_2, "w_up_c": w_up_c_2, "w_out_2": w_out_2, "w_q_x": w_q_x_2, "w_kv_x": w_kv_x_2,
              "w_o_x": w_o_x_2, "w_gu": w_gu_2, "w_down": w_down_2}
    arrays = {n: np.ascontiguousarray(a) for n, a in arrays.items()}
    nc = bacc.Bacc("TRN2", target_bir_lowering=False, num_devices=1, dynamic_dma_scratch_size=1024)
    args = [nc.dram_tensor(n, a.shape, mybir.dt.from_np(a.dtype), kind="ExternalInput").ap() for n, a in arrays.items()]
    out = nc.dram_tensor("out", (1, SEQ, D), F32, kind="ExternalOutput").ap()
    build(nc, *args, out)
    return run(nc, [arrays], core_ids=[0]).results[0]["out"]
```
